# Optimizing a Trainium2 kernel written in Bass

```python
import jax, jax.numpy as jnp
from jax import lax
import numpy as np

D_MODEL = 1024
BATCH = 1
SEQ = 512
DEPTH = 2

D_A = D_MODEL
H_A = 4
DV_A = D_A // H_A
DK_A = DV_A // 2
QK_A = H_A * DK_A
CONV_W = 5
CHUNK = 64
D_B = D_MODEL
N_B = 64
H_B = D_B // N_B
DECAY_LORA = max(32, int(round(1.8 * D_B ** 0.5 / 32)) * 32)
AAA_LORA = max(32, int(round(1.8 * D_B ** 0.5 / 32)) * 32)
GATE_LORA = max(32, int(round(0.6 * D_B ** 0.8 / 32)) * 32)
D_FF = 4 * D_MODEL
RW_SIZES = (D_B, D_B, D_B, DECAY_LORA, DECAY_LORA, AAA_LORA, AAA_LORA, GATE_LORA)
N_RW = sum(RW_SIZES)
IN_SIZES = (2 * QK_A, D_A, D_A, 4 * H_A, N_RW, D_MODEL, D_MODEL)
N_IN = sum(IN_SIZES)
LN_EPS = 1e-5
MH_EPS = 1e-5
GN_EPS = 64e-5
NORM_EPS = 1e-12

kernel_name = 'bidir_mlstm_rwkv7_gated_hybrid_deepnorm_adaln'

def layer_norm(x, g, b, eps=LN_EPS):
    xf = x.astype(jnp.float32)
    mu = jnp.mean(xf, -1, keepdims=True)
    var = jnp.mean(jnp.square(xf - mu), -1, keepdims=True)
    return ((xf - mu) * lax.rsqrt(var + eps) * g + b).astype(x.dtype)

def head_norm(x, eps):
    x = x.astype(jnp.float32)
    mu = jnp.mean(x, -1, keepdims=True)
    var = jnp.mean(jnp.square(x - mu), -1, keepdims=True)
    return (x - mu) * lax.rsqrt(var + eps)

def split_cols(z, sizes):
    out, start = [], 0
    for s in sizes:
        out.append(z[..., start:start + s])
        start += s
    return out

def token_shift(z, mu_prev, mu_next):
    z_prev = jnp.pad(z[:, :-1], ((0, 0), (1, 0), (0, 0)))
    z_next = jnp.pad(z[:, 1:], ((0, 0), (0, 1), (0, 0)))
    return z + mu_prev * (z_prev - z) + mu_next * (z_next - z)

def centred_dwconv(x, w, b):
    pad = w.shape[0] // 2
    y = lax.conv_general_dilated(x, w[:, None, :].astype(x.dtype), window_strides=(1,),
                                 padding=[(pad, pad)], dimension_numbers=('NWC', 'WIO', 'NWC'),
                                 feature_group_count=x.shape[-1])
    return y + b

def mlstm_chunkwise(q, k, v, ig, lf):
    B, T, H, DK = q.shape
    DV = v.shape[-1]
    NC = T // CHUNK
    ch = lambda t: t.reshape(B, NC, CHUNK, H, t.shape[-1]).transpose(1, 0, 3, 2, 4)
    chg = lambda t: t.reshape(B, NC, CHUNK, H).transpose(1, 0, 3, 2)
    tril = jnp.tril(jnp.ones((CHUNK, CHUNK), dtype=bool))

    def step(carry, inp):
        C, n, m = carry
        q_c, k_c, v_c, i_c, f_c = inp
        g = jnp.cumsum(f_c, axis=-1)
        d_log = jnp.where(tril, g[..., :, None] - g[..., None, :] + i_c[..., None, :], -jnp.inf)
        m_inter = g + m[..., None]
        m_j = jnp.maximum(jnp.max(d_log, -1), m_inter)
        s = jnp.einsum('bhld,bhsd->bhls', q_c, k_c) * jnp.exp(d_log - m_j[..., None])
        inter = jnp.exp(m_inter - m_j)
        num = jnp.einsum('bhls,bhsv->bhlv', s, v_c) + inter[..., None] * jnp.einsum('bhld,bhdv->bhlv', q_c, C)
        den = jnp.sum(s, -1) + inter * jnp.einsum('bhld,bhd->bhl', q_c, n)
        h = num / jnp.maximum(jnp.abs(den), jnp.exp(-m_j))[..., None]
        g_last = g[..., -1]
        log_w = g_last[..., None] - g + i_c
        m_new = jnp.maximum(g_last + m, jnp.max(log_w, -1))
        keep = jnp.exp(g_last + m - m_new)
        w_tok = jnp.exp(log_w - m_new[..., None])
        C = keep[..., None, None] * C + jnp.einsum('bhs,bhsd,bhsv->bhdv', w_tok, k_c, v_c)
        n = keep[..., None] * n + jnp.einsum('bhs,bhsd->bhd', w_tok, k_c)
        return (C, n, m_new), h

    init = (jnp.zeros((B, H, DK, DV), jnp.float32), jnp.zeros((B, H, DK), jnp.float32),
            jnp.full((B, H), -jnp.inf, jnp.float32))
    _, hs = lax.scan(step, init, (ch(q), ch(k), ch(v), chg(ig), chg(lf)))
    return hs.transpose(1, 0, 3, 2, 4).reshape(B, T, H, DV)

def mlstm_branch(qk, v, o, gates, conv_w, conv_b, ig_b, fg_b, norm_g):
    B, T, _ = v.shape
    qk = jax.nn.silu(centred_dwconv(qk, conv_w, conv_b)).astype(jnp.float32)
    q = qk[..., :QK_A].reshape(B, T, H_A, DK_A)
    k = qk[..., QK_A:].reshape(B, T, H_A, DK_A) * (DK_A ** -0.5)
    vh = v.astype(jnp.float32).reshape(B, T, H_A, DV_A)
    gates = gates.astype(jnp.float32).reshape(B, T, 2, 2, H_A)
    ig = gates[:, :, :, 0] + ig_b
    lf = jax.nn.log_sigmoid(gates[:, :, :, 1] + fg_b)
    h_fwd = mlstm_chunkwise(q, k, vh, ig[:, :, 0], lf[:, :, 0])
    rev = lambda t: jnp.flip(t, axis=1)
    h_bwd = rev(mlstm_chunkwise(rev(q), rev(k), rev(vh), rev(ig[:, :, 1]), rev(lf[:, :, 1])))
    hn = head_norm(h_fwd + h_bwd, MH_EPS).reshape(B, T, D_A) * norm_g
    return (jax.nn.sigmoid(o) * hn).astype(v.dtype)

def rwkv_scan(r, k, v, kk, decay, a, k_a, reverse):
    def step(S, inp):
        r_t, k_t, v_t, kk_t, w_t, a_t = inp
        k_mod = k_t * (1.0 + (a_t - 1.0) * k_a)
        s_kk = jnp.einsum('bhij,bhj->bhi', S, kk_t)
        S = (S * w_t[:, :, None, :] - s_kk[..., None] * (kk_t * a_t)[:, :, None, :]
             + v_t[..., None] * k_mod[:, :, None, :])
        return S, jnp.einsum('bhij,bhj->bhi', S, r_t)
    S0 = jnp.zeros(r.shape[1:] + (r.shape[-1],), jnp.float32)
    _, y = lax.scan(step, S0, (r, k, v, kk, decay, a), reverse=reverse)
    return y

def rwkv_branch(z, mu, w0, w_up, a0, a_up, g_up, k_k, k_a, r_k, gn_g, gn_b):
    B, T, _ = z.shape
    z = token_shift(z, mu[0], mu[1])
    r, k, v, wd_f, wd_b, ad_f, ad_b, gd = split_cols(z, RW_SIZES)
    wd = jnp.stack([wd_f, wd_b])
    ad = jnp.stack([ad_f, ad_b])
    w = -jax.nn.softplus(-(w0[:, None, None, :] + jnp.einsum('dbtr,drc->dbtc', jnp.tanh(wd), w_up))) - 0.5
    decay = jnp.exp(-jnp.exp(w.astype(jnp.float32)))
    a = jax.nn.sigmoid(a0[:, None, None, :] + jnp.einsum('dbtr,drc->dbtc', ad, a_up))
    g = jax.nn.sigmoid(gd) @ g_up
    heads = lambda t: t.reshape(t.shape[:-1] + (H_B, N_B))
    kk = heads(k * k_k).astype(jnp.float32)
    kk = kk / jnp.maximum(jnp.linalg.norm(kk, axis=-1, keepdims=True), NORM_EPS)
    tm = lambda t: jnp.moveaxis(heads(t).astype(jnp.float32), 1, 0)
    r_t, k_t, v_t, kk_t = tm(r), tm(k), tm(v), jnp.moveaxis(kk, 1, 0)
    k_a_h = k_a.reshape(H_B, N_B)
    y_f = rwkv_scan(r_t, k_t, v_t, kk_t, tm(decay[0]), tm(a[0]), k_a_h, False)
    y_b = rwkv_scan(r_t, k_t, v_t, kk_t, tm(decay[1]), tm(a[1]), k_a_h, True)
    y = head_norm(jnp.moveaxis(y_f + y_b, 0, 1), GN_EPS) * gn_g.reshape(H_B, N_B) + gn_b.reshape(H_B, N_B)
    k_sum = k * (2.0 + (a[0] + a[1] - 2.0) * k_a)
    bonus = jnp.sum(heads(r) * heads(k_sum) * r_k, -1, keepdims=True) * heads(v)
    return ((y + bonus).reshape(B, T, D_B) * g).astype(z.dtype)

def setup_inputs(seed: int = 0) -> dict:
    key = jax.random.key(seed)
    ks = iter(jax.random.split(key, 40))
    nrm = lambda shape, s: jax.random.normal(next(ks), shape, jnp.float32) * s
    beta = (8.0 * DEPTH) ** -0.25
    D = D_MODEL
    return {
        'x': nrm((BATCH, SEQ, D), 1.0),
        'c': nrm((BATCH, D), 1.0),
        'ln0_g': 1.0 + nrm((D,), 0.02),
        'ln0_b': nrm((D,), 0.02),
        'ada_w': nrm((DEPTH, D, 6 * D), 0.1 * D ** -0.5),
        'ada_b': nrm((DEPTH, 6 * D), 0.02),
        'w_in': nrm((DEPTH, D, N_IN), D ** -0.5),
        'mlstm_conv_w': nrm((DEPTH, CONV_W, 2 * QK_A), CONV_W ** -0.5),
        'mlstm_conv_b': nrm((DEPTH, 2 * QK_A), 0.02),
        'mlstm_ig_b': nrm((DEPTH, 2, H_A), 0.1),
        'mlstm_fg_b': jnp.linspace(3.0, 6.0, H_A)[None, None, :] + nrm((DEPTH, 2, H_A), 0.1),
        'mlstm_norm_g': 1.0 + nrm((DEPTH, D_A), 0.02),
        'rwkv_mu': jax.random.uniform(next(ks), (DEPTH, 2, N_RW), jnp.float32, 0.0, 0.5),
        'rwkv_w0': jnp.linspace(-6.5, -1.5, D_B)[None, None, :] + nrm((DEPTH, 2, D_B), 0.1),
        'rwkv_w_up': nrm((DEPTH, 2, DECAY_LORA, D_B), 0.5 * DECAY_LORA ** -0.5),
        'rwkv_a0': nrm((DEPTH, 2, D_B), 0.1),
        'rwkv_a_up': nrm((DEPTH, 2, AAA_LORA, D_B), 0.5 * AAA_LORA ** -0.5),
        'rwkv_g_up': nrm((DEPTH, GATE_LORA, D_B), GATE_LORA ** -0.5),
        'rwkv_k_k': 0.85 + nrm((DEPTH, D_B), 0.02),
        'rwkv_k_a': 1.0 + nrm((DEPTH, D_B), 0.02),
        'rwkv_r_k': nrm((DEPTH, H_B, N_B), 0.1),
        'rwkv_gn_g': 1.0 + nrm((DEPTH, D_B), 0.02),
        'rwkv_gn_b': nrm((DEPTH, D_B), 0.02),
        'w_branch_a': nrm((DEPTH, D_A, D), beta * D_A ** -0.5),
        'w_branch_b': nrm((DEPTH, D_B, D), beta * D_B ** -0.5),
        'w_out': nrm((DEPTH, D, D), beta * D ** -0.5),
        'ln1_g': 1.0 + nrm((DEPTH, D), 0.02),
        'ln1_b': nrm((DEPTH, D), 0.02),
        'mlp_w1': nrm((DEPTH, D, D_FF), beta * D ** -0.5),
        'mlp_b1': nrm((DEPTH, D_FF), 0.02),
        'mlp_w2': nrm((DEPTH, D_FF, D), beta * D_FF ** -0.5),
        'mlp_b2': nrm((DEPTH, D), 0.02),
        'ln2_g': 1.0 + nrm((DEPTH, D), 0.02),
        'ln2_b': nrm((DEPTH, D), 0.02),
    }

def reference(x, c, ln0_g, ln0_b, ada_w, ada_b, w_in, mlstm_conv_w, mlstm_conv_b, mlstm_ig_b,
              mlstm_fg_b, mlstm_norm_g, rwkv_mu, rwkv_w0, rwkv_w_up, rwkv_a0, rwkv_a_up, rwkv_g_up,
              rwkv_k_k, rwkv_k_a, rwkv_r_k, rwkv_gn_g, rwkv_gn_b, w_branch_a, w_branch_b, w_out,
              ln1_g, ln1_b, mlp_w1, mlp_b1, mlp_w2, mlp_b2, ln2_g, ln2_b):
    alpha = (2.0 * DEPTH) ** 0.25
    h = layer_norm(x, ln0_g, ln0_b)
    cond = jax.nn.silu(c)
    for l in range(DEPTH):
        sh1, sc1, gt1, sh2, sc2, gt2 = jnp.split(cond @ ada_w[l] + ada_b[l], 6, axis=-1)
        u = h * (1.0 + sc1[:, None]) + sh1[:, None]
        qk, v_a, o_a, gates_a, z_b, gate_a, gate_b = split_cols(u @ w_in[l], IN_SIZES)
        y_a = mlstm_branch(qk, v_a, o_a, gates_a, mlstm_conv_w[l], mlstm_conv_b[l],
                           mlstm_ig_b[l], mlstm_fg_b[l], mlstm_norm_g[l])
        y_b = rwkv_branch(z_b, rwkv_mu[l], rwkv_w0[l], rwkv_w_up[l], rwkv_a0[l], rwkv_a_up[l],
                          rwkv_g_up[l], rwkv_k_k[l], rwkv_k_a[l], rwkv_r_k[l], rwkv_gn_g[l], rwkv_gn_b[l])
        merged = (jax.nn.sigmoid(gate_a) * (y_a @ w_branch_a[l])
                  + jax.nn.sigmoid(gate_b) * (y_b @ w_branch_b[l]))
        h = layer_norm(alpha * h + (1.0 + gt1[:, None]) * (merged @ w_out[l]), ln1_g[l], ln1_b[l])
        u = h * (1.0 + sc2[:, None]) + sh2[:, None]
        f = jnp.square(jax.nn.relu(u @ mlp_w1[l] + mlp_b1[l])) @ mlp_w2[l] + mlp_b2[l]
        h = layer_norm(alpha * h + (1.0 + gt2[:, None]) * f, ln2_g[l], ln2_b[l])
    return h


_drawn_inputs = setup_inputs


def setup_inputs(seed=0):
    import zlib

    import numpy as np

    out = dict(_drawn_inputs(seed))
    spreads = {}
    factors = {'ln0_g': 2.764,
     'ln0_b': 2.732,
     'ada_b': 4.589,
     'mlstm_conv_b': 8.0,
     'mlstm_ig_b': 34.903,
     'mlstm_norm_g': 64.0,
     'rwkv_w_up': 8.0,
     'rwkv_a0': 8.0,
     'rwkv_a_up': 5.045,
     'rwkv_k_k': 64.0,
     'rwkv_k_a': 8.0,
     'rwkv_r_k': 3.144,
     'rwkv_gn_g': 64.0,
     'rwkv_gn_b': 64.0,
     'mlp_b1': 7.909,
     'mlp_b2': 2.875}
    for name, (base, spread) in spreads.items():
        noise = np.random.default_rng([zlib.crc32(name.encode()), seed]).standard_normal(out[name].shape)
        drawn = base * np.exp(spread * noise) if base else spread * noise
        out[name] = __import__('jax').numpy.asarray(drawn.astype(out[name].dtype))
    for name, factor in factors.items():
        out[name] = (out[name] * factor).astype(out[name].dtype)
    return out
```

```python
from contextlib import ExitStack

import numpy as np
import concourse.bass as bass
from concourse import mybir

ALU = mybir.AluOpType
ACT = mybir.ActivationFunctionType
F32 = mybir.dt.float32
BF16 = mybir.dt.bfloat16
ds = bass.ds

P = 128
D = 1024
T = 512
DEPTH = 2
KT = D // P
NT = T // P
HA = 4
DK = 128
DV = 256
FF = 4 * D
FT = FF // P
C = 64
NC = T // C
HP = 8
LORA = 64
GLORA = 160
N_RW = 3 * D + 4 * LORA + GLORA
QK0, V0, O0, G0, Z0 = 0, D, 2 * D, 3 * D, 3 * D + 16
GA0 = Z0 + N_RW
GB0 = GA0 + D
WD0, AD0, GD0 = Z0 + 3 * D, Z0 + 3 * D + 128, Z0 + 3 * D + 256
ALPHA = (2.0 * DEPTH) ** 0.25
DECAY = float(np.exp(-0.5))
LEVELS = 6
BIG = 1e30

B0 = dict(conv_w=0, conv_b=40, norm_g=48, w0=56, a0=72, k_k=88, k_a=96, r_k=104, gn_g=112, gn_b=120)
B1 = dict(mup=0, mun=24, ln1_g=48, ln1_b=56, b2=64, ln2_g=72, ln2_b=80, b1=88, mup_lo=120, mun_lo=123,
          mup_g2=126, mun_g2=127)
COL = {**B0, **{k: 128 + v for k, v in B1.items()}, "ada_b": 256}

CI, CBD, CG, CL, CR, CC = 0, 128, 256, 640, 640 + 12 * 128, 640 + 12 * 128 + 1024
NCONST = CC + 256


def constants():
    c = np.zeros((P, NCONST), np.float32)
    i = np.arange(P)
    c[:, CI:CI + P] = np.eye(P)
    same = (i[:, None] // C) == (i[None, :] // C)
    c[:, CBD:CBD + P] = same
    s, t = i[:, None] % C, i[None, :] % C
    q = np.arange(C)[None, :]
    for d in range(2):
        before = (s < t) if d == 0 else (s > t)
        upto = (s <= q) if d == 0 else (s >= q)
        c[:, CG + 192 * d:CG + 192 * d + 128] = same & before
        c[:, CG + 192 * d + 128:CG + 192 * d + 192] = upto
        for k in range(LEVELS):
            pair = same & ((s >> (k + 1)) == (t >> (k + 1))) & ((s >> k) != (t >> k))
            low = pair & ((s > t) if d == 0 else (s < t))
            o = CL + (6 * d + k) * 128
            c[:, o:o + 128] = low | (i[:, None] == i[None, :])
        pos = np.arange(T) % C
        c[:, CR + T * d:CR + T * (d + 1)] = pos != (0 if d == 0 else C - 1)
        hidden = (i[:, None] > i[None, :]) if d == 0 else (i[:, None] < i[None, :])
        c[:, CC + 128 * d:CC + 128 * (d + 1)] = np.where(hidden, -BIG, 0.0)
    return c


def encoder(nc, a, consts, out):
    ctx = ExitStack()
    with ctx:
        def sb(name, shape, dt=F32):
            return ctx.enter_context(nc.sbuf_tensor(name, shape, dt))

        hT = sb("hT", [P, KT, T])
        uT = sb("uT", [P, KT, T])
        yA = sb("yA", [P, KT, T])
        yB = sb("yB", [P, KT, T])
        wt = sb("wt", [P, 4, KT, P])
        pcol = sb("pcol", [P, 3 * P, 1])
        mod = sb("mod", [P, 48, 1])
        mix0 = sb("mix0", [P, 28, 1])
        ka1 = sb("ka1", [P, KT, 1])
        lncol = sb("lncol", [P, 24, 1])
        cond = sb("cond", [P, 16, 1])
        eps = sb("eps", [P, 2])
        gbias = sb("gbias", [64, 2])
        ident = sb("ident", [P, P])
        bd = sb("bd", [P, P])
        ones = sb("ones", [P, P])
        mask = sb("mask", [P, NCONST - CG], BF16)
        tw = sb("tw", [P, T])
        ad = sb("ad", [P, T])
        gd = sb("gd", [P, T])
        gd2 = sb("gd2", [32, T])
        NA = 28100
        arena = sb("arena", [P, NA])
        ps = ctx.enter_context(nc.psum_tensor("ps", [P, 8, 512], F32))

        class Carve:
            def __init__(self):
                self.at = 0

            def __call__(self, *shape, parts=P):
                n = int(np.prod(shape))
                v = arena[0:parts, self.at:self.at + n]
                self.at += n
                assert self.at <= NA, self.at
                if len(shape) == 2:
                    v = v.rearrange("p (a b) -> p a b", a=shape[0])
                if len(shape) == 3:
                    v = v.rearrange("p (a b c) -> p a b c", a=shape[0], b=shape[1])
                return v

        def m(o, n):
            return mask[:, o - CG:o - CG + n]

        maskG = [m(CG + 192 * d, 192) for d in range(2)]
        maskL = [[m(CL + (6 * d + k) * 128, 128) for k in range(LEVELS)] for d in range(2)]
        maskR = [m(CR + T * d, T) for d in range(2)]
        maskC = [m(CC + 128 * d, 128) for d in range(2)]

        cv = Carve()
        craw = cv(NCONST)
        xtok = cv(NT, D)
        sq8 = cv(KT, T)
        prow = cv(3, P)
        std = cv(T)
        rstd = cv(T)
        cv = Carve()
        adaw = cv(2 * KT, 512).rearrange("p (s k) n -> p s k n", s=2)
        cv = Carve()
        wg16 = cv(KT, 16)
        wgp = cv(KT, 2, 64)
        gx = cv(6, T, parts=64)
        rows = cv(2, T, parts=64)
        Gs = cv(T, parts=64)
        aS = cv(T, parts=64)
        zero = cv(T, parts=64)
        one = cv(T, parts=64)
        acol = cv(NT, 64)
        selh = cv(2, P, parts=64)
        wv = cv(KT, DV)
        qk = cv(2, T)
        sg = cv(2, T)
        vtok = cv(NT, DV)
        so = cv(2, T)
        Ew = cv(NT, T)
        Pw = cv(NT, T)
        dg = cv(NT, P)
        emx = cv(T)
        rf = cv(T)
        hs = cv(2, T)
        ht = cv(2, T)
        hq = cv(2, T)
        hstd = cv(T)
        cv = Carve()
        AQ = [cv(NC, 192) for _ in range(2)]
        G1 = [cv(NC, 192) for _ in range(2)]
        G3 = [cv(NC, 192) for _ in range(2)]
        XT = [cv(NC, P) for _ in range(2)]
        Bt = [cv(NC, P) for _ in range(2)]
        Ktk = [cv(NC, P) for _ in range(2)]
        Vt = [cv(NC, P) for _ in range(2)]
        Bz = cv(NC, P)
        Kz = cv(NC, P)
        Xm = cv(NC, P)
        Rm = cv(NC, P)
        dend = [cv(NC) for _ in range(2)]
        Sst = cv(2, P)
        Sd = cv(P)
        Zs = cv(P)
        Us = cv(P)
        rr, kr, vr, kk = cv(T), cv(T), cv(T), cv(T)
        Lc, Lx, sw, aa, km, kmf = Rm.rearrange("p a b -> p (a b)")[:, 0:T], Rm.rearrange("p a b -> p (a b)")[:, T:2 * T], cv(T), cv(T), None, cv(T)
        km = sw
        Ep, En, Ex = Xm.rearrange("p a b -> p (a b)")[:, 0:T], Xm.rearrange("p a b -> p (a b)")[:, T:2 * T], cv(T)
        t1 = cv(T)
        spare = wt[:, 3, :, :].rearrange("p a b -> p (a b)")
        bonus, gbuf, yf = spare[:, 0:T], spare[:, T:2 * T], cv(T)
        wup = cv(2, P)
        gup = cv(P)
        gup2 = cv(P, parts=32)
        ysum = t1
        kr_sq = t1
        Vz = XT[0]
        cv = Carve()
        ff = cv(FT, T)
        fr = cv(2, T)
        sga = cv(2, T)
        pa_ = cv(2, T)
        merged = cv(KT, T)

        sems = {}

        def S(name):
            if name not in sems:
                sems[name] = ctx.enter_context(nc.semaphore(name))
            return sems[name]

        arrived = [ctx.enter_context(nc.semaphore(f"arrived{j}")) for j in range(2)]
        opened = [ctx.enter_context(nc.semaphore(f"opened{j}")) for j in range(2)]

        cleared = [
            "ld_w0", "ld_w1", "ld_w2", "ld_w3", "ld_par", "ld_x", "st_out",
            "p_tr", "v_tr", "p_mm0", "p_mm1", "p_mm2", "p_mm3", "ev0", "ev1", "ev2", "ev3",
            "p_mean", "v_cen", "a_sq", "p_var", "a_std", "v_rstd", "v_nrm", "v_out",
            "g_set", "v_set", "a_set", "v_u",
            "a_c0", "v_s1", "v_s2", "a_act", "v_gate", "a_gate",
            "ld_v", "ld_up", "v_conv", "a_sig", "v_qk", "p_v", "a_v", "a_o", "v_sel", "p_s", "p_nm", "p_nx",
            "v_dg", "a_E", "a_emx", "v_P", "p_den", "v_den", "p_num", "v_num", "v_h", "p_m2", "a_h2",
            "a_kk", "p_ss", "v_ss", "a_nrm", "v_kk", "p_lw", "a_lw", "v_L", "g_Lx", "a_exp", "v_km", "v_bd",
            "g_dend", "v_dend", "p_g", "v_g", "g_in", "p_bt", "a_bt", "g_vz", "g_vb",
            "p_T", "v_R", "g_Y", "p_XY", "a_X", "a_Y",
            "p_Z", "a_Z", "p_U", "v_U", "p_S", "v_Sd", "v_S", "p_Y", "a_y",
            "p_pm", "v_pc", "a_psq", "p_pv", "a_pstd", "v_pr", "v_py", "v_rk", "p_bon", "v_bon", "p_gu", "a_gu",
        ]
        for n in cleared:
            S(n)
        lo = min(sems[n].num for n in cleared)
        hi = max(sems[n].num for n in cleared)
        assert hi - lo + 1 == len(cleared)

        def meet(e):
            e.sem_inc(arrived[0], 1)
            e.wait_ge(opened[0], 1)
            e.sem_inc(arrived[1], 1)
            e.wait_ge(opened[1], 1)

        def meet_sp(e):
            e.wait_ge(arrived[0], 4)
            e.sem_clear(range(lo, hi + 1))
            e.sem_clear(arrived[0])
            e.sem_clear(opened[1])
            e.sem_inc(opened[0], 1)
            e.wait_ge(arrived[1], 4)
            e.sem_clear(arrived[1])
            e.sem_clear(opened[0])
            e.sem_inc(opened[1], 1)

        block = ctx.enter_context(nc.Block())
        w_in, w_a, w_b, w_o = a["w_in"], a["w_branch_a"], a["w_branch_b"], a["w_out"]

        def ln_pe(p):
            for t in range(KT):
                mm = p.matmul(ps[:, 0, :], ones[:, 0:P], hT[:, t, :], start=t == 0, stop=t == KT - 1)
            mm.then_inc(S("p_mean"), 1)
            for t in range(KT):
                p.wait_ge(S("a_sq"), t + 1)
                mm = p.matmul(ps[:, 1, :], ones[:, 0:P], sq8[:, t, :], start=t == 0, stop=t == KT - 1)
            mm.then_inc(S("p_var"), 1)

        def ln_act(s, b):
            for t in range(KT):
                s.wait_ge(S("v_cen"), t + 1)
                s.activation(sq8[:, t, :], hT[:, t, :], ACT.Square).then_inc(S("a_sq"), 1)
            s.wait_ge(S("p_var"), 1)
            s.activation(std, ps[:, 1, :], ACT.Sqrt, bias=eps[:, 0:1], scale=1.0 / D).then_inc(S("a_std"), 1)
            for t in range(KT):
                s.wait_ge(S("v_nrm"), t + 1)
                s.activation(hT[:, t, :], hT[:, t, :], ACT.Identity, bias=b(t)).then_inc(S("v_out"), 1)
            s.wait_ge(S("v_out"), KT)

        def ln_dve(v, g):
            v.wait_ge(S("p_mean"), 1)
            for t in range(KT):
                v.scalar_tensor_tensor(hT[:, t, :], ps[:, 0, :], -1.0 / D, hT[:, t, :], ALU.mult,
                                       ALU.add).then_inc(S("v_cen"), 1)
            v.wait_ge(S("a_std"), 1)
            v.reciprocal(rstd, std).then_inc(S("v_rstd"), 1)
            v.wait_ge(S("v_rstd"), 1)
            v.wait_ge(S("a_sq"), KT)
            for t in range(KT):
                v.scalar_tensor_tensor(hT[:, t, :], hT[:, t, :], g(t), rstd, ALU.mult,
                                       ALU.mult).then_inc(S("v_nrm"), 1)

        def modulate(v, first):
            for t in range(KT):
                v.tensor_scalar(uT[:, t, :], hT[:, t, :], mod[:, first + 8 + t, :], mod[:, first + t, :],
                                ALU.mult, ALU.add).then_inc(S("v_u"), 1)

        def load_w(e, slot, src, col, n=P):
            e.dma_start(wt[:, slot, :, 0:n], src.rearrange("(k p) n -> p k n", p=P)[:, :, ds(col, n)])\
             .then_inc(S(f"ld_w{slot}"), 16)

        def dense(p, slot, bank, rhs, n=P):
            for k in range(KT):
                mm = p.matmul(ps[0:n, bank, :], wt[:, slot, k, 0:n], rhs[:, k, :], start=k == 0, stop=k == KT - 1)
            return mm

        def shift(v, x, z, mp, mn, j):
            v.wait_ge(S("a_c0"), j + 1)
            v.scalar_tensor_tensor(x[:, 1:T], z[:, 0:T - 1], mp, x[:, 1:T], ALU.mult, ALU.add).then_inc(S("v_s1"), 1)
            v.wait_ge(S("v_s1"), j + 1)
            v.scalar_tensor_tensor(x[:, 0:T - 1], z[:, 1:T], mn, x[:, 0:T - 1], ALU.mult, ALU.add)\
             .then_inc(S("v_s2"), 1)

        def scale_h(v):
            for t in range(KT):
                v.tensor_scalar(hT[:, t, :], hT[:, t, :], ALPHA, None, ALU.mult).then_inc(S("v_cen"), 1)
            v.wait_ge(S("v_cen"), KT)

        def rw_regions(e, half, meet_):
            half(0, True, False, False, True, 0)
            meet_(e)
            half(1, True, True, False, False, 0)
            meet_(e)
            with e.Fori(1, HP) as hp:
                half(0, True, True, False, False, hp)
                meet_(e)
                half(1, True, True, True, False, hp)
                meet_(e)
            half(0, False, True, False, False, HP)
            meet_(e)
            half(1, False, False, True, False, HP)
            meet_(e)

        @block.sync
        def _(e):
            e.dma_start(craw, consts).then_inc(S("ld_par"), 16)
            e.dma_start(xtok, a["x"][0].rearrange("(t p) d -> p t d", p=P)).then_inc(S("ld_x"), 16)
            for j, n in enumerate(("ln0_g", "ln0_b")):
                e.dma_start(prow[8 * j:8 * j + 8, 0, :], a[n].rearrange("(t p) -> t p", p=P))\
                 .then_inc(S("ld_par"), 16)
            e.dma_start(prow[16:24, 0, :], a["c"].rearrange("o (t p) -> (o t) p", p=P)).then_inc(S("ld_par"), 16)
            meet_sp(e)
            with e.Fori(0, DEPTH) as l:
                def par(row, blk, src, n=8):
                    e.dma_start(prow[row:row + n, blk, :], src).then_inc(S("ld_par"), 16)

                def vec(x):
                    return x.rearrange("(t p) -> t p", p=P)

                def vec2(x):
                    return x.rearrange("j (t p) -> (j t) p", p=P)
                par(B0["conv_w"], 0, vec2(a["mlstm_conv_w"][l]), 40)
                par(B0["conv_b"], 0, vec(a["mlstm_conv_b"][l]))
                par(B0["norm_g"], 0, vec(a["mlstm_norm_g"][l]))
                par(B0["w0"], 0, vec2(a["rwkv_w0"][l]), 16)
                par(B0["a0"], 0, vec2(a["rwkv_a0"][l]), 16)
                par(B0["k_k"], 0, vec(a["rwkv_k_k"][l]))
                par(B0["k_a"], 0, vec(a["rwkv_k_a"][l]))
                par(B0["r_k"], 0, a["rwkv_r_k"][l].rearrange("(t h) n -> t (h n)", h=2))
                par(B0["gn_g"], 0, vec(a["rwkv_gn_g"][l]))
                par(B0["gn_b"], 0, vec(a["rwkv_gn_b"][l]))
                mu = a["rwkv_mu"][l]
                e.wait_ge(S("v_set"), 1)
                par(B1["mup"], 1, vec(mu[0, 0:3 * D]), 24)
                par(B1["mun"], 1, vec(mu[1, 0:3 * D]), 24)
                par(B1["mup_lo"], 1, vec(mu[0, 3 * D:3 * D + 384]), 3)
                par(B1["mun_lo"], 1, vec(mu[1, 3 * D:3 * D + 384]), 3)
                for j in range(2):
                    e.dma_start(prow[126 + j:127 + j, 1, 0:32], mu[j:j + 1, 3 * D + 384:N_RW])\
                     .then_inc(S("ld_par"), 16)
                par(B1["ln1_g"], 1, vec(a["ln1_g"][l]))
                par(B1["ln1_b"], 1, vec(a["ln1_b"][l]))
                par(B1["b2"], 1, vec(a["mlp_b2"][l]))
                par(B1["ln2_g"], 1, vec(a["ln2_g"][l]))
                par(B1["ln2_b"], 1, vec(a["ln2_b"][l]))
                par(B1["b1"], 1, vec(a["mlp_b1"][l]), 32)
                par(0, 2, vec(a["ada_b"][l]), 48)
                for j, n in enumerate(("mlstm_ig_b", "mlstm_fg_b")):
                    for d in range(2):
                        e.dma_start(gbias[32 * d:32 * d + 4, j:j + 1], a[n][l][d].rearrange("(h o) -> h o", o=1))\
                         .then_inc(S("ld_par"), 16)
                ada = a["ada_w"][l].rearrange("(k p) n -> p k n", p=P)
                for s in range(2):
                    e.dma_start(adaw[:, s, :, :], ada[:, :, 512 * s:512 * s + 512]).then_inc(S(f"ld_w{s}"), 16)
                with e.Fori(0, 5) as i:
                    for s in range(2):
                        e.wait_ge(S(f"p_mm{s}"), i + 1)
                        e.dma_start(adaw[:, s, :, :], ada[:, :, ds((2 * i + 2 + s) * 512, 512)])\
                         .then_inc(S(f"ld_w{s}"), 16)
                e.wait_ge(S("ld_w0"), 96)
                meet_sp(e)
                for s, (col, n) in enumerate(((WD0, P), (AD0, P), (GD0, P), (GD0 + P, 32))):
                    load_w(e, s, w_in[l], col, n)
                e.dma_start(wg16, w_in[l].rearrange("(k p) n -> p k n", p=P)[:, :, G0:G0 + 16]).then_inc(S("ld_v"), 16)
                meet_sp(e)
                with e.Fori(0, HA) as h:
                    load_w(e, 0, w_in[l], QK0 + h * DK)
                    load_w(e, 1, w_in[l], QK0 + 512 + h * DK)
                    e.dma_start(wv, w_in[l].rearrange("(k p) n -> p k n", p=P)[:, :, ds(V0 + h * DV, DV)])\
                     .then_inc(S("ld_v"), 16)
                    load_w(e, 2, w_in[l], O0 + h * DV)
                    load_w(e, 3, w_in[l], O0 + P + h * DV)
                    meet_sp(e)

                def rw_loads(hp):
                    for s in range(3):
                        load_w(e, s, w_in[l], Z0 + s * D + hp * P)
                    for j, n in enumerate(("rwkv_w_up", "rwkv_a_up")):
                        e.dma_start(wup[:, j, :], a[n][l].rearrange("d r c -> (d r) c")[:, ds(hp * P, P)])\
                         .then_inc(S("ld_up"), 16)
                    e.dma_start(gup, a["rwkv_g_up"][l][0:P, ds(hp * P, P)]).then_inc(S("ld_up"), 16)
                    e.dma_start(gup2, a["rwkv_g_up"][l][P:GLORA, ds(hp * P, P)]).then_inc(S("ld_up"), 16)
                rw_loads(0)
                meet_sp(e)
                meet_sp(e)
                with e.Fori(1, HP) as hp:
                    rw_loads(hp)
                    meet_sp(e)
                    meet_sp(e)
                meet_sp(e)
                meet_sp(e)

                def stream(n_iter, col, src):
                    for s in range(4):
                        load_w(e, s, src(s), col(0, s))
                    with e.Fori(1, n_iter) as i:
                        for s in range(4):
                            e.wait_ge(S(f"p_mm{s}"), i)
                            load_w(e, s, src(s), col(i, s))
                    for s in range(4):
                        e.wait_ge(S(f"ld_w{s}"), 16 * n_iter)
                merge_src = [w_in[l], w_a[l], w_in[l], w_b[l]]
                merge_col = [GA0, 0, GB0, 0]
                stream(KT, lambda i, s: merge_col[s] + i * P, lambda s: merge_src[s])
                meet_sp(e)
                stream(2, lambda i, s: i * 512 + s * P, lambda s: w_o[l])
                meet_sp(e)
                meet_sp(e)
                stream(8, lambda i, s: i * 512 + s * P, lambda s: a["mlp_w1"][l])
                meet_sp(e)
                stream(8, lambda i, s: i * P, lambda s: a["mlp_w2"][l][s * D:(s + 1) * D, :])
                meet_sp(e)
                meet_sp(e)
            for t in range(NT):
                e.wait_ge(S("v_tr"), 2 * t + 2)
                e.dma_start(out[0, t * P:(t + 1) * P, :], xtok[:, t, :]).then_inc(S("st_out"), 16)
            e.wait_ge(S("st_out"), 16 * NT)

        @block.tensor
        def _(p):
            p.wait_ge(S("v_set"), 5)
            p.wait_ge(S("ld_par"), 64)
            p.transpose(ps[:, 7, 0:24], prow[0:24, 0, :], ident[0:24, 0:24]).then_inc(S("p_tr"), 1)
            p.wait_ge(S("ld_x"), 16)
            for t in range(KT):
                if t >= 4:
                    p.wait_ge(S("v_tr"), t - 2)
                for q in range(NT):
                    mm = p.transpose(ps[:, t % 4, q * P:(q + 1) * P], xtok[:, q, t * P:(t + 1) * P], ident[:, :])
                mm.then_inc(S("p_tr"), 1)
            p.wait_ge(S("v_tr"), KT + 1)
            ln_pe(p)
            meet(p)
            with p.Fori(0, DEPTH) as l:
                p.wait_ge(S("ld_par"), 16 * 27)
                for b in range(3):
                    n = P if b < 2 else 48
                    mm = p.transpose(ps[:, b, 0:n], prow[0:n, b, :], ident[0:n, 0:n])
                mm.then_inc(S("p_tr"), 1)
                with p.Fori(0, 6) as i:
                    for s in range(2):
                        p.wait_ge(S(f"ld_w{s}"), 16 * i + 16)
                        for j in range(4):
                            for k in range(KT):
                                mm = p.matmul(ps[:, 3, ds(8 * i + 4 * s + j, 1)], adaw[:, s, k, j * P:(j + 1) * P],
                                              cond[:, 8 + k, :], start=k == 0, stop=k == KT - 1)
                        mm.then_inc(S(f"p_mm{s}"), 1)
                meet(p)
                p.wait_ge(S("v_u"), KT)
                for s, n in enumerate((P, P, P, 32)):
                    p.wait_ge(S(f"ld_w{s}"), 16)
                    dense(p, s, s, uT, n).then_inc(S("p_mm0"), 1)
                p.wait_ge(S("g_set"), 5)
                for j in range(2):
                    for k in range(KT):
                        mm = p.matmul(ps[0:64, 4 + j, :], wgp[:, k, j, :], uT[:, k, :], start=k == 0, stop=k == KT - 1)
                    mm.then_inc(S("p_mm1"), 1)
                p.wait_ge(S("v_gate"), 4)
                for t in range(NT):
                    mm = p.transpose(ps[:, 6, t * 64:(t + 1) * 64], aS[:, t * P:(t + 1) * P], ident[0:64, 0:64])
                mm.then_inc(S("p_tr"), 1)
                meet(p)
                with p.Fori(0, HA) as h:
                    for s in range(2):
                        p.wait_ge(S(f"ld_w{s}"), 16)
                        dense(p, s, s, uT).then_inc(S("p_mm0"), 1)
                    p.wait_ge(S("ld_v"), 16)
                    for t in range(NT):
                        for k in range(KT):
                            mm = p.matmul(ps[:, 2 + t // 2, (t % 2) * DV:(t % 2 + 1) * DV], uT[:, k, t * P:(t + 1) * P],
                                          wv[:, k, :], start=k == 0, stop=k == KT - 1)
                        mm.then_inc(S("p_v"), 1)
                    for s in range(2):
                        p.wait_ge(S(f"ld_w{2 + s}"), 16)
                        dense(p, 2 + s, 4 + s, uT).then_inc(S("p_mm1"), 1)
                    p.wait_ge(S("v_qk"), 2)
                    p.wait_ge(S("a_v"), 2)
                    for t in range(NT):
                        p.matmul(ps[:, t, :], qk[:, 1, t * P:(t + 1) * P], qk[:, 0, :], start=True, stop=True)\
                         .then_inc(S("p_s"), 1)
                    p.wait_ge(S("v_sel"), 2)
                    for d in range(2):
                        if d:
                            p.wait_ge(S("a_E"), 7)
                            p.wait_ge(S("v_dg"), NT)
                        p.matmul(ps[:, 6, :], selh[:, d, :], rows[:, 0, :], start=True, stop=True).then_inc(S("p_nm"), 1)
                        if d:
                            p.wait_ge(S("v_den"), 1)
                        p.matmul(ps[:, 7, :], selh[:, d, :], rows[:, 1, :], start=True, stop=True).then_inc(S("p_nx"), 1)
                        p.wait_ge(S("v_P"), NT * (d + 1))
                        p.wait_ge(S("a_emx"), d + 1)
                        order = range(NT) if d == 0 else range(NT - 1, -1, -1)
                        for n, t in enumerate(order):
                            lo_, hi_ = (t * P, T) if d == 0 else (0, (t + 1) * P)
                            mm = p.matmul(ps[:, 7, lo_:hi_], ones[:, 0:P], Pw[:, t, lo_:hi_], start=n == 0,
                                          stop=n == NT - 1)
                        mm.then_inc(S("p_den"), 1)
                        if d:
                            p.wait_ge(S("v_num"), 2)
                        else:
                            p.wait_ge(S("a_o"), 2)
                        for c in range(2):
                            for n, t in enumerate(order):
                                lo_, hi_ = (t * P, T) if d == 0 else (0, (t + 1) * P)
                                mm = p.matmul(ps[:, 4 + c, lo_:hi_], vtok[:, t, c * P:(c + 1) * P], Pw[:, t, lo_:hi_],
                                              start=n == 0, stop=n == NT - 1)
                            mm.then_inc(S("p_num"), 1)
                    p.wait_ge(S("v_h"), 2)
                    for c in range(2):
                        mm = p.matmul(ps[:, 6, :], ones[:, 0:P], hs[:, c, :], start=c == 0, stop=c == 1)
                    mm.then_inc(S("p_m2"), 1)
                    p.wait_ge(S("a_h2"), 2)
                    for c in range(2):
                        mm = p.matmul(ps[:, 7, :], ones[:, 0:P], hq[:, c, :], start=c == 0, stop=c == 1)
                    mm.then_inc(S("p_m2"), 1)
                    meet(p)


                def half(d, has_inv, has_chain, post, first, hp):
                    if has_inv:
                        if d == 0:
                            for s in range(3):
                                p.wait_ge(S(f"ld_w{s}"), 16)
                                dense(p, s, s, uT).then_inc(S("p_mm0"), 1)
                            p.wait_ge(S("ld_up"), 64)
                        for j, x in enumerate((tw, ad)):
                            p.matmul(ps[:, 3 + j, :], wup[64 * d:64 * d + 64, j, :], x[64 * d:64 * d + 64, :], start=True,
                                     stop=True).then_inc(S("p_lw"), 1)
                        if d == 0:
                            p.wait_ge(S("a_kk"), 1)
                            p.matmul(ps[:, 5, :], bd[:, :], kr_sq, start=True, stop=True).then_inc(S("p_ss"), 1)
                    if post:
                        p.matmul(ps[:, 0, :], bd[:, :], ysum, start=True, stop=True).then_inc(S("p_pm"), 1)
                        p.wait_ge(S("a_psq"), 1)
                        p.matmul(ps[:, 1, :], bd[:, :], yf, start=True, stop=True).then_inc(S("p_pv"), 1)
                    if has_inv and d == 1:
                        p.wait_ge(S("v_rk"), 2)
                        p.matmul(ps[:, 2, :], bd[:, :], Ex, start=True, stop=True).then_inc(S("p_bon"), 1)
                        p.matmul(ps[:, 5, :], gup, gd[:, :], start=True, stop=False)
                        p.matmul(ps[:, 5, :], gup2, gd2[:, :], start=False, stop=True).then_inc(S("p_gu"), 1)
                    if has_inv:
                        p.wait_ge(S("v_bd"), 7)
                        if d == 1:
                            p.wait_ge(S("v_bon"), 1)
                            p.wait_ge(S("a_gu"), 1)
                            if post:
                                p.wait_ge(S("a_pstd"), 1)
                        for b in range(NC):
                            if b >= 6:
                                p.wait_ge(S("v_g"), b - 5)
                            for c in range(2 * (b // 2), 2 * (b // 2) + 2):
                                mm = p.matmul(ps[:, b % 6, (c % 2) * 192:(c % 2 + 1) * 192], (Bz if b % 2 == 0 else Kz)[:, c, :],
                                              AQ[d][:, c, :], start=True, stop=True)
                            mm.then_inc(S("p_g"), 1)
                        srcs = [Bz, Kz] + [Vz] * (d == 0)
                        for j, z in enumerate(srcs):
                            if j == 2:
                                p.wait_ge(S("g_vz"), 2)
                            for q in range(2):
                                n = 2 * j + q
                                bank = (NC + n) % 6
                                if n < 6:
                                    p.wait_ge(S("v_g"), min(NC, 3 + n))
                                for c in range(4):
                                    mm = p.transpose(ps[:, bank, c * P:(c + 1) * P], z[:, 4 * q + c, :], ident[:, :])
                                mm.then_inc(S("p_bt"), 1)
                        nbt = 2 * len(srcs)
                    for n in range(24):
                        if has_inv:
                            k, ph, q = n // 4, n // 2 % 2, n % 2
                            cs = range(4 * q, 4 * q + 4)
                            if ph == 0:
                                if k == 0:
                                    p.wait_ge(S("a_bt"), nbt)
                                    p.wait_ge(S("g_in"), NC)
                                    p.wait_ge(S("v_g"), NC)
                                elif k == 1:
                                    p.wait_ge(S("v_R"), q + 1)
                                else:
                                    p.wait_ge(S("a_X"), 2 * (k - 2) + q + 1)
                                for c in cs:
                                    mm = p.matmul(ps[:, 3 * q, (c % 4) * P:(c % 4 + 1) * P], G1[d][:, c, 0:P],
                                                  ident[:, :] if k == 0 else Xm[:, c, :], start=True, stop=True)
                                mm.then_inc(S("p_T"), 1)
                            elif k >= 1:
                                p.wait_ge(S("v_R"), 2 * k + q + 1)
                                if k == 1:
                                    p.wait_ge(S("g_Y"), 4 * q + 4)
                                else:
                                    p.wait_ge(S("a_Y"), 2 * (k - 2) + q + 1)
                                for c in cs:
                                    p_c = slice((c % 4) * P, (c % 4 + 1) * P)
                                    if k < LEVELS - 1:
                                        p.matmul(ps[:, 3 * q + 1, p_c], XT[d][:, c, :], Rm[:, c, :], start=True, stop=True)
                                    mm = p.matmul(ps[:, 3 * q + 2, p_c], Rm[:, c, :], XT[d][:, c, :], start=True, stop=True)
                                mm.then_inc(S("p_XY"), 1)
                        if has_chain:
                            cd = 1 - d
                            i, ph = n // 3, n % 3
                            c = i if cd == 0 else NC - 1 - i
                            S_in = Sst[:, (i + 1) % 2, :]
                            if ph == 0:
                                if i >= 1:
                                    p.wait_ge(S("v_S"), i)
                                mm = p.matmul(ps[:, 6, 0:P], G3[cd][:, c, 0:P], Vt[cd][:, c, :], start=True, stop=i == 0)
                                if i:
                                    mm = p.matmul(ps[:, 6, 0:P], AQ[cd][:, c, 0:P], S_in, start=False, stop=True)
                                mm.then_inc(S("p_Z"), 1)
                            elif ph == 1:
                                p.wait_ge(S("a_Z"), i + 1)
                                if i:
                                    p.wait_ge(S("a_y"), i)
                                p.matmul(ps[:, 7, 0:P], XT[cd][:, c, :], Zs, start=True, stop=True).then_inc(S("p_U"), 1)
                            else:
                                p.wait_ge(S("v_U"), i + 1)
                                if i < NC - 1:
                                    p.matmul(ps[:, 6, P:2 * P], Ktk[cd][:, c, :], Vt[cd][:, c, :], start=True, stop=False)
                                    p.matmul(ps[:, 6, P:2 * P], Bt[cd][:, c, :], Us, start=False, stop=True)\
                                     .then_inc(S("p_S"), 1)
                                if i:
                                    p.matmul(ps[:, 7, P:P + C], S_in, AQ[cd][:, c, P:P + C], start=True, stop=False)
                                p.matmul(ps[:, 7, P:P + C], Us, G1[cd][:, c, P:P + C], start=i == 0, stop=False)
                                p.matmul(ps[:, 7, P:P + C], Vt[cd][:, c, :], G3[cd][:, c, P:P + C], start=False, stop=True)\
                                 .then_inc(S("p_Y"), 1)
                rw_regions(p, half, meet)

                with p.Fori(0, KT) as n:
                    for s, x in enumerate((uT, yA, uT, yB)):
                        p.wait_ge(S(f"ld_w{s}"), 16 * n + 16)
                        p.wait_ge(S(f"ev{s}"), n + 1)
                        dense(p, s, s, x).then_inc(S(f"p_mm{s}"), 1)
                meet(p)
                with p.Fori(0, 2) as n:
                    for s in range(4):
                        p.wait_ge(S(f"ld_w{s}"), 16 * n + 16)
                        p.wait_ge(S(f"ev{s}"), n + 1)
                        dense(p, s, s, merged).then_inc(S(f"p_mm{s}"), 1)
                meet(p)
                ln_pe(p)
                meet(p)
                p.wait_ge(S("v_u"), KT)
                with p.Fori(0, 8) as n:
                    for s in range(4):
                        p.wait_ge(S(f"ld_w{s}"), 16 * n + 16)
                        p.wait_ge(S(f"ev{s}"), n + 1)
                        dense(p, s, s, uT).then_inc(S(f"p_mm{s}"), 1)
                meet(p)
                with p.Fori(0, 8) as n:
                    for s in range(4):
                        p.wait_ge(S(f"ld_w{s}"), 16 * n + 16)
                        if s == 0:
                            p.wait_ge(S("ev0"), n + 1)
                        for k in range(KT):
                            mm = p.matmul(ps[:, 0, :], wt[:, s, k, :], ff[:, s * KT + k, :], start=s == 0 and k == 0,
                                          stop=s == 3 and k == KT - 1)
                        mm.then_inc(S(f"p_mm{s}"), 1)
                meet(p)
                ln_pe(p)
                meet(p)
            for t in range(NT):
                for q in range(2):
                    b = 2 * t + q
                    if b >= 4:
                        p.wait_ge(S("v_tr"), b - 3)
                    for c in range(4):
                        mm = p.transpose(ps[:, b % 4, c * P:(c + 1) * P], hT[:, 4 * q + c, t * P:(t + 1) * P], ident[:, :])
                    mm.then_inc(S("p_tr"), 1)

        @block.scalar
        def _(s):
            s.wait_ge(S("v_set"), 7)
            s.wait_ge(S("v_tr"), KT + 1)
            s.activation(cond[:, 0:8, :], lncol[:, 16:24, :], ACT.Sigmoid).then_inc(S("a_set"), 1)
            ln_act(s, lambda t: lncol[:, 8 + t, :])
            meet(s)
            with s.Fori(0, DEPTH) as l:
                meet(s)
                for j, (x, n) in enumerate(((tw, P), (ad, P), (gd, P), (gd2, 32))):
                    s.wait_ge(S("p_mm0"), j + 1)
                    s.activation(x[0:n, :], ps[0:n, j, :], ACT.Identity, scale=mix0[0:n, 24 + j, :]).then_inc(S("a_c0"), 1)
                for j in range(2):
                    s.wait_ge(S("p_mm1"), j + 1)
                    s.activation(gx[:, j, :], ps[0:64, 4 + j, :], ACT.Identity, bias=gbias[:, j:j + 1]).then_inc(S("a_gate"), 1)
                s.wait_ge(S("a_gate"), 2)
                s.activation(gx[:, 2, :], gx[:, 1, :], ACT.Abs).then_inc(S("a_gate"), 1)
                s.wait_ge(S("a_gate"), 3)
                s.activation(gx[:, 3, :], gx[:, 2, :], ACT.Exp, scale=-1.0).then_inc(S("a_gate"), 1)
                s.wait_ge(S("a_gate"), 4)
                s.activation(gx[:, 4, :], gx[:, 3, :], ACT.Ln, bias=1.0).then_inc(S("a_gate"), 1)
                s.wait_ge(S("v_s2"), 4)
                s.activation(tw[:, :], tw[:, :], ACT.Tanh).then_inc(S("a_act"), 1)
                s.activation(gd[:, :], gd[:, :], ACT.Sigmoid).then_inc(S("a_act"), 1)
                s.activation(gd2[:, :], gd2[:, :], ACT.Sigmoid).then_inc(S("a_act"), 1)
                s.wait_ge(S("p_tr"), 1)
                s.activation(acol.rearrange("p a b -> p (a b)"), ps[:, 6, 0:256], ACT.Copy).then_inc(S("a_act"), 1)
                s.wait_ge(S("a_act"), 4)
                meet(s)
                with s.Fori(0, HA) as h:
                    for j in range(2):
                        s.wait_ge(S("p_mm0"), j + 1)
                        s.activation(qk[:, j, :], ps[:, j, :], ACT.Identity, scale=pcol[:, 2 * 8 + 4 * j + h, :],
                                     bias=pcol[:, COL["conv_b"] + 4 * j + h, :]).then_inc(S("a_c0"), 1)
                    for j in range(2):
                        s.wait_ge(S("p_v"), 2 * j + 2)
                        s.activation(vtok[:, 2 * j:2 * j + 2, :].rearrange("p a b -> p (a b)"), ps[:, 2 + j, :], ACT.Copy)\
                         .then_inc(S("a_v"), 1)
                    for j in range(2):
                        s.wait_ge(S("v_conv"), 4 * j + 4)
                        s.activation(sg[:, j, :], qk[:, j, :], ACT.Sigmoid).then_inc(S("a_sig"), 1)
                    for j in range(2):
                        s.wait_ge(S("p_mm1"), j + 1)
                        s.activation(so[:, j, :], ps[:, 4 + j, :], ACT.Sigmoid).then_inc(S("a_o"), 1)
                    for d in range(2):
                        s.wait_ge(S("p_nx"), d + 1)
                        if d:
                            s.wait_ge(S("v_den"), 1)
                        s.activation(emx, ps[:, 7, :], ACT.Exp).then_inc(S("a_emx"), 1)
                        s.wait_ge(S("p_nm"), d + 1)
                        if d:
                            s.wait_ge(S("v_P"), NT)
                        s.wait_ge(S("v_dg"), NT * d + NT)
                        for t in range(NT):
                            bias = acol[:, t, ds(32 * d + h, 1)]
                            s.activation(Ew[:, t, t * P:(t + 1) * P], dg[:, t, :], ACT.Exp, bias=bias).then_inc(S("a_E"), 1)
                            lo_, hi_ = ((t + 1) * P, T) if d == 0 else (0, t * P)
                            if hi_ > lo_:
                                s.activation(Ew[:, t, lo_:hi_], ps[:, 6, lo_:hi_], ACT.Exp, bias=bias).then_inc(S("a_E"), 1)
                    for c in range(2):
                        s.wait_ge(S("v_h"), 3 + c)
                        s.activation(hq[:, c, :], hs[:, c, :], ACT.Square).then_inc(S("a_h2"), 1)
                    s.wait_ge(S("p_m2"), 2)
                    s.activation(hstd, ps[:, 7, :], ACT.Sqrt, bias=eps[:, 0:1], scale=1.0 / DV).then_inc(S("a_std"), 1)
                    meet(s)

                def half(d, has_inv, has_chain, post, first, hp):
                    if has_inv:
                        if d == 0:
                            for j, x in enumerate((rr, kr, vr)):
                                s.wait_ge(S("p_mm0"), j + 1)
                                s.activation(x, ps[:, j, :], ACT.Identity, scale=mix0[:, 8 * j + hp, :]).then_inc(S("a_c0"), 1)
                        s.wait_ge(S("p_lw"), 1)
                        s.activation(sw, ps[:, 3, :], ACT.Sigmoid, bias=pcol[:, COL["w0"] + 8 * d + hp, :]).then_inc(S("a_lw"), 1)
                        s.wait_ge(S("p_lw"), 2)
                        s.activation(aa, ps[:, 4, :], ACT.Sigmoid, bias=pcol[:, COL["a0"] + 8 * d + hp, :]).then_inc(S("a_lw"), 1)
                        if d == 0:
                            s.wait_ge(S("v_s2"), 2)
                            s.activation(kr_sq, kr, ACT.Square, scale=pcol[:, COL["k_k"] + hp, :]).then_inc(S("a_kk"), 1)
                            s.wait_ge(S("v_ss"), 1)
                            s.activation(Ex, Ex, ACT.Sqrt).then_inc(S("a_nrm"), 1)
                    if post:
                        s.wait_ge(S("v_pc"), 1)
                        s.activation(yf, ysum, ACT.Square).then_inc(S("a_psq"), 1)
                        s.wait_ge(S("p_pv"), 1)
                        s.activation(yf, ps[:, 1, :], ACT.Sqrt, bias=eps[:, 1:2], scale=1.0 / C).then_inc(S("a_pstd"), 1)
                    if has_inv:
                        if d == 1:
                            s.wait_ge(S("p_gu"), 1)
                            if post:
                                s.wait_ge(S("v_py"), 3)
                            s.activation(gbuf, ps[:, 5, :], ACT.Copy).then_inc(S("a_gu"), 1)
                        s.wait_ge(S("v_L"), 1)
                        s.activation(Ep, Lc, ACT.Exp, scale=-DECAY).then_inc(S("a_exp"), 1)
                        s.activation(En, Lc, ACT.Exp, scale=DECAY).then_inc(S("a_exp"), 1)
                        s.wait_ge(S("g_Lx"), 1)
                        if d == 0:
                            s.wait_ge(S("v_kk"), 1)
                        else:
                            s.wait_ge(S("p_bon"), 1)
                        s.activation(Ex, Lx, ACT.Exp, scale=-DECAY).then_inc(S("a_exp"), 1)
                        dst = [Bt[d], Ktk[d]] + [Vt[0]] * (d == 0)
                        for j, z in enumerate(dst):
                            for q in range(2):
                                n = 2 * j + q
                                s.wait_ge(S("p_bt"), n + 1)
                                s.activation(z[:, 4 * q:4 * q + 4, :].rearrange("p a b -> p (a b)"), ps[:, (NC + n) % 6, :],
                                             ACT.Copy).then_inc(S("a_bt"), 1)
                    for n in range(24):
                        if has_inv:
                            k, ph, q = n // 4, n // 2 % 2, n % 2
                            if ph == 1 and k >= 1:
                                s.wait_ge(S("p_XY"), 2 * (k - 1) + q + 1)
                                if k < LEVELS - 1:
                                    s.activation(Xm[:, 4 * q:4 * q + 4, :].rearrange("p a b -> p (a b)"), ps[:, 3 * q + 1, :],
                                                 ACT.Copy).then_inc(S("a_X"), 1)
                                s.activation(XT[d][:, 4 * q:4 * q + 4, :].rearrange("p a b -> p (a b)"), ps[:, 3 * q + 2, :],
                                             ACT.Copy).then_inc(S("a_Y"), 1)
                        if has_chain:
                            cd = 1 - d
                            i, ph = n // 3, n % 3
                            c = i if cd == 0 else NC - 1 - i
                            if ph == 0:
                                s.wait_ge(S("p_Z"), i + 1)
                                if i:
                                    s.wait_ge(S("p_U"), i)
                                s.activation(Zs, ps[:, 6, 0:P], ACT.Copy).then_inc(S("a_Z"), 1)
                            elif ph == 2 and cd == 0:
                                s.wait_ge(S("p_Y"), i + 1)
                                if i == 0 and post:
                                    s.wait_ge(S("v_py"), 1)
                                s.activation(yf[:, c * C:(c + 1) * C], ps[:, 7, P:P + C], ACT.Copy).then_inc(S("a_y"), 1)
                    if has_chain and d == 1:
                        s.wait_ge(S("a_y"), NC)
                    elif has_inv:
                        s.wait_ge(S("a_Y"), 2 * (LEVELS - 1))
                    elif has_chain:
                        s.wait_ge(S("a_Z"), NC)
                rw_regions(s, half, meet)
                for j in range(2):
                    s.sem_inc(S(f"ev{2 * j}"), 1)
                with s.Fori(0, KT) as n:
                    for j in range(2):
                        s.wait_ge(S(f"p_mm{2 * j}"), n + 1)
                        s.wait_ge(S("v_out"), n + 1)
                        s.activation(sga[:, j, :], ps[:, 2 * j, :], ACT.Sigmoid).then_inc(S(f"ev{2 * j}"), 1)
                meet(s)
                meet(s)
                ln_act(s, lambda t: pcol[:, COL["ln1_b"] + t, :])
                meet(s)
                for j in range(4):
                    s.sem_inc(S(f"ev{j}"), 1)
                with s.Fori(0, 8) as n:
                    for j in range(4):
                        s.wait_ge(S(f"p_mm{j}"), n + 1)
                        s.activation(ff[:, 4 * n + j, :], ps[:, j, :], ACT.Relu, bias=pcol[:, COL["b1"] + 4 * n + j, :])\
                         .then_inc(S(f"ev{j}"), 1)
                meet(s)
                meet(s)
                ln_act(s, lambda t: pcol[:, COL["ln2_b"] + t, :])
                meet(s)

        @block.gpsimd
        def _(g):
            meet(g)
            with g.Fori(0, DEPTH) as l:
                meet(g)
                g.memset(wgp, 0.0).then_inc(S("g_set"), 1)
                g.wait_ge(S("g_set"), 1)
                g.wait_ge(S("ld_v"), 16)
                for d in range(2):
                    for j in range(2):
                        g.tensor_copy(wgp[:, :, j, 32 * d:32 * d + 4], wg16[:, :, 8 * d + 4 * j:8 * d + 4 * j + 4])\
                         .then_inc(S("g_set"), 1)
                meet(g)
                with g.Fori(0, HA) as h:
                    meet(g)

                def half(d, has_inv, has_chain, post, first, hp):
                    if first:
                        g.memset(AQ[0], 0.0).then_inc(S("g_dend"), 1)
                        g.memset(AQ[1], 0.0).then_inc(S("g_dend"), 1)
                        g.memset(Bz, 0.0).then_inc(S("g_dend"), 1)
                        g.memset(Kz, 0.0).then_inc(S("g_dend"), 1)
                        g.memset(Vz, 0.0).then_inc(S("g_dend"), 1)
                    if not has_inv:
                        return
                    if d == 0:
                        g.wait_ge(S("v_s2"), 3)
                        if first:
                            g.wait_ge(S("g_dend"), 5)
                        for z in range(2):
                            if z:
                                g.wait_ge(S("g_vz"), 1)
                            g.tensor_copy(Vz[64 * z:64 * z + 64, :, 64 * z:64 * z + 64],
                                          vr[64 * z:64 * z + 64, :].rearrange("p (c t) -> p c t", c=NC)).then_inc(S("g_vz"), 1)
                        g.wait_ge(S("g_vz"), 2)
                    g.wait_ge(S("v_L"), 1)
                    g.wait_ge(S("a_lw"), 1)
                    g.tensor_tensor(Lx, Lc, sw, ALU.subtract).then_inc(S("g_Lx"), 1)
                    if d == 1:
                        g.tensor_copy(Vt[1], Vt[0]).then_inc(S("g_vb"), 1)
                    for c in range(4):
                        g.wait_ge(S("v_g"), 2 * c + 1)
                        for c2 in range(2 * c, 2 * c + 2):
                            g.tensor_tensor(G1[d][:, c2, 0:P], G1[d][:, c2, 0:P], ident[:, :], ALU.add)\
                             .then_inc(S("g_in"), 1)
                    if d == 0:
                        g.wait_ge(S("p_bt"), 6)
                    for q in range(2):
                        g.wait_ge(S("g_in"), 4 * q + 4)
                        for c in range(4 * q, 4 * q + 4):
                            g.tensor_tensor(XT[d][:, c, :], G1[d][:, c, 0:P], maskL[1 - d][0], ALU.mult)\
                             .then_inc(S("g_Y"), 1)
                    g.wait_ge(S("g_Y"), NC)
                rw_regions(g, half, meet)
                for _ in range(3):
                    meet(g)
                with g.Fori(0, 8) as n:
                    for j in range(4):
                        g.wait_ge(S(f"ev{j}"), n + 2)
                        g.tensor_tensor(ff[:, 4 * n + j, :], ff[:, 4 * n + j, :], ff[:, 4 * n + j, :], ALU.mult)\
                         .then_inc(S("g_set"), 1)
                g.wait_ge(S("g_set"), 32)
                for _ in range(3):
                    meet(g)

        @block.vector
        def _(v):
            v.memset(ones[:, :], 1.0).then_inc(S("v_set"), 1)
            v.memset(gbias[:, :], 0.0).then_inc(S("v_set"), 1)
            v.memset(eps[:, 0:1], 1e-5).then_inc(S("v_set"), 1)
            v.wait_ge(S("ld_par"), 64)
            v.tensor_copy(ident[:, :], craw[:, CI:CI + P]).then_inc(S("v_set"), 1)
            v.tensor_copy(bd[:, :], craw[:, CBD:CBD + P]).then_inc(S("v_set"), 1)
            v.tensor_copy(mask[:, :], craw[:, CG:NCONST]).then_inc(S("v_set"), 1)
            v.memset(eps[:, 1:2], 64e-5).then_inc(S("v_set"), 1)
            v.wait_ge(S("p_tr"), 1)
            v.tensor_copy(lncol[:, :, 0], ps[:, 7, 0:24]).then_inc(S("v_tr"), 1)
            for t in range(KT):
                v.wait_ge(S("p_tr"), t + 2)
                v.tensor_copy(hT[:, t, :], ps[:, t % 4, :]).then_inc(S("v_tr"), 1)
            v.wait_ge(S("v_tr"), KT + 1)
            ln_dve(v, lambda t: lncol[:, t, :])
            v.wait_ge(S("a_set"), 1)
            v.tensor_tensor(cond[:, 8:16, :], cond[:, 0:8, :], lncol[:, 16:24, :], ALU.mult).then_inc(S("v_set"), 1)
            v.wait_ge(S("v_set"), 8)
            meet(v)
            with v.Fori(0, DEPTH) as l:
                v.memset(prow[96:128, 1, :], 0.0).then_inc(S("v_set"), 1)
                v.wait_ge(S("p_tr"), 1)
                for b in range(3):
                    n = P if b < 2 else 48
                    v.tensor_copy(pcol[:, b * P:b * P + n, 0], ps[:, b, 0:n]).then_inc(S("v_tr"), 1)
                v.wait_ge(S("v_tr"), 3)
                cmu = COL["mup"]
                v.tensor_tensor(mix0[:, 0:24, 0], pcol[:, cmu:cmu + 24, 0], pcol[:, cmu + 24:cmu + 48, 0], ALU.add).then_inc(S("v_gate"), 1)
                lo_ = COL["mup_lo"]
                v.tensor_tensor(mix0[:, 24:27, 0], pcol[:, lo_:lo_ + 3, 0], pcol[:, lo_ + 3:lo_ + 6, 0], ALU.add).then_inc(S("v_gate"), 1)
                v.tensor_tensor(mix0[:, 27:28, 0], pcol[:, lo_ + 6:lo_ + 7, 0], pcol[:, lo_ + 7:lo_ + 8, 0], ALU.add).then_inc(S("v_gate"), 1)
                v.tensor_scalar(ka1[:, :, 0], pcol[:, COL["k_a"]:COL["k_a"] + 8, 0], -1.0, 1.0, ALU.mult, ALU.add).then_inc(S("v_gate"), 1)
                v.wait_ge(S("v_gate"), 3)
                v.tensor_scalar(mix0[:, :, 0], mix0[:, :, 0], -1.0, 1.0, ALU.mult, ALU.add).then_inc(S("v_gate"), 1)
                v.wait_ge(S("p_mm0"), 6)
                v.wait_ge(S("p_mm1"), 6)
                v.tensor_tensor(mod[:, :, 0], ps[:, 3, 0:48], pcol[:, 256:304, 0], ALU.add).then_inc(S("v_gate"), 1)
                v.wait_ge(S("v_gate"), 6)
                for o in (8, 16, 32, 40):
                    v.tensor_scalar(mod[:, o:o + 8, 0], mod[:, o:o + 8, 0], 1.0, None, ALU.add).then_inc(S("v_gate"), 1)
                v.wait_ge(S("v_gate"), 10)
                meet(v)
                v.memset(zero, 0.0).then_inc(S("v_set"), 1)
                v.memset(one, 1.0).then_inc(S("v_set"), 1)
                modulate(v, 0)
                for j, (x, n) in enumerate(((tw, P), (ad, P), (gd, P), (gd2, 32))):
                    mp = pcol[0:n, COL["mup_lo"] + j, :] if j < 3 else pcol[0:32, COL["mup_g2"], :]
                    mn = pcol[0:n, COL["mun_lo"] + j, :] if j < 3 else pcol[0:32, COL["mun_g2"], :]
                    shift(v, x[0:n, :], ps[0:n, j, :], mp, mn, j)
                v.wait_ge(S("a_gate"), 5)
                v.scalar_tensor_tensor(gx[:, 5, :], gx[:, 1, :], 0.0, gx[:, 4, :], ALU.min, ALU.subtract).then_inc(S("v_gate"), 1)
                v.wait_ge(S("v_gate"), 1)
                v.wait_ge(S("v_set"), 2)
                v.tensor_tensor_scan(Gs[0:32, :], one[0:32, :], gx[0:32, 5, :], 0.0, ALU.mult, ALU.add).then_inc(S("v_gate"), 1)
                v.tensor_tensor_scan(Gs[32:64, ::-1], one[32:64, :], gx[32:64, 5, ::-1], 0.0, ALU.mult, ALU.add).then_inc(S("v_gate"), 1)
                v.wait_ge(S("v_gate"), 3)
                v.tensor_tensor(aS, gx[:, 0, :], Gs, ALU.subtract).then_inc(S("v_gate"), 1)
                v.wait_ge(S("v_gate"), 4)
                v.tensor_tensor_scan(gx[0:32, 2, :], zero[0:32, :], aS[0:32, :], -3e38, ALU.add, ALU.max).then_inc(S("v_gate"), 1)
                v.tensor_tensor_scan(gx[32:64, 2, ::-1], zero[32:64, :], aS[32:64, ::-1], -3e38, ALU.add, ALU.max).then_inc(S("v_gate"), 1)
                v.wait_ge(S("v_gate"), 6)
                v.tensor_scalar(rows[:, 0, :], gx[:, 2, :], -1.0, None, ALU.mult).then_inc(S("v_gate"), 1)
                v.wait_ge(S("v_gate"), 7)
                v.tensor_tensor(rows[:, 1, :], rows[:, 0, :], Gs, ALU.subtract).then_inc(S("v_gate"), 1)
                v.wait_ge(S("v_gate"), 8)
                meet(v)
                with v.Fori(0, HA) as h:
                    for d in range(2):
                        v.tensor_copy(selh[:, d, :], ident[0:64, ds(32 * d + h, 1)].broadcast_to([64, P])).then_inc(S("v_sel"), 1)
                    for j in range(2):
                        v.wait_ge(S("a_c0"), j + 1)
                        for n, tap in enumerate((0, 1, 3, 4)):
                            o = tap - 2
                            dst = slice(max(0, -o), T - max(0, o))
                            src = slice(max(0, o), T - max(0, -o))
                            if n:
                                v.wait_ge(S("v_conv"), 4 * j + n)
                            v.scalar_tensor_tensor(qk[:, j, dst], ps[:, j, src], pcol[:, 8 * tap + 4 * j + h, :],
                                                   qk[:, j, dst], ALU.mult, ALU.add).then_inc(S("v_conv"), 1)
                    for j in range(2):
                        v.wait_ge(S("a_sig"), j + 1)
                        v.scalar_tensor_tensor(qk[:, j, :], qk[:, j, :], 1.0 if j == 0 else DK ** -0.5, sg[:, j, :],
                                               ALU.mult, ALU.mult).then_inc(S("v_qk"), 1)
                    nE = 0
                    for d in range(2):
                        v.wait_ge(S("p_nm"), d + 1)
                        if d:
                            v.wait_ge(S("a_E"), 7)
                        for t in range(NT):
                            v.tensor_tensor(dg[:, t, :], ps[:, 6, t * P:(t + 1) * P], maskC[d], ALU.add).then_inc(S("v_dg"), 1)
                        if d:
                            v.wait_ge(S("p_num"), 2)
                        for t in range(NT):
                            lo_, hi_ = (t * P, T) if d == 0 else (0, (t + 1) * P)
                            nE += 2 if hi_ - lo_ > P else 1
                            v.wait_ge(S("a_E"), nE)
                            v.wait_ge(S("p_s"), t + 1)
                            v.tensor_tensor(Pw[:, t, lo_:hi_], ps[:, t, lo_:hi_], Ew[:, t, lo_:hi_], ALU.mult).then_inc(S("v_P"), 1)
                        v.wait_ge(S("p_den"), d + 1)
                        v.wait_ge(S("a_emx"), d + 1)
                        v.tensor_scalar(rf, ps[:, 7, :], -1.0, None, ALU.mult).then_inc(S("v_gate"), 1)
                        v.wait_ge(S("v_gate"), 3 * d + 1)
                        v.tensor_tensor(rf, ps[:, 7, :], rf, ALU.max).then_inc(S("v_gate"), 1)
                        v.wait_ge(S("v_gate"), 3 * d + 2)
                        v.tensor_tensor(rf, rf, emx, ALU.max).then_inc(S("v_den"), 1)
                        v.wait_ge(S("v_den"), d + 1)
                        v.reciprocal(rf, rf).then_inc(S("v_gate"), 1)
                        v.wait_ge(S("v_gate"), 3 * d + 3)
                        for c in range(2):
                            v.wait_ge(S("p_num"), 2 * d + c + 1)
                            v.tensor_tensor((hs if d == 0 else ht)[:, c, :], ps[:, 4 + c, :], rf, ALU.mult).then_inc(S("v_num"), 1)
                        v.wait_ge(S("v_num"), 2 * d + 2)
                    for c in range(2):
                        v.tensor_tensor(hs[:, c, :], hs[:, c, :], ht[:, c, :], ALU.add).then_inc(S("v_h"), 1)
                    v.wait_ge(S("p_m2"), 1)
                    v.wait_ge(S("v_h"), 2)
                    for c in range(2):
                        v.scalar_tensor_tensor(hs[:, c, :], ps[:, 6, :], -1.0 / DV, hs[:, c, :], ALU.mult, ALU.add).then_inc(S("v_h"), 1)
                    v.wait_ge(S("a_std"), 1)
                    v.reciprocal(rf, hstd).then_inc(S("v_rstd"), 1)
                    v.wait_ge(S("v_rstd"), 1)
                    v.wait_ge(S("v_h"), 4)
                    v.wait_ge(S("a_h2"), 2)
                    for c in range(2):
                        v.scalar_tensor_tensor(hs[:, c, :], hs[:, c, :], pcol[:, COL["norm_g"] + 2 * h + c, :], rf, ALU.mult,
                                               ALU.mult).then_inc(S("v_nrm"), 1)
                    v.wait_ge(S("v_nrm"), 2)
                    v.wait_ge(S("a_o"), 2)
                    for c in range(2):
                        v.tensor_tensor(yA[:, 2 * h + c, :], hs[:, c, :], so[:, c, :], ALU.mult).then_inc(S("v_out"), 1)
                    v.wait_ge(S("v_out"), 2)
                    meet(v)

                def half(d, has_inv, has_chain, post, first, hp):
                    def ch(x):
                        return x.rearrange("p (c t) -> p c t", c=NC)

                    def bdiag(dst, x, y):
                        for z in range(2):
                            h0, h1 = 64 * z, 64 * z + 64
                            v.tensor_tensor(dst[h0:h1, :, h0:h1], ch(x)[h0:h1], ch(y)[h0:h1], ALU.mult).then_inc(S("v_bd"), 1)

                    if has_inv:
                        if d == 0:
                            for j, x in enumerate((rr, kr, vr)):
                                shift(v, x, ps[:, j, :], pcol[:, COL["mup"] + 8 * j + hp, :], pcol[:, COL["mun"] + 8 * j + hp, :], j)
                            v.wait_ge(S("v_s2"), 3)
                            v.wait_ge(S("p_ss"), 1)
                            v.tensor_scalar(Ex, ps[:, 5, :], 1e-24, None, ALU.max).then_inc(S("v_ss"), 1)
                    if post:
                        v.wait_ge(S("p_pm"), 1)
                        v.scalar_tensor_tensor(ysum, ps[:, 0, :], -1.0 / C, ysum, ALU.mult, ALU.add).then_inc(S("v_pc"), 1)
                    if has_inv:
                        v.wait_ge(S("a_lw"), 1)
                        if d == 0:
                            v.tensor_tensor_scan(Lc, maskR[0], sw, 0.0, ALU.mult, ALU.add).then_inc(S("v_L"), 1)
                        else:
                            v.tensor_tensor_scan(Lc[:, ::-1], maskR[1][:, ::-1], sw[:, ::-1], 0.0, ALU.mult, ALU.add).then_inc(S("v_L"), 1)
                        v.wait_ge(S("a_lw"), 2)
                        kmd = kmf if d == 0 else km
                        if d == 1:
                            v.wait_ge(S("g_Lx"), 1)
                        v.tensor_scalar(kmd, aa, pcol[:, COL["k_a"] + hp, :], ka1[:, hp, :], ALU.mult, ALU.add).then_inc(S("v_km"), 1)
                        v.wait_ge(S("v_km"), 1)
                        v.tensor_tensor(kmd, kmd, kr, ALU.mult).then_inc(S("v_km"), 1)
                        if d == 0:
                            v.wait_ge(S("a_nrm"), 1)
                            v.reciprocal(Ex, Ex).then_inc(S("v_ss"), 1)
                            v.wait_ge(S("v_ss"), 2)
                            v.scalar_tensor_tensor(kk, kr, pcol[:, COL["k_k"] + hp, :], Ex, ALU.mult, ALU.mult).then_inc(S("v_kk"), 1)
                            v.wait_ge(S("v_kk"), 1)
                        v.scalar_tensor_tensor(aa, kk, -1.0, aa, ALU.mult, ALU.mult).then_inc(S("v_km"), 1)
                        v.wait_ge(S("v_km"), 3)
                    if post:
                        v.wait_ge(S("a_pstd"), 1)
                        v.reciprocal(yf, yf).then_inc(S("v_pr"), 1)
                        v.wait_ge(S("v_pr"), 1)
                        v.scalar_tensor_tensor(ysum, ysum, pcol[:, COL["gn_g"] + hp - 1, :] if has_inv else pcol[:, COL["gn_g"] + HP - 1, :],
                                               yf, ALU.mult, ALU.mult).then_inc(S("v_py"), 1)
                        v.wait_ge(S("v_py"), 1)
                        v.scalar_tensor_tensor(ysum, ysum, pcol[:, COL["gn_b"] + hp - 1, :] if has_inv else pcol[:, COL["gn_b"] + HP - 1, :],
                                               bonus, ALU.add, ALU.add).then_inc(S("v_py"), 1)
                        v.wait_ge(S("v_py"), 2)
                        v.tensor_tensor(yB[:, hp - 1 if has_inv else HP - 1, :], ysum, gbuf, ALU.mult).then_inc(S("v_py"), 1)
                        if not has_inv:
                            v.wait_ge(S("v_py"), 3)
                    if has_inv:
                        if d == 1:
                            if post:
                                v.wait_ge(S("v_py"), 3)
                            v.tensor_tensor(Ex, km, kmf, ALU.add).then_inc(S("v_rk"), 1)
                            v.wait_ge(S("v_rk"), 1)
                            v.scalar_tensor_tensor(Ex, rr, pcol[:, COL["r_k"] + hp, :], Ex, ALU.mult, ALU.mult).then_inc(S("v_rk"), 1)
                            v.wait_ge(S("p_bon"), 1)
                            v.tensor_tensor(bonus, ps[:, 2, :], vr, ALU.mult).then_inc(S("v_bon"), 1)
                        if first:
                            v.wait_ge(S("g_dend"), 5)
                        v.wait_ge(S("a_exp"), 3)
                        v.tensor_copy(dend[d], Ep[:, (C - 1 if d == 0 else 0):T:C]).then_inc(S("v_dend"), 1)
                        bdiag(Bz, aa, En)
                        bdiag(AQ[d], kk, Ex)
                        v.tensor_tensor(AQ[d][:, :, P:P + C], ch(rr), ch(Ep), ALU.mult).then_inc(S("v_bd"), 1)
                        bdiag(Kz, kmd, En)
                        for b in range(NC):
                            v.wait_ge(S("p_g"), b + 1)
                            G = G1[d] if b % 2 == 0 else G3[d]
                            c0 = 2 * (b // 2)
                            v.tensor_tensor(G[:, c0:c0 + 2, :], ps[:, b % 6, 0:384].rearrange("p (c x) -> p c x", c=2),
                                            maskG[d].rearrange("p (o x) -> p o x", o=1).broadcast_to([P, 2, 192]), ALU.mult)\
                             .then_inc(S("v_g"), 1)
                    for n in range(24):
                        if has_inv:
                            k, ph, q = n // 4, n // 2 % 2, n % 2
                            if ph == 0:
                                v.wait_ge(S("p_T"), 2 * k + q + 1)
                                if k >= 2:
                                    v.wait_ge(S("p_XY"), 2 * (k - 2) + q + 1)
                                if k == 0:
                                    v.wait_ge(S("v_bd"), 7)
                                R = Xm if k == 0 else Rm
                                v.tensor_tensor(R[:, 4 * q:4 * q + 4, :], ps[:, 3 * q, :].rearrange("p (c x) -> p c x", c=4),
                                                maskL[d][k].rearrange("p (o x) -> p o x", o=1).broadcast_to([P, 4, P]), ALU.mult)\
                                 .then_inc(S("v_R"), 1)
                        if has_chain:
                            cd = 1 - d
                            i, ph = n // 3, n % 3
                            c = i if cd == 0 else NC - 1 - i
                            S_in, S_out = Sst[:, (i + 1) % 2, :], Sst[:, i % 2, :]
                            if ph == 1:
                                if i and i < NC - 1:
                                    v.tensor_scalar(Sd, S_in, dend[cd][:, c:c + 1], None, ALU.mult).then_inc(S("v_Sd"), 1)
                                v.wait_ge(S("p_U"), i + 1)
                                if i:
                                    v.wait_ge(S("p_Y"), i)
                                v.tensor_copy(Us, ps[:, 7, 0:P]).then_inc(S("v_U"), 1)
                            elif ph == 2:
                                if i < NC - 1:
                                    v.wait_ge(S("p_S"), i + 1)
                                    if i:
                                        v.wait_ge(S("v_Sd"), i)
                                        v.scalar_tensor_tensor(S_out, ps[:, 6, P:2 * P], dend[cd][:, c:c + 1], Sd, ALU.mult, ALU.add)\
                                         .then_inc(S("v_S"), 1)
                                    else:
                                        v.tensor_scalar(S_out, ps[:, 6, P:2 * P], dend[cd][:, c:c + 1], None, ALU.mult).then_inc(S("v_S"), 1)
                                    v.wait_ge(S("v_S"), i + 1)
                                if cd == 1:
                                    v.wait_ge(S("p_Y"), i + 1)
                                    v.tensor_tensor(ysum[:, c * C:(c + 1) * C], yf[:, c * C:(c + 1) * C], ps[:, 7, P:P + C], ALU.add)\
                                     .then_inc(S("a_y"), 1)
                    if has_chain and d == 0:
                        v.wait_ge(S("a_y"), NC)
                    elif has_chain:
                        v.wait_ge(S("v_U"), NC)
                    elif has_inv:
                        v.wait_ge(S("v_R"), 2 * LEVELS)
                rw_regions(v, half, meet)
                v.sem_inc(S("v_out"), 1)
                for j in range(2):
                    v.sem_inc(S(f"ev{2 * j + 1}"), 1)
                with v.Fori(0, KT) as n:
                    v.wait_ge(S("v_out"), n + 1)
                    for j in range(2):
                        v.wait_ge(S(f"ev{2 * j}"), n + 2)
                        v.wait_ge(S(f"p_mm{2 * j + 1}"), n + 1)
                        v.tensor_tensor(pa_[:, j, :], ps[:, 2 * j + 1, :], sga[:, j, :], ALU.mult).then_inc(S(f"ev{2 * j + 1}"), 1)
                    v.wait_ge(S("ev1"), n + 2)
                    v.wait_ge(S("ev3"), n + 2)
                    v.tensor_tensor(merged[:, n, :], pa_[:, 0, :], pa_[:, 1, :], ALU.add).then_inc(S("v_out"), 1)
                v.wait_ge(S("v_out"), KT + 1)
                meet(v)
                scale_h(v)
                for j in range(4):
                    v.sem_inc(S(f"ev{j}"), 1)
                with v.Fori(0, 2) as n:
                    for j in range(4):
                        v.wait_ge(S(f"p_mm{j}"), n + 1)
                        v.scalar_tensor_tensor(hT[:, 4 * n + j, :], ps[:, j, :], mod[:, 16 + 4 * n + j, :], hT[:, 4 * n + j, :],
                                               ALU.mult, ALU.add).then_inc(S(f"ev{j}"), 1)
                for j in range(4):
                    v.wait_ge(S(f"ev{j}"), 3)
                meet(v)
                ln_dve(v, lambda t: pcol[:, COL["ln1_g"] + t, :])
                meet(v)
                modulate(v, 24)
                meet(v)
                scale_h(v)
                v.sem_inc(S("ev0"), 1)
                with v.Fori(0, 8) as n:
                    v.wait_ge(S("p_mm3"), n + 1)
                    v.tensor_scalar(fr[:, 0, :], ps[:, 0, :], pcol[:, COL["b2"] + n, :], mod[:, 40 + n, :], ALU.add, ALU.mult)\
                     .then_inc(S("ev0"), 1)
                    v.wait_ge(S("ev0"), n + 2)
                    v.tensor_tensor(hT[:, n, :], hT[:, n, :], fr[:, 0, :], ALU.add).then_inc(S("v_out"), 1)
                    v.wait_ge(S("v_out"), n + 1)
                meet(v)
                ln_dve(v, lambda t: pcol[:, COL["ln2_g"] + t, :])
                meet(v)
            for b in range(2 * NT):
                v.wait_ge(S("p_tr"), b + 1)
                v.tensor_copy(xtok[:, b // 2, (b % 2) * 512:(b % 2 + 1) * 512], ps[:, b % 4, :]).then_inc(S("v_tr"), 1)


def kernel(**inputs):
    import concourse.bacc as _bacc
    from concourse.bass_utils import run_bass_kernel_spmd as _run

    nc = _bacc.Bacc("TRN2", target_bir_lowering=False, num_devices=1)
    arrays, args = {}, {}
    for name, x in inputs.items():
        x = np.ascontiguousarray(x)
        arrays[f"in_{name}"] = x
        args[name] = nc.dram_tensor(f"in_{name}", x.shape, mybir.dt.from_np(x.dtype), kind="ExternalInput").ap()
    arrays["in_consts"] = constants()
    consts = nc.dram_tensor("in_consts", (P, NCONST), F32, kind="ExternalInput").ap()
    out = nc.dram_tensor("out_h", (1, T, D), F32, kind="ExternalOutput").ap()
    encoder(nc, args, consts, out)
    r = _run(nc, [arrays], core_ids=[0])
    return r.results[0]["out_h"]
```

```python
from contextlib import ExitStack

import numpy as np
import concourse.bass as bass
from concourse import mybir

ALU = mybir.AluOpType
ACT = mybir.ActivationFunctionType
F32 = mybir.dt.float32
F32R = mybir.dt.float32r
BF16 = mybir.dt.bfloat16
ds = bass.ds

P = 128
D = 1024
T = 512
DEPTH = 2
KT = D // P
NT = T // P
HA = 4
DK = 128
DV = 256
FF = 4 * D
FT = FF // P
C = 64
NC = T // C
HP = 8
LORA = 64
GLORA = 160
N_RW = 3 * D + 4 * LORA + GLORA
QK0, V0, O0, G0, Z0 = 0, D, 2 * D, 3 * D, 3 * D + 16
GA0 = Z0 + N_RW
GB0 = GA0 + D
WD0, AD0, GD0 = Z0 + 3 * D, Z0 + 3 * D + 128, Z0 + 3 * D + 256
ALPHA = (2.0 * DEPTH) ** 0.25
DECAY = float(np.exp(-0.5))
LEVELS = 6
BIG = 1e30

B0 = dict(conv_w=0, conv_b=40, norm_g=48, w0=56, a0=72, k_k=88, k_a=96, r_k=104, gn_g=112, gn_b=120)
B1 = dict(mup=0, mun=24, ln1_g=48, ln1_b=56, b2=64, ln2_g=72, ln2_b=80, b1=88, mup_lo=120, mun_lo=123,
          mup_g2=126, mun_g2=127)
COL = {**B0, **{k: 128 + v for k, v in B1.items()}, "ada_b": 256}

CI, CBD, CG, CL, CR, CC = 0, 128, 256, 640, 640 + 12 * 128, 640 + 12 * 128 + 1024
NCONST = CC + 256


def constants():
    c = np.zeros((P, NCONST), np.float32)
    i = np.arange(P)
    c[:, CI:CI + P] = np.eye(P)
    same = (i[:, None] // C) == (i[None, :] // C)
    c[:, CBD:CBD + P] = same
    s, t = i[:, None] % C, i[None, :] % C
    q = np.arange(C)[None, :]
    for d in range(2):
        before = (s < t) if d == 0 else (s > t)
        upto = (s <= q) if d == 0 else (s >= q)
        c[:, CG + 192 * d:CG + 192 * d + 128] = same & before
        c[:, CG + 192 * d + 128:CG + 192 * d + 192] = upto
        for k in range(LEVELS):
            pair = same & ((s >> (k + 1)) == (t >> (k + 1))) & ((s >> k) != (t >> k))
            low = pair & ((s > t) if d == 0 else (s < t))
            o = CL + (6 * d + k) * 128
            c[:, o:o + 128] = low | (i[:, None] == i[None, :])
        pos = np.arange(T) % C
        c[:, CR + T * d:CR + T * (d + 1)] = pos != (0 if d == 0 else C - 1)
        hidden = (i[:, None] > i[None, :]) if d == 0 else (i[:, None] < i[None, :])
        c[:, CC + 128 * d:CC + 128 * (d + 1)] = np.where(hidden, -BIG, 0.0)
    return c


def encoder(nc, a, consts, out):
    ctx = ExitStack()
    h_dram = nc.dram_tensor("h_dram", (P, KT, T), F32).ap()
    with ctx:
        def sb(name, shape, dt=F32):
            return ctx.enter_context(nc.sbuf_tensor(name, shape, dt))

        NA = 28100
        both = ExitStack()
        uT = both.enter_context(nc.sbuf_tensor("uT", [P, KT, T], F32))
        yA = both.enter_context(nc.sbuf_tensor("yA", [P, KT, T], F32))
        yB = both.enter_context(nc.sbuf_tensor("yB", [P, KT, T], F32))
        arena = both.enter_context(nc.sbuf_tensor("arena", [P, NA], F32))
        both.close()
        o_uh = NC * 2 * 192 * 3 + NC * P * 8
        o_ah = o_uh + NC * P * 4 + 2 * NC + 5 * P
        ul = sb("ul", [P, KT, T], F32R)
        abl = sb("abl", [P, 2 * KT, T], F32R)
        wh = sb("wh", [P, 4, KT, P], F32R)
        wl = sb("wl", [P, 4, KT, P], F32R)
        hh = sb("hh", [P, 2 * KT, T], F32R)
        sb("skip0", [P, o_uh - 16 * D])
        uh = sb("uh", [P, KT, T], F32R)
        sb("skip1", [P, o_ah - o_uh - KT * T])
        ah = sb("ah", [P, KT, T], F32R)
        sb("skip2", [P, NA - o_ah - KT * T])

        hT = sb("hT", [P, KT, T])
        wt = sb("wt", [P, 4, KT, P])
        pcol = sb("pcol", [P, 3 * P, 1])
        mod = sb("mod", [P, 48, 1])
        mix0 = sb("mix0", [P, 28, 1])
        ka1 = sb("ka1", [P, KT, 1])
        b2g = sb("b2g", [P, KT])
        lncol = sb("lncol", [P, 24, 1])
        cond = sb("cond", [P, 16, 1])
        eps = sb("eps", [P, 2])
        gbias = sb("gbias", [64, 2])
        ident = sb("ident", [P, P])
        bd = sb("bd", [P, P])
        ones = sb("ones", [P, P])
        mask = sb("mask", [P, NCONST - CG], BF16)
        tw = sb("tw", [P, T])
        ad = sb("ad", [P, T])
        gd = sb("gd", [P, T])
        gd2 = sb("gd2", [P, T])
        ps = ctx.enter_context(nc.psum_tensor("ps", [P, 8, 512], F32))

        class Carve:
            def __init__(self):
                self.at = 0

            def __call__(self, *shape, parts=P):
                n = int(np.prod(shape))
                v = arena[0:parts, self.at:self.at + n]
                self.at += n
                assert self.at <= NA, self.at
                if len(shape) == 2:
                    v = v.rearrange("p (a b) -> p a b", a=shape[0])
                if len(shape) == 3:
                    v = v.rearrange("p (a b c) -> p a b c", a=shape[0], b=shape[1])
                return v

        def m(o, n):
            return mask[:, o - CG:o - CG + n]

        maskG = [m(CG + 192 * d, 192) for d in range(2)]
        maskL = [[m(CL + (6 * d + k) * 128, 128) for k in range(LEVELS)] for d in range(2)]
        maskR = [m(CR + T * d, T) for d in range(2)]
        maskC = [m(CC + 128 * d, 128) for d in range(2)]

        cv = Carve()
        craw = cv(NCONST)
        xtok = cv(NT, D)
        sq8 = cv(KT, T)
        prow = cv(3, P)
        std = cv(T)
        rstd = cv(T)
        cv = Carve()
        adaw = cv(2 * KT, 512).rearrange("p (s k) n -> p s k n", s=2)
        adas = cv(2, 512)
        cv = Carve()
        wg16 = cv(KT, 16)
        wgp = cv(KT, 2, 64)
        gx = cv(6, T, parts=64)
        rows = cv(2, T)
        Gs = cv(T, parts=64)
        aS = cv(T, parts=64)
        zero = cv(T, parts=64)
        one = cv(T, parts=64)
        acol = cv(NT, 64)
        selh = cv(2, P)
        wv = cv(KT, DV)
        qk = cv(2, T)
        sg = cv(2, T)
        vtok = cv(NT, DV)
        so = cv(2, T)
        Ew = cv(NT, T)
        Pw = cv(NT, T)
        dg = cv(NT, P)
        emx = cv(T)
        rf = cv(T)
        hs = cv(2, T)
        ht = cv(2, T)
        hq = cv(2, T)
        hstd = cv(T)
        cv = Carve()
        AQ = [cv(NC, 192) for _ in range(2)]
        G1 = [cv(NC, 192) for _ in range(2)]
        G3 = [cv(NC, 192) for _ in range(2)]
        XT = [cv(NC, P) for _ in range(2)]
        Bt = [cv(NC, P) for _ in range(2)]
        Ktk = [cv(NC, P) for _ in range(2)]
        Vt = [cv(NC, P) for _ in range(2)]
        Bz = cv(NC, P)
        Kz = cv(NC, P)
        Xm = cv(NC, P)
        Rm = cv(NC, P)
        dend = [cv(NC) for _ in range(2)]
        Sst = cv(2, P)
        Sd = cv(P)
        Zs = cv(P)
        Us = cv(P)
        assert cv.at == NC * 2 * 192 * 3 + NC * P * 12 + 2 * NC + 5 * P
        rr, kr, vr, kk = cv(T), cv(T), cv(T), cv(T)
        sw, aa, kmf, Ex, ysum, yf = cv(T), cv(T), cv(T), cv(T), cv(T), cv(T)
        km = sw
        Lc, Lx, Ep, En, rks = (hT[:, q, :] for q in range(5))
        spare = wt[:, 3, :, :].rearrange("p a b -> p (a b)")
        bonus, gbuf = spare[:, 0:T], spare[:, T:2 * T]
        wup = cv(2, 2, P)
        gup = cv(P)
        gup2 = cv(P)
        kr_sq = En
        ysq = yB[:, HP - 1, :]
        Vz = XT[0]
        al, bl = abl[:, 0:KT, :], abl[:, KT:2 * KT, :]
        bh = hh[:, 0:KT, :]
        mh, ml = uh, hh[:, KT:2 * KT, :]
        merged = arena[:, 12 * D:16 * D].rearrange("p (a b) -> p a b", a=KT)
        pa_ = arena[:, 16 * D:17 * D].rearrange("p (a b) -> p a b", a=2)
        sga = arena[:, o_ah + KT * T:o_ah + KT * T + 2 * T].rearrange("p (a b) -> p a b", a=2)
        FH = FT // 2
        assert FH == 2 * KT
        fh, fl = hh, abl
        fr = arena[:, o_ah:o_ah + 4 * T].rearrange("p (a b) -> p a b", a=4)
        fsq = arena[:, o_ah + 4 * T:o_ah + 8 * T].rearrange("p (a b) -> p a b", a=4)

        sems = {}

        def S(name):
            if name not in sems:
                sems[name] = ctx.enter_context(nc.semaphore(name))
            return sems[name]

        arrived = [ctx.enter_context(nc.semaphore(f"arrived{j}")) for j in range(2)]
        opened = [ctx.enter_context(nc.semaphore(f"opened{j}")) for j in range(2)]

        cleared = [
            "ld_w0", "ld_w1", "ld_w2", "ld_w3", "ld_par", "ld_x", "st_out",
            "p_tr", "v_tr", "p_mm0", "p_mm1", "p_mm2", "p_mm3", "ev0", "ev1", "ev2", "ev3",
            "p_mean", "v_cen", "a_sq", "p_var", "a_std", "v_rstd", "v_nrm", "v_out",
            "hi0", "hi1", "hi2", "hi3", "lo0", "lo1", "lo2", "lo3", "v_xh", "g_xl", "a_f", "v_sq", "v_fh", "g_fl",
            "g_set", "v_set", "a_set", "v_u",
            "a_c0", "v_s1", "v_s2", "a_act", "v_gate", "a_gate",
            "ld_v", "ld_up", "ld_gu", "st_h", "ld_h", "v_conv", "a_sig", "v_qk", "p_v", "a_v", "a_o", "v_sel", "p_s", "p_nm", "p_nx",
            "v_dg", "a_E", "a_emx", "v_P", "p_den", "v_den", "p_num", "v_num", "v_h", "p_m2", "a_h2",
            "a_kk", "p_ss", "v_ss", "a_nrm", "v_kk", "p_lw", "a_lw", "v_L", "g_Lx", "a_exp", "v_km", "v_bd",
            "g_dend", "v_dend", "p_g", "v_g", "g_in", "p_bt", "a_bt", "g_vz", "g_vb",
            "p_T", "v_R", "g_Y", "p_XY", "a_X", "a_Y",
            "p_Z", "a_Z", "p_U", "v_U", "p_S", "v_Sd", "v_S", "p_Y", "a_y",
            "p_pm", "v_pc", "a_psq", "p_pv", "a_pstd", "v_pr", "v_py", "v_rk", "p_bon", "v_bon", "p_gu", "a_gu",
        ]
        for n in cleared:
            S(n)
        lo = min(sems[n].num for n in cleared)
        hi = max(sems[n].num for n in cleared)
        assert hi - lo + 1 == len(cleared)

        def meet(e):
            e.sem_inc(arrived[0], 1)
            e.wait_ge(opened[0], 1)
            e.sem_inc(arrived[1], 1)
            e.wait_ge(opened[1], 1)

        def meet_sp(e):
            e.wait_ge(arrived[0], 4)
            e.sem_clear(range(lo, hi + 1))
            e.sem_clear(arrived[0])
            e.sem_clear(opened[1])
            e.sem_inc(opened[0], 1)
            e.wait_ge(arrived[1], 4)
            e.sem_clear(arrived[1])
            e.sem_clear(opened[0])
            e.sem_inc(opened[1], 1)

        block = ctx.enter_context(nc.Block())
        w_in, w_a, w_b, w_o = a["w_in"], a["w_branch_a"], a["w_branch_b"], a["w_out"]

        def ln_pe(p):
            for t in range(KT):
                mm = p.matmul(ps[:, 0, :], ones[:, 0:P], hT[:, t, :], start=t == 0, stop=t == KT - 1)
            mm.then_inc(S("p_mean"), 1)
            for t in range(KT):
                p.wait_ge(S("a_sq"), t + 1)
                mm = p.matmul(ps[:, 1, :], ones[:, 0:P], sq8[:, t, :], start=t == 0, stop=t == KT - 1)
            mm.then_inc(S("p_var"), 1)

        def ln_act(s, b):
            for t in range(KT):
                s.wait_ge(S("v_cen"), t + 1)
                s.activation(sq8[:, t, :], hT[:, t, :], ACT.Square).then_inc(S("a_sq"), 1)
            s.wait_ge(S("p_var"), 1)
            s.activation(std, ps[:, 1, :], ACT.Sqrt, bias=eps[:, 0:1], scale=1.0 / D).then_inc(S("a_std"), 1)
            for t in range(KT):
                s.wait_ge(S("v_nrm"), t + 1)
                s.activation(hT[:, t, :], hT[:, t, :], ACT.Identity, bias=b(t)).then_inc(S("v_out"), 1)
            s.wait_ge(S("v_out"), KT)

        def ln_dve(v, g):
            v.wait_ge(S("p_mean"), 1)
            for t in range(KT):
                v.scalar_tensor_tensor(hT[:, t, :], ps[:, 0, :], -1.0 / D, hT[:, t, :], ALU.mult,
                                       ALU.add).then_inc(S("v_cen"), 1)
            v.wait_ge(S("a_std"), 1)
            v.reciprocal(rstd, std).then_inc(S("v_rstd"), 1)
            v.wait_ge(S("v_rstd"), 1)
            v.wait_ge(S("a_sq"), KT)
            for t in range(KT):
                v.scalar_tensor_tensor(hT[:, t, :], hT[:, t, :], g(t), rstd, ALU.mult,
                                       ALU.mult).then_inc(S("v_nrm"), 1)

        def modulate(v, first):
            for t in range(KT):
                v.tensor_scalar(uT[:, t, :], hT[:, t, :], mod[:, first + 8 + t, :], mod[:, first + t, :],
                                ALU.mult, ALU.add).then_inc(S("v_u"), 1)

        def load_w(e, slot, src, col, n=P):
            e.dma_start(wt[:, slot, :, 0:n], src.rearrange("(k p) n -> p k n", p=P)[:, :, ds(col, n)])\
             .then_inc(S(f"ld_w{slot}"), 16)

        def dense(p, slot, bank, rhs, n=P):
            for k in range(KT):
                mm = p.matmul(ps[0:n, bank, :], wt[:, slot, k, 0:n], rhs[:, k, :], start=k == 0, stop=k == KT - 1)
            return mm

        def w_hi(v, j, i):
            v.wait_ge(S(f"ld_w{j}"), 16 * i + 16)
            v.wait_ge(S(f"p_mm{j}"), i + 1)
            v.tensor_copy(wh[:, j, :, :], wt[:, j, :, :]).then_inc(S(f"hi{j}"), 1)

        def w_lo(g, j, i):
            g.wait_ge(S(f"hi{j}"), i + 1)
            g.tensor_tensor(wl[:, j, :, :], wt[:, j, :, :], wh[:, j, :, :].bitcast(F32), ALU.subtract)\
             .then_inc(S(f"lo{j}"), 1)

        def dense3(p, j, i, bank, xh, xl, first=True, last=True):
            p.wait_ge(S(f"hi{j}"), i + 1)
            for n, x in enumerate((xh, xl)):
                for k in range(KT):
                    p.matmul(ps[:, bank, :], wh[:, j, k, :], x[:, k, :], start=first and n == 0 and k == 0, stop=False)
            p.wait_ge(S(f"lo{j}"), i + 1)
            for k in range(KT):
                mm = p.matmul(ps[:, bank, :], wl[:, j, k, :], xh[:, k, :], start=False, stop=last and k == KT - 1)
            mm.then_inc(S(f"p_mm{j}"), 1)

        def free(e, name):
            for j in range(4):
                e.sem_inc(S(f"{name}{j}"), 1)

        def x_hi(v, x, xh, t):
            v.tensor_copy(xh[:, t, :], x[:, t, :]).then_inc(S("v_xh"), 1)

        def x_lo(g, x, xh, xl, t, n):
            g.wait_ge(S("v_xh"), n + 1)
            g.tensor_tensor(xl[:, t, :], x[:, t, :], xh[:, t, :].bitcast(F32), ALU.subtract).then_inc(S("g_xl"), 1)

        def shift(v, x, z, mp, mn, j):
            v.wait_ge(S("a_c0"), j + 1)
            v.scalar_tensor_tensor(x[:, 1:T], z[:, 0:T - 1], mp, x[:, 1:T], ALU.mult, ALU.add).then_inc(S("v_s1"), 1)
            v.wait_ge(S("v_s1"), j + 1)
            v.scalar_tensor_tensor(x[:, 0:T - 1], z[:, 1:T], mn, x[:, 0:T - 1], ALU.mult, ALU.add)\
             .then_inc(S("v_s2"), 1)

        def scale_h(v):
            for t in range(KT):
                v.tensor_scalar(hT[:, t, :], hT[:, t, :], ALPHA, None, ALU.mult).then_inc(S("v_cen"), 1)
            v.wait_ge(S("v_cen"), KT)

        CHG = 6

        def rw_regions(e, half, meet_):
            half(1, False, False, False, True, -1)
            meet_(e)
            half(0, True, False, False, True, 0)
            meet_(e)
            half(1, True, True, False, True, 0)
            meet_(e)
            with e.Fori(1, HP - 1) as hp:
                half(0, True, True, False, True, hp)
                meet_(e)
                half(1, True, True, True, True, hp)
                meet_(e)
            half(0, True, True, False, True, HP - 1)
            meet_(e)
            half(1, True, True, True, False, HP - 1)
            meet_(e)
            half(0, False, True, False, False, HP)
            meet_(e)
            half(1, False, False, True, False, HP)
            meet_(e)

        @block.sync
        def _(e):
            e.dma_start(craw, consts).then_inc(S("ld_par"), 16)
            e.dma_start(xtok, a["x"][0].rearrange("(t p) d -> p t d", p=P)).then_inc(S("ld_x"), 16)
            for j, n in enumerate(("ln0_g", "ln0_b")):
                e.dma_start(prow[8 * j:8 * j + 8, 0, :], a[n].rearrange("(t p) -> t p", p=P))\
                 .then_inc(S("ld_par"), 16)
            e.dma_start(prow[16:24, 0, :], a["c"].rearrange("o (t p) -> (o t) p", p=P)).then_inc(S("ld_par"), 16)
            meet_sp(e)
            with e.Fori(0, DEPTH) as l:
                def par(row, blk, src, n=8):
                    e.dma_start(prow[row:row + n, blk, :], src).then_inc(S("ld_par"), 16)

                def vec(x):
                    return x.rearrange("(t p) -> t p", p=P)

                def vec2(x):
                    return x.rearrange("j (t p) -> (j t) p", p=P)
                par(B0["conv_w"], 0, vec2(a["mlstm_conv_w"][l]), 40)
                par(B0["conv_b"], 0, vec(a["mlstm_conv_b"][l]))
                par(B0["norm_g"], 0, vec(a["mlstm_norm_g"][l]))
                par(B0["w0"], 0, vec2(a["rwkv_w0"][l]), 16)
                par(B0["a0"], 0, vec2(a["rwkv_a0"][l]), 16)
                par(B0["k_k"], 0, vec(a["rwkv_k_k"][l]))
                par(B0["k_a"], 0, vec(a["rwkv_k_a"][l]))
                par(B0["r_k"], 0, a["rwkv_r_k"][l].rearrange("(t h) n -> t (h n)", h=2))
                par(B0["gn_g"], 0, vec(a["rwkv_gn_g"][l]))
                par(B0["gn_b"], 0, vec(a["rwkv_gn_b"][l]))
                mu = a["rwkv_mu"][l]
                e.wait_ge(S("v_set"), 1)
                par(B1["mup"], 1, vec(mu[0, 0:3 * D]), 24)
                par(B1["mun"], 1, vec(mu[1, 0:3 * D]), 24)
                par(B1["mup_lo"], 1, vec(mu[0, 3 * D:3 * D + 384]), 3)
                par(B1["mun_lo"], 1, vec(mu[1, 3 * D:3 * D + 384]), 3)
                for j in range(2):
                    e.dma_start(prow[126 + j:127 + j, 1, 0:32], mu[j:j + 1, 3 * D + 384:N_RW])\
                     .then_inc(S("ld_par"), 16)
                par(B1["ln1_g"], 1, vec(a["ln1_g"][l]))
                par(B1["ln1_b"], 1, vec(a["ln1_b"][l]))
                par(B1["b2"], 1, vec(a["mlp_b2"][l]))
                par(B1["ln2_g"], 1, vec(a["ln2_g"][l]))
                par(B1["ln2_b"], 1, vec(a["ln2_b"][l]))
                par(B1["b1"], 1, vec(a["mlp_b1"][l]), 32)
                par(0, 2, vec(a["ada_b"][l]), 48)
                for j, n in enumerate(("mlstm_ig_b", "mlstm_fg_b")):
                    for d in range(2):
                        e.dma_start(gbias[32 * d:32 * d + 4, j:j + 1], a[n][l][d].rearrange("(h o) -> h o", o=1))\
                         .then_inc(S("ld_par"), 16)
                ada = a["ada_w"][l].rearrange("(k p) n -> p k n", p=P)
                for s in range(2):
                    e.dma_start(adaw[:, s, :, :], ada[:, :, 512 * s:512 * s + 512]).then_inc(S(f"ld_w{s}"), 16)
                with e.Fori(0, 5) as i:
                    for s in range(2):
                        e.wait_ge(S(f"ev{s}"), KT * (i + 1))
                        e.dma_start(adaw[:, s, :, :], ada[:, :, ds((2 * i + 2 + s) * 512, 512)])\
                         .then_inc(S(f"ld_w{s}"), 16)
                e.wait_ge(S("ld_w0"), 96)
                meet_sp(e)
                for s, (col, n) in enumerate(((WD0, P), (AD0, P), (GD0, P), (GD0 + P, 32))):
                    load_w(e, s, w_in[l], col, n)
                e.dma_start(wg16, w_in[l].rearrange("(k p) n -> p k n", p=P)[:, :, G0:G0 + 16]).then_inc(S("ld_v"), 16)
                e.dma_start(h_dram, hT[:, :, :]).then_inc(S("st_h"), 16)
                e.wait_ge(S("st_h"), 16)
                meet_sp(e)
                with e.Fori(0, HA) as h:
                    load_w(e, 0, w_in[l], QK0 + h * DK)
                    load_w(e, 1, w_in[l], QK0 + 512 + h * DK)
                    e.dma_start(wv, w_in[l].rearrange("(k p) n -> p k n", p=P)[:, :, ds(V0 + h * DV, DV)])\
                     .then_inc(S("ld_v"), 16)
                    load_w(e, 2, w_in[l], O0 + h * DV)
                    load_w(e, 3, w_in[l], O0 + P + h * DV)
                    meet_sp(e)

                def rw_w(hp):
                    for s in range(3):
                        load_w(e, s, w_in[l], Z0 + s * D + hp * P)

                def rw_up(hp):
                    for j, n in enumerate(("rwkv_w_up", "rwkv_a_up")):
                        for d in range(2):
                            e.dma_start(wup[64 * d:64 * d + 64, j, d, :], a[n][l][d][:, ds(hp * P, P)])\
                             .then_inc(S("ld_up"), 16)

                def rw_gup(hp):
                    e.dma_start(gup, a["rwkv_g_up"][l][0:P, ds(hp * P, P)]).then_inc(S("ld_gu"), 16)
                    e.dma_start(gup2[0:GLORA - P, :], a["rwkv_g_up"][l][P:GLORA, ds(hp * P, P)]).then_inc(S("ld_gu"), 16)

                def half0(hp):
                    rw_w(hp + 1)
                    for s in range(3):
                        e.wait_ge(S(f"ld_w{s}"), 16)
                    meet_sp(e)

                def half1(hp):
                    rw_up(hp + 1)
                    e.wait_ge(S("p_gu"), 1)
                    rw_gup(hp + 1)
                    e.wait_ge(S("ld_gu"), 32)
                    meet_sp(e)
                rw_w(0)
                e.wait_ge(S("g_dend"), 2)
                rw_up(0)
                rw_gup(0)
                e.wait_ge(S("ld_gu"), 32)
                meet_sp(e)
                half0(0)
                half1(0)
                with e.Fori(1, HP - 1) as hp:
                    half0(hp)
                    half1(hp)
                meet_sp(e)
                meet_sp(e)
                merge_src, merge_col = [w_in[l], w_a[l], w_in[l], w_b[l]], [GA0, 0, GB0, 0]

                def stream(n_iter, load, loaded):
                    for s in range(4):
                        if s in loaded:
                            e.sem_inc(S(f"ld_w{s}"), 16)
                        else:
                            load(0, s)
                    with e.Fori(1, n_iter) as i:
                        for s in range(4):
                            e.wait_ge(S(f"lo{s}"), i)
                            load(i, s)

                def ahead(n_iter, load, slots=range(4)):
                    for s in slots:
                        if n_iter:
                            e.wait_ge(S(f"lo{s}"), n_iter)
                        load(0, s)
                    for s in slots:
                        e.wait_ge(S(f"ld_w{s}"), 16 * n_iter + 16)

                def merge_w(i, s):
                    load_w(e, s, merge_src[s], merge_col[s] + i * P)

                def out_w(i, s):
                    load_w(e, s, w_o[l], i * 512 + s * P)

                def up_w(half_):
                    return lambda i, s: load_w(e, s, a["mlp_w1"][l], half_ * (FF // 2) + i * 512 + s * P)

                def down_w(half_):
                    def load(i, s):
                        q = 2 * half_ + s % 2
                        load_w(e, s, a["mlp_w2"][l][q * D:(q + 1) * D, :], i * 256 + (s // 2) * P)
                    return load
                e.dma_start(hT[:, :, :], h_dram).then_inc(S("ld_h"), 16)
                ahead(0, merge_w, range(3))
                e.wait_ge(S("ld_h"), 16)
                meet_sp(e)
                meet_sp(e)
                stream(KT, merge_w, range(3))
                ahead(KT, out_w)
                meet_sp(e)
                stream(2, out_w, range(4))
                ahead(2, up_w(0))
                meet_sp(e)
                meet_sp(e)
                for half_ in range(2):
                    stream(4, up_w(half_), range(4))
                    ahead(4, down_w(half_))
                    meet_sp(e)
                    stream(4, down_w(half_), range(4))
                    if half_ == 0:
                        ahead(4, up_w(1))
                    else:
                        for s in range(4):
                            e.wait_ge(S(f"ld_w{s}"), 64)
                    meet_sp(e)
                meet_sp(e)
            for t in range(NT):
                e.wait_ge(S("v_tr"), 2 * t + 2)
                e.dma_start(out[0, t * P:(t + 1) * P, :], xtok[:, t, :]).then_inc(S("st_out"), 16)
            e.wait_ge(S("st_out"), 16 * NT)

        @block.tensor
        def _(p):
            p.wait_ge(S("v_set"), 6)
            p.wait_ge(S("ld_par"), 64)
            p.transpose(ps[:, 7, 0:24], prow[0:24, 0, :], ident[0:24, 0:24]).then_inc(S("p_tr"), 1)
            p.wait_ge(S("ld_x"), 16)
            for t in range(KT):
                if t >= 4:
                    p.wait_ge(S("v_tr"), t - 2)
                for q in range(NT):
                    mm = p.transpose(ps[:, t % 4, q * P:(q + 1) * P], xtok[:, q, t * P:(t + 1) * P], ident[:, :])
                mm.then_inc(S("p_tr"), 1)
            p.wait_ge(S("v_tr"), KT + 1)
            ln_pe(p)
            meet(p)
            with p.Fori(0, DEPTH) as l:
                p.wait_ge(S("ld_par"), 16 * 27)
                for b in range(3):
                    n = P if b < 2 else 48
                    mm = p.transpose(ps[:, b, 0:n], prow[0:n, b, :], ident[0:n, 0:n])
                mm.then_inc(S("p_tr"), 1)
                with p.Fori(0, 6) as i:
                    for s in range(2):
                        p.wait_ge(S(f"ev{s}"), KT * (i + 1))
                        for j in range(4):
                            mm = p.matmul(ps[:, 3, ds(8 * i + 4 * s + j, 1)], adas[:, s, j * P:(j + 1) * P],
                                          ones[:, 0:1], start=True, stop=True)
                        mm.then_inc(S(f"p_mm{s}"), 1)
                meet(p)
                p.wait_ge(S("v_u"), KT)
                for s, n in enumerate((P, P, P, 32)):
                    p.wait_ge(S(f"ld_w{s}"), 16)
                    dense(p, s, s, uT, n).then_inc(S("p_mm0"), 1)
                p.wait_ge(S("g_set"), 5)
                for j in range(2):
                    for k in range(KT):
                        mm = p.matmul(ps[0:64, 4 + j, :], wgp[:, k, j, :], uT[:, k, :], start=k == 0, stop=k == KT - 1)
                    mm.then_inc(S("p_mm1"), 1)
                p.wait_ge(S("v_gate"), 4)
                for t in range(NT):
                    mm = p.transpose(ps[:, 6, t * 64:(t + 1) * 64], aS[:, t * P:(t + 1) * P], ident[0:64, 0:64])
                mm.then_inc(S("p_tr"), 1)
                meet(p)
                with p.Fori(0, HA) as h:
                    for s in range(2):
                        p.wait_ge(S(f"ld_w{s}"), 16)
                        dense(p, s, s, uT).then_inc(S("p_mm0"), 1)
                    p.wait_ge(S("ld_v"), 16)
                    for t in range(NT):
                        for k in range(KT):
                            mm = p.matmul(ps[:, 2 + t // 2, (t % 2) * DV:(t % 2 + 1) * DV], uT[:, k, t * P:(t + 1) * P],
                                          wv[:, k, :], start=k == 0, stop=k == KT - 1)
                        mm.then_inc(S("p_v"), 1)
                    for s in range(2):
                        p.wait_ge(S(f"ld_w{2 + s}"), 16)
                        dense(p, 2 + s, 4 + s, uT).then_inc(S("p_mm1"), 1)
                    p.wait_ge(S("v_qk"), 2)
                    p.wait_ge(S("a_v"), 2)
                    for t in range(NT):
                        p.matmul(ps[:, t, :], qk[:, 1, t * P:(t + 1) * P], qk[:, 0, :], start=True, stop=True)\
                         .then_inc(S("p_s"), 1)
                    p.wait_ge(S("v_sel"), 2)
                    for d in range(2):
                        if d:
                            p.wait_ge(S("a_E"), 7)
                            p.wait_ge(S("v_dg"), NT)
                        p.matmul(ps[:, 6, :], selh[:, d, :], rows[:, 0, :], start=True, stop=True).then_inc(S("p_nm"), 1)
                        if d:
                            p.wait_ge(S("v_den"), 1)
                        p.matmul(ps[:, 7, :], selh[:, d, :], rows[:, 1, :], start=True, stop=True).then_inc(S("p_nx"), 1)
                        p.wait_ge(S("v_P"), NT * (d + 1))
                        p.wait_ge(S("a_emx"), d + 1)
                        order = range(NT) if d == 0 else range(NT - 1, -1, -1)
                        for n, t in enumerate(order):
                            lo_, hi_ = (t * P, T) if d == 0 else (0, (t + 1) * P)
                            mm = p.matmul(ps[:, 7, lo_:hi_], ones[:, 0:P], Pw[:, t, lo_:hi_], start=n == 0,
                                          stop=n == NT - 1)
                        mm.then_inc(S("p_den"), 1)
                        if d:
                            p.wait_ge(S("v_num"), 2)
                        else:
                            p.wait_ge(S("a_o"), 2)
                        for c in range(2):
                            for n, t in enumerate(order):
                                lo_, hi_ = (t * P, T) if d == 0 else (0, (t + 1) * P)
                                mm = p.matmul(ps[:, 4 + c, lo_:hi_], vtok[:, t, c * P:(c + 1) * P], Pw[:, t, lo_:hi_],
                                              start=n == 0, stop=n == NT - 1)
                            mm.then_inc(S("p_num"), 1)
                    p.wait_ge(S("v_h"), 2)
                    for c in range(2):
                        mm = p.matmul(ps[:, 6, :], ones[:, 0:P], hs[:, c, :], start=c == 0, stop=c == 1)
                    mm.then_inc(S("p_m2"), 1)
                    p.wait_ge(S("a_h2"), 2)
                    for c in range(2):
                        mm = p.matmul(ps[:, 7, :], ones[:, 0:P], hq[:, c, :], start=c == 0, stop=c == 1)
                    mm.then_inc(S("p_m2"), 1)
                    meet(p)


                def half(d, inv, has_chain, post, prep, hp):
                    def chain(lo_, hi_):
                        if not has_chain:
                            return
                        for n in range(lo_, hi_):
                            cd = 1 - d
                            i, ph = n // 3, n % 3
                            c = i if cd == 0 else NC - 1 - i
                            S_in = Sst[:, (i + 1) % 2, :]
                            if ph == 0:
                                if i >= 1:
                                    p.wait_ge(S("v_S"), i)
                                mm = p.matmul(ps[:, 6, 0:P], G3[cd][:, c, 0:P], Vt[cd][:, c, :], start=True, stop=i == 0)
                                if i:
                                    mm = p.matmul(ps[:, 6, 0:P], AQ[cd][:, c, 0:P], S_in, start=False, stop=True)
                                mm.then_inc(S("p_Z"), 1)
                            elif ph == 1:
                                p.wait_ge(S("a_Z"), i + 1)
                                if i:
                                    p.wait_ge(S("a_y"), i)
                                p.matmul(ps[:, 7, 0:P], XT[cd][:, c, :], Zs, start=True, stop=True).then_inc(S("p_U"), 1)
                            else:
                                p.wait_ge(S("v_U"), i + 1)
                                if i < NC - 1:
                                    p.matmul(ps[:, 6, P:2 * P], Ktk[cd][:, c, :], Vt[cd][:, c, :], start=True, stop=False)
                                    p.matmul(ps[:, 6, P:2 * P], Bt[cd][:, c, :], Us, start=False, stop=True)\
                                     .then_inc(S("p_S"), 1)
                                if i:
                                    p.matmul(ps[:, 7, P:2 * P], S_in, AQ[cd][:, c, C:C + P], start=True, stop=False)
                                p.matmul(ps[:, 7, P:2 * P], Us, G1[cd][:, c, C:C + P], start=i == 0, stop=False)
                                p.matmul(ps[:, 7, P:2 * P], Vt[cd][:, c, :], G3[cd][:, c, C:C + P], start=False, stop=True)\
                                 .then_inc(S("p_Y"), 1)

                    def invert(n):
                        k, ph, q = n // 4, n // 2 % 2, n % 2
                        cs = range(4 * q, 4 * q + 4)
                        if ph == 0:
                            if k == 0:
                                p.wait_ge(S("a_bt"), 6 - 2 * d)
                                p.wait_ge(S("g_in"), NC)
                                p.wait_ge(S("v_g"), NC)
                            elif k == 1:
                                p.wait_ge(S("v_R"), q + 1)
                            else:
                                p.wait_ge(S("a_X"), 2 * (k - 2) + q + 1)
                            for c in cs:
                                dst = ps[:, 2 * q, (c % 4) * P:(c % 4 + 1) * P]
                                if k == 0:
                                    mm = p.transpose(dst, G1[d][:, c, 0:P], ident[:, :])
                                else:
                                    mm = p.matmul(dst, G1[d][:, c, 0:P], Xm[:, c, :], start=True, stop=True)
                            mm.then_inc(S("p_T"), 1)
                        elif k >= 1:
                            p.wait_ge(S("v_R"), 2 * k + q + 1)
                            if k == 1:
                                p.wait_ge(S("g_Y"), 4 * q + 4)
                            else:
                                p.wait_ge(S("a_Y"), 2 * (k - 2) + q + 1)
                            for c in cs:
                                p_c = slice((c % 4) * P, (c % 4 + 1) * P)
                                if k < LEVELS - 1:
                                    p.matmul(ps[:, 2 * q, p_c], XT[d][:, c, :], Rm[:, c, :], start=True, stop=True)
                                mm = p.matmul(ps[:, 2 * q + 1, p_c], Rm[:, c, :], XT[d][:, c, :], start=True, stop=True)
                            mm.then_inc(S("p_XY"), 1)

                    def lora(j, bank, dd):
                        p.matmul(ps[:, bank, :], wup[:, j, dd, :], (tw, ad)[j][:, :], start=True, stop=True)\
                         .then_inc(S("p_lw"), 1)

                    def prepare(n):
                        if d == 0 and not prep:
                            return
                        if d == 0:
                            if n == 0:
                                lora(0, 4, 1)
                                lora(1, 5, 1)
                            return
                        if n == 0 and post:
                            p.matmul(ps[:, 5, :], bd[:, :], ysum, start=True, stop=True).then_inc(S("p_pm"), 1)
                        if n == 2 and post:
                            p.wait_ge(S("a_psq"), 1)
                            p.matmul(ps[:, 5, :], bd[:, :], ysq, start=True, stop=True).then_inc(S("p_pv"), 1)
                        if n == 4 and inv:
                            if post:
                                p.wait_ge(S("a_pstd"), 1)
                            p.matmul(ps[:, 5, :], gup, gd[:, :], start=True, stop=False)
                            p.matmul(ps[:, 5, :], gup2, gd2[:, :], start=False, stop=True).then_inc(S("p_gu"), 1)
                        if n == 6 and inv:
                            p.wait_ge(S("a_gu"), 1)
                            p.matmul(ps[:, 5, :], bd[:, :], rks, start=True, stop=True).then_inc(S("p_bon"), 1)
                        if not prep:
                            return
                        j, k = n // KT, n % KT
                        s = (1, 0, 2)[j]
                        if k == 0:
                            if not inv:
                                p.wait_ge(S(f"ld_w{s}"), 16)
                            if j == 1 and inv:
                                p.wait_ge(S("v_bon"), 1)
                            if j == 2:
                                p.wait_ge(S("a_lw"), 2)
                        mm = p.matmul(ps[:, 4 + j % 2, :], wt[:, s, k, :], uT[:, k, :], start=k == 0, stop=k == KT - 1)
                        if k == KT - 1:
                            mm.then_inc(S("p_mm0"), 1)
                        if n == 10:
                            p.wait_ge(S("v_s2"), 1)
                            p.wait_ge(S("a_kk"), 1)
                            p.matmul(ps[:, 4, :], bd[:, :], kr_sq, start=True, stop=True).then_inc(S("p_ss"), 1)
                        if n == 12:
                            p.wait_ge(S("v_ss"), 1)
                            p.wait_ge(S("ld_up"), 64)
                            lora(0, 4, 0)
                        if n == 14:
                            p.wait_ge(S("a_lw"), 1)
                            lora(1, 4, 0)

                    if inv:
                        for b in range(NC):
                            if b >= 6:
                                p.wait_ge(S("v_g"), b - 5)
                            for c in range(2 * (b // 2), 2 * (b // 2) + 2):
                                mm = p.matmul(ps[:, b % 6, (c % 2) * 192:(c % 2 + 1) * 192], (Bz if b % 2 == 0 else Kz)[:, c, :],
                                              AQ[d][:, c, :], start=True, stop=True)
                            mm.then_inc(S("p_g"), 1)
                            if b % 2:
                                chain(b // 2, b // 2 + 1)
                        for j, z in enumerate([Bz, Kz] + [Vz] * (d == 0)):
                            for q in range(2):
                                n = 2 * j + q
                                bank = (NC + n) % 6
                                p.wait_ge(S("v_g"), min(NC, 3 + n))
                                for c in range(4):
                                    mm = p.transpose(ps[:, bank, c * P:(c + 1) * P], z[:, 4 * q + c, :], ident[:, :])
                                mm.then_inc(S("p_bt"), 1)
                            if j < 2:
                                chain(4 + j, 5 + j)
                    else:
                        chain(0, CHG)
                    for n in range(24):
                        if inv:
                            invert(n)
                        if CHG + n < 24:
                            chain(CHG + n, CHG + n + 1)
                        prepare(n)
                rw_regions(p, half, meet)

                free(p, "p_mm")
                with p.Fori(0, KT) as n:
                    for j, (xh, xl) in enumerate(((uh, ul), (ah, al), (uh, ul), (bh, bl))):
                        p.wait_ge(S(f"ev{j}"), n + 1)
                        dense3(p, j, n, j, xh, xl)
                meet(p)
                free(p, "p_mm")
                p.wait_ge(S("g_xl"), KT)
                with p.Fori(0, 2) as n:
                    for j in range(4):
                        p.wait_ge(S(f"ev{j}"), n + 1)
                        dense3(p, j, n, j, mh, ml)
                meet(p)
                ln_pe(p)
                meet(p)
                for half_ in range(2):
                    free(p, "p_mm")
                    with p.Fori(0, 4) as n:
                        for j in range(4):
                            p.wait_ge(S(f"ev{j}"), n + 1)
                            dense3(p, j, n, j, uh, ul)
                    meet(p)
                    free(p, "p_mm")
                    with p.Fori(0, 4) as n:
                        for j in range(4):
                            k0, q = (j % 2) * KT, j // 2
                            if j % 2 == 0:
                                p.wait_ge(S(f"ev{q}"), n + 1)
                            dense3(p, j, n, q, fh[:, k0:k0 + KT, :], fl[:, k0:k0 + KT, :], j % 2 == 0, j % 2 == 1)
                    meet(p)
                ln_pe(p)
                meet(p)
            for t in range(NT):
                for q in range(2):
                    b = 2 * t + q
                    if b >= 4:
                        p.wait_ge(S("v_tr"), b - 3)
                    for c in range(4):
                        mm = p.transpose(ps[:, b % 4, c * P:(c + 1) * P], hT[:, 4 * q + c, t * P:(t + 1) * P], ident[:, :])
                    mm.then_inc(S("p_tr"), 1)

        @block.scalar
        def _(s):
            s.wait_ge(S("v_set"), 8)
            s.wait_ge(S("v_tr"), KT + 1)
            s.activation(cond[:, 0:8, :], lncol[:, 16:24, :], ACT.Sigmoid).then_inc(S("a_set"), 1)
            ln_act(s, lambda t: lncol[:, 8 + t, :])
            meet(s)
            with s.Fori(0, DEPTH) as l:
                meet(s)
                for j, (x, n) in enumerate(((tw, P), (ad, P), (gd, P), (gd2, 32))):
                    s.wait_ge(S("p_mm0"), j + 1)
                    s.activation(x[0:n, :], ps[0:n, j, :], ACT.Identity, scale=mix0[0:n, 24 + j, :]).then_inc(S("a_c0"), 1)
                for j in range(2):
                    s.wait_ge(S("p_mm1"), j + 1)
                    s.activation(gx[:, j, :], ps[0:64, 4 + j, :], ACT.Identity, bias=gbias[:, j:j + 1]).then_inc(S("a_gate"), 1)
                s.wait_ge(S("a_gate"), 2)
                s.activation(gx[:, 2, :], gx[:, 1, :], ACT.Abs).then_inc(S("a_gate"), 1)
                s.wait_ge(S("a_gate"), 3)
                s.activation(gx[:, 3, :], gx[:, 2, :], ACT.Exp, scale=-1.0).then_inc(S("a_gate"), 1)
                s.wait_ge(S("a_gate"), 4)
                s.activation(gx[:, 4, :], gx[:, 3, :], ACT.Ln, bias=1.0).then_inc(S("a_gate"), 1)
                s.wait_ge(S("v_s2"), 4)
                s.activation(tw[:, :], tw[:, :], ACT.Tanh).then_inc(S("a_act"), 1)
                s.activation(gd[:, :], gd[:, :], ACT.Sigmoid).then_inc(S("a_act"), 1)
                s.activation(gd2[0:32, :], gd2[0:32, :], ACT.Sigmoid).then_inc(S("a_act"), 1)
                s.wait_ge(S("p_tr"), 1)
                s.activation(acol.rearrange("p a b -> p (a b)"), ps[:, 6, 0:256], ACT.Copy).then_inc(S("a_act"), 1)
                s.wait_ge(S("a_act"), 4)
                meet(s)
                with s.Fori(0, HA) as h:
                    for j in range(2):
                        s.wait_ge(S("p_mm0"), j + 1)
                        s.activation(qk[:, j, :], ps[:, j, :], ACT.Identity, scale=pcol[:, 2 * 8 + 4 * j + h, :],
                                     bias=pcol[:, COL["conv_b"] + 4 * j + h, :]).then_inc(S("a_c0"), 1)
                    for j in range(2):
                        s.wait_ge(S("p_v"), 2 * j + 2)
                        s.activation(vtok[:, 2 * j:2 * j + 2, :].rearrange("p a b -> p (a b)"), ps[:, 2 + j, :], ACT.Copy)\
                         .then_inc(S("a_v"), 1)
                    for j in range(2):
                        s.wait_ge(S("v_conv"), 4 * j + 4)
                        s.activation(sg[:, j, :], qk[:, j, :], ACT.Sigmoid).then_inc(S("a_sig"), 1)
                    for j in range(2):
                        s.wait_ge(S("p_mm1"), j + 1)
                        s.activation(so[:, j, :], ps[:, 4 + j, :], ACT.Sigmoid).then_inc(S("a_o"), 1)
                    for d in range(2):
                        s.wait_ge(S("p_nx"), d + 1)
                        if d:
                            s.wait_ge(S("v_den"), 1)
                        s.activation(emx, ps[:, 7, :], ACT.Exp).then_inc(S("a_emx"), 1)
                        s.wait_ge(S("p_nm"), d + 1)
                        if d:
                            s.wait_ge(S("v_P"), NT)
                        s.wait_ge(S("v_dg"), NT * d + NT)
                        for t in range(NT):
                            bias = acol[:, t, ds(32 * d + h, 1)]
                            s.activation(Ew[:, t, t * P:(t + 1) * P], dg[:, t, :], ACT.Exp, bias=bias).then_inc(S("a_E"), 1)
                            lo_, hi_ = ((t + 1) * P, T) if d == 0 else (0, t * P)
                            if hi_ > lo_:
                                s.activation(Ew[:, t, lo_:hi_], ps[:, 6, lo_:hi_], ACT.Exp, bias=bias).then_inc(S("a_E"), 1)
                    for c in range(2):
                        s.wait_ge(S("v_h"), 3 + c)
                        s.activation(hq[:, c, :], hs[:, c, :], ACT.Square).then_inc(S("a_h2"), 1)
                    s.wait_ge(S("p_m2"), 2)
                    s.activation(hstd, ps[:, 7, :], ACT.Sqrt, bias=eps[:, 0:1], scale=1.0 / DV).then_inc(S("a_std"), 1)
                    meet(s)

                def half(d, inv, has_chain, post, prep, hp):
                    def chain(lo_, hi_):
                        if not has_chain:
                            return
                        for n in range(lo_, hi_):
                            cd = 1 - d
                            i, ph = n // 3, n % 3
                            c = i if cd == 0 else NC - 1 - i
                            if ph == 0:
                                s.wait_ge(S("p_Z"), i + 1)
                                if i:
                                    s.wait_ge(S("p_U"), i)
                                s.activation(Zs, ps[:, 6, 0:P], ACT.Copy).then_inc(S("a_Z"), 1)
                            elif ph == 2 and cd == 0:
                                s.wait_ge(S("p_Y"), i + 1)
                                s.activation(yf[:, c * C:(c + 1) * C], ps[:, 7, P + C:2 * P], ACT.Copy).then_inc(S("a_y"), 1)

                    def invert(n):
                        k, ph, q = n // 4, n // 2 % 2, n % 2
                        if ph == 1 and k >= 1:
                            s.wait_ge(S("p_XY"), 2 * (k - 1) + q + 1)
                            if k < LEVELS - 1:
                                s.activation(Xm[:, 4 * q:4 * q + 4, :].rearrange("p a b -> p (a b)"), ps[:, 2 * q, :],
                                             ACT.Copy).then_inc(S("a_X"), 1)
                            s.activation(XT[d][:, 4 * q:4 * q + 4, :].rearrange("p a b -> p (a b)"), ps[:, 2 * q + 1, :],
                                         ACT.Copy).then_inc(S("a_Y"), 1)

                    def evac(j, x, w, bank):
                        s.wait_ge(S("p_mm0"), j + 1)
                        s.activation(x, ps[:, bank, :], ACT.Identity, scale=mix0[:, 8 * w + hp + 1, :]).then_inc(S("a_c0"), 1)

                    def decay(bank, dd, pair):
                        s.wait_ge(S("p_lw"), 1)
                        s.activation(sw, ps[:, bank, :], ACT.Sigmoid, bias=pcol[:, COL["w0"] + 8 * dd + pair, :])\
                         .then_inc(S("a_lw"), 1)

                    def rate(bank, dd, pair):
                        s.wait_ge(S("p_lw"), 2)
                        s.activation(aa, ps[:, bank, :], ACT.Sigmoid, bias=pcol[:, COL["a0"] + 8 * dd + pair, :])\
                         .then_inc(S("a_lw"), 1)

                    def exps():
                        s.wait_ge(S("v_L"), 1)
                        s.activation(Ep, Lc, ACT.Exp, scale=-DECAY).then_inc(S("a_exp"), 1)
                        s.activation(En, Lc, ACT.Exp, scale=DECAY).then_inc(S("a_exp"), 1)

                    def exps_x():
                        s.wait_ge(S("g_Lx"), 1)
                        s.activation(Ex, Lx, ACT.Exp, scale=-DECAY).then_inc(S("a_exp"), 1)

                    def prepare(n):
                        if d == 0 and not prep:
                            return
                        if d == 0:
                            if n == 1:
                                decay(4, 1, hp)
                                rate(5, 1, hp)
                            if n == 3:
                                exps()
                            if n == 6:
                                exps_x()
                            return
                        if n == 1 and post:
                            s.wait_ge(S("v_pc"), 1)
                            s.activation(ysq, ysum, ACT.Square).then_inc(S("a_psq"), 1)
                        if n == 3 and post:
                            s.wait_ge(S("p_pv"), 1)
                            s.activation(ysq, ps[:, 5, :], ACT.Sqrt, bias=eps[:, 1:2], scale=1.0 / C).then_inc(S("a_pstd"), 1)
                        if n == 5 and inv:
                            if post:
                                s.wait_ge(S("v_py"), 3)
                            s.wait_ge(S("p_gu"), 1)
                            s.activation(gbuf, ps[:, 5, :], ACT.Copy).then_inc(S("a_gu"), 1)
                        if not prep:
                            return
                        if n == 8:
                            evac(0, kr, 1, 4)
                        if n == 9:
                            s.wait_ge(S("v_s2"), 1)
                            s.activation(kr_sq, kr, ACT.Square, scale=pcol[:, COL["k_k"] + hp + 1, :]).then_inc(S("a_kk"), 1)
                        if n == 12:
                            s.wait_ge(S("v_ss"), 1)
                            s.activation(Ex, Ex, ACT.Sqrt).then_inc(S("a_nrm"), 1)
                        if n == 13:
                            decay(4, 0, hp + 1)
                        if n == 15:
                            rate(4, 0, hp + 1)
                        if n == 16:
                            evac(1, rr, 0, 5)
                        if n == 17:
                            exps()
                        if n == 18:
                            s.wait_ge(S("v_kk"), 1)
                            exps_x()
                        if n == 23:
                            evac(2, vr, 2, 4)

                    if inv:
                        chain(0, 4)
                        for j, z in enumerate([Bt[d], Ktk[d]] + [Vt[0]] * (d == 0)):
                            for q in range(2):
                                n = 2 * j + q
                                s.wait_ge(S("p_bt"), n + 1)
                                s.activation(z[:, 4 * q:4 * q + 4, :].rearrange("p a b -> p (a b)"), ps[:, (NC + n) % 6, :],
                                             ACT.Copy).then_inc(S("a_bt"), 1)
                            if j < 2:
                                chain(4 + j, 5 + j)
                    else:
                        chain(0, CHG)
                    for n in range(24):
                        if inv:
                            invert(n)
                        if CHG + n < 24:
                            chain(CHG + n, CHG + n + 1)
                        prepare(n)
                    if inv:
                        s.wait_ge(S("a_Y"), 2 * (LEVELS - 1))
                    if prep:
                        s.wait_ge(S("a_exp"), 3)
                    if has_chain:
                        s.wait_ge(S("a_Z"), NC)
                        if d == 1:
                            s.wait_ge(S("a_y"), NC)
                    if d == 1 and inv:
                        s.wait_ge(S("a_gu"), 1)
                rw_regions(s, half, meet)
                for j in range(2):
                    s.sem_inc(S(f"ev{2 * j}"), 1)
                with s.Fori(0, KT) as n:
                    for j in range(2):
                        s.wait_ge(S(f"p_mm{2 * j}"), n + 2)
                        s.wait_ge(S("v_out"), n + 1)
                        s.activation(sga[:, j, :], ps[:, 2 * j, :], ACT.Sigmoid).then_inc(S(f"ev{2 * j}"), 1)
                meet(s)
                meet(s)
                ln_act(s, lambda t: pcol[:, COL["ln1_b"] + t, :])
                meet(s)
                for half_ in range(2):
                    free(s, "ev")
                    s.sem_inc(S("v_sq"), 4)
                    with s.Fori(0, 4) as n:
                        for j in range(4):
                            s.wait_ge(S(f"p_mm{j}"), n + 2)
                            s.wait_ge(S("v_sq"), 4 * n + j + 1)
                            s.activation(fr[:, j, :], ps[:, j, :], ACT.Relu,
                                         bias=pcol[:, COL["b1"] + FH * half_ + 4 * n + j, :]).then_inc(S(f"ev{j}"), 1)
                    meet(s)
                    meet(s)
                ln_act(s, lambda t: pcol[:, COL["ln2_b"] + t, :])
                meet(s)

        @block.gpsimd
        def _(g):
            meet(g)
            with g.Fori(0, DEPTH) as l:
                meet(g)
                g.memset(wgp, 0.0).then_inc(S("g_set"), 1)
                g.wait_ge(S("g_set"), 1)
                g.wait_ge(S("ld_v"), 16)
                for d in range(2):
                    for j in range(2):
                        g.tensor_copy(wgp[:, :, j, 32 * d:32 * d + 4], wg16[:, :, 8 * d + 4 * j:8 * d + 4 * j + 4])\
                         .then_inc(S("g_set"), 1)
                meet(g)
                with g.Fori(0, HA) as h:
                    meet(g)

                def half(d, inv, has_chain, post, prep, hp):
                    if not inv and prep:
                        g.memset(wup, 0.0).then_inc(S("g_dend"), 1)
                        g.memset(gup2, 0.0).then_inc(S("g_dend"), 1)
                        g.memset(Bz, 0.0).then_inc(S("g_dend"), 1)
                        g.memset(Kz, 0.0).then_inc(S("g_dend"), 1)
                        g.memset(AQ[0], 0.0).then_inc(S("g_dend"), 1)
                        g.memset(Vz, 0.0).then_inc(S("g_dend"), 1)
                        g.memset(AQ[1], 0.0).then_inc(S("g_dend"), 1)
                    if not inv and not prep:
                        if d == 0:
                            for t in range(KT):
                                x_lo(g, uT, uh, ul, t, t)
                            for t in range(KT):
                                x_lo(g, yA, ah, al, t, KT + t)
                        else:
                            for t in range(KT):
                                x_lo(g, yB, bh, bl, t, t)
                        g.wait_ge(S("g_xl"), KT * (2 - d))
                        return
                    if inv:
                        if d == 1:
                            g.tensor_copy(Vt[1], Vt[0]).then_inc(S("g_vb"), 1)
                        for c in range(4):
                            g.wait_ge(S("v_g"), 2 * c + 1)
                            for c2 in range(2 * c, 2 * c + 2):
                                g.tensor_tensor(G1[d][:, c2, 0:P], G1[d][:, c2, 0:P], ident[:, :], ALU.add)\
                                 .then_inc(S("g_in"), 1)
                        if d == 0:
                            g.wait_ge(S("p_bt"), 6)
                        for q in range(2):
                            g.wait_ge(S("g_in"), 4 * q + 4)
                            for c in range(4 * q, 4 * q + 4):
                                g.tensor_tensor(XT[d][:, c, :], G1[d][:, c, 0:P], maskL[1 - d][0], ALU.mult)\
                                 .then_inc(S("g_Y"), 1)
                    if prep:
                        g.wait_ge(S("v_L"), 1)
                        g.wait_ge(S("a_lw"), 1)
                        g.tensor_tensor(Lx, Lc, sw, ALU.subtract).then_inc(S("g_Lx"), 1)
                        g.wait_ge(S("g_Lx"), 1)
                    if inv:
                        g.wait_ge(S("g_Y"), NC)
                    if not inv:
                        g.wait_ge(S("g_dend"), 7)
                rw_regions(g, half, meet)
                def weights(n_iter):
                    with g.Fori(0, n_iter) as n:
                        for j in range(4):
                            w_lo(g, j, n)
                weights(KT)
                meet(g)
                for t in range(KT):
                    x_lo(g, merged, mh, ml, t, t)
                weights(2)
                meet(g)
                for t in range(KT):
                    x_lo(g, uT, uh, ul, t, t)
                g.wait_ge(S("g_xl"), KT)
                meet(g)
                for half_ in range(2):
                    for j in range(4):
                        w_lo(g, j, 0)

                    def units(n, last):
                        for j in range(4):
                            g.wait_ge(S("v_fh"), 4 * n + j + 1)
                            g.tensor_tensor(fl[:, ds(4 * n + j, 1), :], fsq[:, j:j + 1, :], fh[:, ds(4 * n + j, 1), :].bitcast(F32),
                                            ALU.subtract).then_inc(S("g_fl"), 1)
                            if not last:
                                w_lo(g, j, n + 1)
                    with g.Fori(0, 3) as n:
                        units(n, False)
                    units(3, True)
                    g.wait_ge(S("g_fl"), FH + 4)
                    meet(g)
                    weights(4)
                    meet(g)
                meet(g)

        @block.vector
        def _(v):
            v.memset(ones[:, :], 1.0).then_inc(S("v_set"), 1)
            v.memset(gbias[:, :], 0.0).then_inc(S("v_set"), 1)
            v.memset(gd2[:, :], 0.0).then_inc(S("v_set"), 1)
            v.memset(eps[:, 0:1], 1e-5).then_inc(S("v_set"), 1)
            v.wait_ge(S("ld_par"), 64)
            v.tensor_copy(ident[:, :], craw[:, CI:CI + P]).then_inc(S("v_set"), 1)
            v.tensor_copy(bd[:, :], craw[:, CBD:CBD + P]).then_inc(S("v_set"), 1)
            v.tensor_copy(mask[:, :], craw[:, CG:NCONST]).then_inc(S("v_set"), 1)
            v.memset(eps[:, 1:2], 64e-5).then_inc(S("v_set"), 1)
            v.wait_ge(S("p_tr"), 1)
            v.tensor_copy(lncol[:, :, 0], ps[:, 7, 0:24]).then_inc(S("v_tr"), 1)
            for t in range(KT):
                v.wait_ge(S("p_tr"), t + 2)
                v.tensor_copy(hT[:, t, :], ps[:, t % 4, :]).then_inc(S("v_tr"), 1)
            v.wait_ge(S("v_tr"), KT + 1)
            ln_dve(v, lambda t: lncol[:, t, :])
            v.wait_ge(S("a_set"), 1)
            v.tensor_tensor(cond[:, 8:16, :], cond[:, 0:8, :], lncol[:, 16:24, :], ALU.mult).then_inc(S("v_set"), 1)
            v.wait_ge(S("v_set"), 9)
            meet(v)
            with v.Fori(0, DEPTH) as l:
                v.memset(prow[96:128, 1, :], 0.0).then_inc(S("v_set"), 1)
                v.wait_ge(S("p_tr"), 1)
                for b in range(3):
                    n = P if b < 2 else 48
                    v.tensor_copy(pcol[:, b * P:b * P + n, 0], ps[:, b, 0:n]).then_inc(S("v_tr"), 1)
                v.wait_ge(S("v_tr"), 3)
                cmu = COL["mup"]
                v.tensor_tensor(mix0[:, 0:24, 0], pcol[:, cmu:cmu + 24, 0], pcol[:, cmu + 24:cmu + 48, 0], ALU.add).then_inc(S("v_gate"), 1)
                lo_ = COL["mup_lo"]
                v.tensor_tensor(mix0[:, 24:27, 0], pcol[:, lo_:lo_ + 3, 0], pcol[:, lo_ + 3:lo_ + 6, 0], ALU.add).then_inc(S("v_gate"), 1)
                v.tensor_tensor(mix0[:, 27:28, 0], pcol[:, lo_ + 6:lo_ + 7, 0], pcol[:, lo_ + 7:lo_ + 8, 0], ALU.add).then_inc(S("v_gate"), 1)
                v.tensor_scalar(ka1[:, :, 0], pcol[:, COL["k_a"]:COL["k_a"] + 8, 0], -1.0, 1.0, ALU.mult, ALU.add).then_inc(S("v_gate"), 1)
                v.wait_ge(S("v_gate"), 3)
                v.tensor_scalar(mix0[:, :, 0], mix0[:, :, 0], -1.0, 1.0, ALU.mult, ALU.add).then_inc(S("v_gate"), 1)
                for s in range(2):
                    v.sem_inc(S(f"p_mm{s}"), 1)
                with v.Fori(0, 6) as i:
                    for s in range(2):
                        v.wait_ge(S(f"ld_w{s}"), 16 * i + 16)
                        v.wait_ge(S(f"p_mm{s}"), i + 1)
                        for k in range(KT):
                            if k == 0:
                                v.tensor_scalar(adas[:, s, :], adaw[:, s, k, :], cond[:, 8 + k, :], None, ALU.mult).then_inc(S(f"ev{s}"), 1)
                            else:
                                v.wait_ge(S(f"ev{s}"), KT * i + k)
                                v.scalar_tensor_tensor(adas[:, s, :], adaw[:, s, k, :], cond[:, 8 + k, :], adas[:, s, :],
                                                       ALU.mult, ALU.add).then_inc(S(f"ev{s}"), 1)
                v.wait_ge(S("p_mm0"), 7)
                v.wait_ge(S("p_mm1"), 7)
                v.tensor_tensor(mod[:, :, 0], ps[:, 3, 0:48], pcol[:, 256:304, 0], ALU.add).then_inc(S("v_gate"), 1)
                v.wait_ge(S("v_gate"), 6)
                for o in (8, 16, 32, 40):
                    v.tensor_scalar(mod[:, o:o + 8, 0], mod[:, o:o + 8, 0], 1.0, None, ALU.add).then_inc(S("v_gate"), 1)
                v.wait_ge(S("v_gate"), 10)
                v.tensor_tensor(b2g[:, :], pcol[:, COL["b2"]:COL["b2"] + 8, 0], mod[:, 40:48, 0], ALU.mult).then_inc(S("v_gate"), 1)
                v.wait_ge(S("v_gate"), 11)
                meet(v)
                v.memset(zero, 0.0).then_inc(S("v_set"), 1)
                v.memset(one, 1.0).then_inc(S("v_set"), 1)
                v.memset(rows[64:P, :, :], 0.0).then_inc(S("v_out"), 1)
                modulate(v, 0)
                for j, (x, n) in enumerate(((tw, P), (ad, P), (gd, P), (gd2, 32))):
                    mp = pcol[0:n, COL["mup_lo"] + j, :] if j < 3 else pcol[0:32, COL["mup_g2"], :]
                    mn = pcol[0:n, COL["mun_lo"] + j, :] if j < 3 else pcol[0:32, COL["mun_g2"], :]
                    shift(v, x[0:n, :], ps[0:n, j, :], mp, mn, j)
                v.wait_ge(S("a_gate"), 5)
                v.scalar_tensor_tensor(gx[:, 5, :], gx[:, 1, :], 0.0, gx[:, 4, :], ALU.min, ALU.subtract).then_inc(S("v_gate"), 1)
                v.wait_ge(S("v_gate"), 1)
                v.wait_ge(S("v_set"), 2)
                v.tensor_tensor_scan(Gs[0:32, :], one[0:32, :], gx[0:32, 5, :], 0.0, ALU.mult, ALU.add).then_inc(S("v_gate"), 1)
                v.tensor_tensor_scan(Gs[32:64, ::-1], one[32:64, :], gx[32:64, 5, ::-1], 0.0, ALU.mult, ALU.add).then_inc(S("v_gate"), 1)
                v.wait_ge(S("v_gate"), 3)
                v.tensor_tensor(aS, gx[:, 0, :], Gs, ALU.subtract).then_inc(S("v_gate"), 1)
                v.wait_ge(S("v_gate"), 4)
                v.tensor_tensor_scan(gx[0:32, 2, :], zero[0:32, :], aS[0:32, :], -3e38, ALU.add, ALU.max).then_inc(S("v_gate"), 1)
                v.tensor_tensor_scan(gx[32:64, 2, ::-1], zero[32:64, :], aS[32:64, ::-1], -3e38, ALU.add, ALU.max).then_inc(S("v_gate"), 1)
                v.wait_ge(S("v_gate"), 6)
                v.tensor_scalar(rows[0:64, 0, :], gx[:, 2, :], -1.0, None, ALU.mult).then_inc(S("v_gate"), 1)
                v.wait_ge(S("v_gate"), 7)
                v.tensor_tensor(rows[0:64, 1, :], rows[0:64, 0, :], Gs, ALU.subtract).then_inc(S("v_gate"), 1)
                v.wait_ge(S("v_gate"), 8)
                v.wait_ge(S("v_out"), 1)
                meet(v)
                with v.Fori(0, HA) as h:
                    for d in range(2):
                        v.tensor_copy(selh[:, d, :], ident[:, ds(32 * d + h, 1)].broadcast_to([P, P])).then_inc(S("v_sel"), 1)
                    for j in range(2):
                        v.wait_ge(S("a_c0"), j + 1)
                        for n, tap in enumerate((0, 1, 3, 4)):
                            o = tap - 2
                            dst = slice(max(0, -o), T - max(0, o))
                            src = slice(max(0, o), T - max(0, -o))
                            if n:
                                v.wait_ge(S("v_conv"), 4 * j + n)
                            v.scalar_tensor_tensor(qk[:, j, dst], ps[:, j, src], pcol[:, 8 * tap + 4 * j + h, :],
                                                   qk[:, j, dst], ALU.mult, ALU.add).then_inc(S("v_conv"), 1)
                    for j in range(2):
                        v.wait_ge(S("a_sig"), j + 1)
                        v.scalar_tensor_tensor(qk[:, j, :], qk[:, j, :], 1.0 if j == 0 else DK ** -0.5, sg[:, j, :],
                                               ALU.mult, ALU.mult).then_inc(S("v_qk"), 1)
                    nE = 0
                    for d in range(2):
                        v.wait_ge(S("p_nm"), d + 1)
                        if d:
                            v.wait_ge(S("a_E"), 7)
                        for t in range(NT):
                            v.tensor_tensor(dg[:, t, :], ps[:, 6, t * P:(t + 1) * P], maskC[d], ALU.add).then_inc(S("v_dg"), 1)
                        if d:
                            v.wait_ge(S("p_num"), 2)
                        for t in range(NT):
                            lo_, hi_ = (t * P, T) if d == 0 else (0, (t + 1) * P)
                            nE += 2 if hi_ - lo_ > P else 1
                            v.wait_ge(S("a_E"), nE)
                            v.wait_ge(S("p_s"), t + 1)
                            v.tensor_tensor(Pw[:, t, lo_:hi_], ps[:, t, lo_:hi_], Ew[:, t, lo_:hi_], ALU.mult).then_inc(S("v_P"), 1)
                        v.wait_ge(S("p_den"), d + 1)
                        v.wait_ge(S("a_emx"), d + 1)
                        v.tensor_scalar(rf, ps[:, 7, :], -1.0, None, ALU.mult).then_inc(S("v_gate"), 1)
                        v.wait_ge(S("v_gate"), 3 * d + 1)
                        v.tensor_tensor(rf, ps[:, 7, :], rf, ALU.max).then_inc(S("v_gate"), 1)
                        v.wait_ge(S("v_gate"), 3 * d + 2)
                        v.tensor_tensor(rf, rf, emx, ALU.max).then_inc(S("v_den"), 1)
                        v.wait_ge(S("v_den"), d + 1)
                        v.reciprocal(rf, rf).then_inc(S("v_gate"), 1)
                        v.wait_ge(S("v_gate"), 3 * d + 3)
                        for c in range(2):
                            v.wait_ge(S("p_num"), 2 * d + c + 1)
                            v.tensor_tensor((hs if d == 0 else ht)[:, c, :], ps[:, 4 + c, :], rf, ALU.mult).then_inc(S("v_num"), 1)
                        v.wait_ge(S("v_num"), 2 * d + 2)
                    for c in range(2):
                        v.tensor_tensor(hs[:, c, :], hs[:, c, :], ht[:, c, :], ALU.add).then_inc(S("v_h"), 1)
                    v.wait_ge(S("p_m2"), 1)
                    v.wait_ge(S("v_h"), 2)
                    for c in range(2):
                        v.scalar_tensor_tensor(hs[:, c, :], ps[:, 6, :], -1.0 / DV, hs[:, c, :], ALU.mult, ALU.add).then_inc(S("v_h"), 1)
                    v.wait_ge(S("a_std"), 1)
                    v.reciprocal(rf, hstd).then_inc(S("v_rstd"), 1)
                    v.wait_ge(S("v_rstd"), 1)
                    v.wait_ge(S("v_h"), 4)
                    v.wait_ge(S("a_h2"), 2)
                    for c in range(2):
                        v.scalar_tensor_tensor(hs[:, c, :], hs[:, c, :], pcol[:, COL["norm_g"] + 2 * h + c, :], rf, ALU.mult,
                                               ALU.mult).then_inc(S("v_nrm"), 1)
                    v.wait_ge(S("v_nrm"), 2)
                    v.wait_ge(S("a_o"), 2)
                    for c in range(2):
                        v.tensor_tensor(yA[:, 2 * h + c, :], hs[:, c, :], so[:, c, :], ALU.mult).then_inc(S("v_out"), 1)
                    v.wait_ge(S("v_out"), 2)
                    meet(v)

                def half(d, inv, has_chain, post, prep, hp):
                    dd = 1 - d
                    pair = hp if d == 0 else hp + 1
                    last = HP - 1 if not inv else hp - 1
                    kmd = km if d == 0 else kmf

                    def ch(x):
                        return x.rearrange("p (c t) -> p c t", c=NC)

                    def bdiag(dst, x, y):
                        for z in range(2):
                            h0, h1 = 64 * z, 64 * z + 64
                            v.tensor_tensor(dst[h0:h1, :, h0:h1], ch(x)[h0:h1], ch(y)[h0:h1], ALU.mult).then_inc(S("v_bd"), 1)

                    def chain(lo_, hi_):
                        if not has_chain:
                            return
                        for n in range(lo_, hi_):
                            cd = 1 - d
                            i, ph = n // 3, n % 3
                            c = i if cd == 0 else NC - 1 - i
                            S_in, S_out = Sst[:, (i + 1) % 2, :], Sst[:, i % 2, :]
                            if ph == 1:
                                if i and i < NC - 1:
                                    v.tensor_scalar(Sd, S_in, dend[cd][:, c:c + 1], None, ALU.mult).then_inc(S("v_Sd"), 1)
                                v.wait_ge(S("p_U"), i + 1)
                                if i:
                                    v.wait_ge(S("p_Y"), i)
                                v.tensor_copy(Us, ps[:, 7, 0:P]).then_inc(S("v_U"), 1)
                            elif ph == 2:
                                if i < NC - 1:
                                    v.wait_ge(S("p_S"), i + 1)
                                    if i:
                                        v.wait_ge(S("v_Sd"), i)
                                        v.scalar_tensor_tensor(S_out, ps[:, 6, P:2 * P], dend[cd][:, c:c + 1], Sd, ALU.mult, ALU.add)\
                                         .then_inc(S("v_S"), 1)
                                    else:
                                        v.tensor_scalar(S_out, ps[:, 6, P:2 * P], dend[cd][:, c:c + 1], None, ALU.mult).then_inc(S("v_S"), 1)
                                    v.wait_ge(S("v_S"), i + 1)
                                if cd == 1:
                                    v.wait_ge(S("p_Y"), i + 1)
                                    v.tensor_tensor(ysum[:, c * C:(c + 1) * C], yf[:, c * C:(c + 1) * C], ps[:, 7, P + C:2 * P], ALU.add)\
                                     .then_inc(S("a_y"), 1)

                    def invert(n):
                        k, ph, q = n // 4, n // 2 % 2, n % 2
                        if ph == 0:
                            v.wait_ge(S("p_T"), 2 * k + q + 1)
                            if k >= 2:
                                v.wait_ge(S("p_XY"), 2 * (k - 2) + q + 1)
                            R = Xm if k == 0 else Rm
                            v.tensor_tensor(R[:, 4 * q:4 * q + 4, :], ps[:, 2 * q, :].rearrange("p (c x) -> p c x", c=4),
                                            maskL[d][k].rearrange("p (o x) -> p o x", o=1).broadcast_to([P, 4, P]), ALU.mult)\
                             .then_inc(S("v_R"), 1)

                    def token_shift(j, x, b, bank):
                        shift(v, x, ps[:, bank, :], pcol[:, COL["mup"] + 8 * b + pair, :], pcol[:, COL["mun"] + 8 * b + pair, :], j)

                    def scan():
                        v.wait_ge(S("a_lw"), 1)
                        if dd == 0:
                            v.tensor_tensor_scan(Lc, maskR[0], sw, 0.0, ALU.mult, ALU.add).then_inc(S("v_L"), 1)
                        else:
                            v.tensor_tensor_scan(Lc[:, ::-1], maskR[1][:, ::-1], sw[:, ::-1], 0.0, ALU.mult, ALU.add).then_inc(S("v_L"), 1)

                    def k_scale():
                        v.wait_ge(S("a_lw"), 2)
                        if dd == 1:
                            v.wait_ge(S("g_Lx"), 1)
                        v.tensor_scalar(kmd, aa, pcol[:, COL["k_a"] + pair, :], ka1[:, pair, :],
                                        ALU.mult, ALU.add).then_inc(S("v_km"), 1)

                    def k_mul():
                        v.wait_ge(S("v_km"), 1)
                        v.tensor_tensor(kmd, kmd, kr, ALU.mult).then_inc(S("v_km"), 1)

                    def rate():
                        v.scalar_tensor_tensor(aa, kk, -1.0, aa, ALU.mult, ALU.mult).then_inc(S("v_km"), 1)

                    def fill_b():
                        if not inv:
                            v.wait_ge(S("g_dend"), 7)
                        else:
                            v.wait_ge(S("p_bt"), 6 - 2 * d)
                        v.wait_ge(S("a_exp"), 2)
                        v.wait_ge(S("v_km"), 3)
                        bdiag(Bz, aa, En)

                    def fill_a():
                        if has_chain:
                            v.wait_ge(S("p_Y"), NC)
                        v.wait_ge(S("a_exp"), 3)
                        v.tensor_copy(dend[dd], Ep[:, (C - 1 if dd == 0 else 0):T:C]).then_inc(S("v_dend"), 1)
                        bdiag(AQ[dd], kk, Ex)

                    def fill_q():
                        v.tensor_tensor(AQ[dd][:, :, P:P + C], ch(rr), ch(Ep), ALU.mult).then_inc(S("v_bd"), 1)

                    def finish(n):
                        if n == 1:
                            v.wait_ge(S("p_pm"), 1)
                            v.scalar_tensor_tensor(ysum, ps[:, 5, :], -1.0 / C, ysum, ALU.mult, ALU.add).then_inc(S("v_pc"), 1)
                        if n == 3:
                            v.wait_ge(S("a_pstd"), 1)
                            v.reciprocal(ysq, ysq).then_inc(S("v_pr"), 1)
                            v.wait_ge(S("v_pr"), 1)
                            v.scalar_tensor_tensor(ysum, ysum, pcol[:, COL["gn_g"] + last, :], ysq, ALU.mult, ALU.mult).then_inc(S("v_py"), 1)
                        if n == 4:
                            v.wait_ge(S("v_py"), 1)
                            v.scalar_tensor_tensor(ysum, ysum, pcol[:, COL["gn_b"] + last, :], bonus, ALU.add, ALU.add).then_inc(S("v_py"), 1)
                            v.wait_ge(S("v_py"), 2)
                            v.tensor_tensor(yB[:, last, :], ysum, gbuf, ALU.mult).then_inc(S("v_py"), 1)

                    def prepare(n):
                        if d == 0 and not prep:
                            return
                        if d == 0:
                            if n == 2:
                                scan()
                            if n == 5:
                                k_scale()
                            if n == 6:
                                k_mul()
                            if n == 7:
                                v.wait_ge(S("v_km"), 2)
                                rate()
                            if n == 8:
                                v.tensor_tensor(rks, km, kmf, ALU.add).then_inc(S("v_rk"), 1)
                            if n == 9:
                                v.wait_ge(S("v_rk"), 1)
                                v.scalar_tensor_tensor(rks, rr, pcol[:, COL["r_k"] + pair, :], rks, ALU.mult, ALU.mult).then_inc(S("v_rk"), 1)
                            if n == 10:
                                fill_b()
                            if n == 12:
                                bdiag(Kz, kmd, En)
                            if n == 19:
                                fill_a()
                            if n == 20:
                                fill_q()
                            return
                        if post:
                            finish(n)
                        if n == 7 and inv:
                            v.wait_ge(S("p_bon"), 1)
                            v.tensor_tensor(bonus, ps[:, 5, :], vr, ALU.mult).then_inc(S("v_bon"), 1)
                        if not prep:
                            return
                        if n == 8:
                            token_shift(0, kr, 1, 4)
                        if n == 11:
                            v.wait_ge(S("p_ss"), 1)
                            v.tensor_scalar(Ex, ps[:, 4, :], 1e-24, None, ALU.max).then_inc(S("v_ss"), 1)
                        if n == 13:
                            v.wait_ge(S("a_nrm"), 1)
                            v.reciprocal(Ex, Ex).then_inc(S("v_ss"), 1)
                        if n == 14:
                            v.wait_ge(S("v_ss"), 2)
                            v.scalar_tensor_tensor(kk, kr, pcol[:, COL["k_k"] + pair, :], Ex, ALU.mult, ALU.mult).then_inc(S("v_kk"), 1)
                            scan()
                        if n == 16:
                            k_scale()
                            token_shift(1, rr, 0, 5)
                        if n == 17:
                            k_mul()
                            v.wait_ge(S("v_kk"), 1)
                            v.wait_ge(S("v_km"), 2)
                            rate()
                        if n == 18:
                            fill_b()
                        if n == 19:
                            bdiag(Kz, kmd, En)
                        if n == 20:
                            fill_a()
                        if n == 21:
                            v.wait_ge(S("v_s2"), 2)
                            fill_q()
                        if n == 23:
                            token_shift(2, vr, 2, 4)
                            v.wait_ge(S("v_s2"), 3)
                            for z in range(2):
                                v.tensor_copy(Vz[64 * z:64 * z + 64, :, 64 * z:64 * z + 64], ch(vr)[64 * z:64 * z + 64])\
                                 .then_inc(S("v_bd"), 1)

                    if not inv and not prep:
                        if d == 0:
                            for n in range(24):
                                chain(n, n + 1)
                                if n < 16:
                                    x_hi(v, uT if n < KT else yA, uh if n < KT else ah, n % KT)
                            v.wait_ge(S("v_xh"), 2 * KT)
                            v.wait_ge(S("a_y"), NC)
                        else:
                            for t in range(KT - 1):
                                finish(t)
                                x_hi(v, yB, bh, t)
                            v.wait_ge(S("v_py"), 3)
                            x_hi(v, yB, bh, KT - 1)
                            scale_h(v)
                            v.wait_ge(S("v_xh"), KT)
                        return
                    if inv:
                        for b in range(NC):
                            v.wait_ge(S("p_g"), b + 1)
                            G = G1[d] if b % 2 == 0 else G3[d]
                            c0 = 2 * (b // 2)
                            v.tensor_tensor(G[:, c0:c0 + 2, :], ps[:, b % 6, 0:384].rearrange("p (c x) -> p c x", c=2),
                                            maskG[d].rearrange("p (o x) -> p o x", o=1).broadcast_to([P, 2, 192]), ALU.mult)\
                             .then_inc(S("v_g"), 1)
                            if b % 2:
                                chain(b // 2, b // 2 + 1)
                        chain(4, CHG)
                    for n in range(24):
                        if inv:
                            invert(n)
                        if CHG + n < 24:
                            chain(CHG + n, CHG + n + 1)
                        prepare(n)
                    if inv:
                        v.wait_ge(S("v_R"), 2 * LEVELS)
                    if prep:
                        v.wait_ge(S("v_bd"), 7 + 2 * d)
                    if has_chain and d == 0:
                        v.wait_ge(S("a_y"), NC)
                rw_regions(v, half, meet)
                def stream(n_iter, evac):
                    with v.Fori(0, n_iter - 1) as n:
                        for j in range(4):
                            evac(n, j)
                            w_hi(v, j, n + 1)
                    for j in range(4):
                        evac(n_iter - 1, j)

                v.sem_inc(S("v_out"), 1)
                for j in range(2):
                    v.sem_inc(S(f"ev{2 * j + 1}"), 1)
                for j in range(4):
                    w_hi(v, j, 0)

                def merge(n, j):
                    if j % 2 == 0:
                        return
                    if j == 1:
                        v.wait_ge(S("v_out"), n + 1)
                    v.wait_ge(S(f"ev{j - 1}"), n + 2)
                    v.wait_ge(S(f"p_mm{j}"), n + 2)
                    v.tensor_tensor(pa_[:, j // 2, :], ps[:, j, :], sga[:, j // 2, :], ALU.mult).then_inc(S(f"ev{j}"), 1)
                    if j == 3:
                        v.wait_ge(S("ev1"), n + 2)
                        v.wait_ge(S("ev3"), n + 2)
                        v.tensor_tensor(merged[:, ds(n, 1), :], pa_[:, 0:1, :], pa_[:, 1:2, :], ALU.add).then_inc(S("v_out"), 1)
                stream(KT, merge)
                v.wait_ge(S("v_out"), KT + 1)
                meet(v)
                free(v, "ev")
                w_hi(v, 0, 0)
                for t in range(KT):
                    x_hi(v, merged, mh, t)
                for j in range(1, 4):
                    w_hi(v, j, 0)

                def add_out(n, j):
                    v.wait_ge(S(f"p_mm{j}"), n + 2)
                    v.scalar_tensor_tensor(hT[:, ds(4 * n + j, 1), :], ps[:, j:j + 1, :], mod[:, 16 + 4 * n + j, :],
                                           hT[:, ds(4 * n + j, 1), :], ALU.mult, ALU.add).then_inc(S(f"ev{j}"), 1)
                stream(2, add_out)
                for j in range(4):
                    v.wait_ge(S(f"ev{j}"), 3)
                meet(v)
                ln_dve(v, lambda t: pcol[:, COL["ln1_g"] + t, :])
                for t in range(KT):
                    v.wait_ge(S("v_out"), t + 1)
                    v.tensor_scalar(uT[:, t, :], hT[:, t, :], mod[:, 32 + t, :], mod[:, 24 + t, :], ALU.mult, ALU.add)\
                     .then_inc(S("v_u"), 1)
                    v.wait_ge(S("v_u"), t + 1)
                    x_hi(v, uT, uh, t)
                    v.tensor_scalar(hT[:, t, :], hT[:, t, :], ALPHA, b2g[:, t:t + 1], ALU.mult, ALU.add).then_inc(S("v_gate"), 1)
                v.wait_ge(S("v_gate"), KT)
                v.wait_ge(S("v_xh"), KT)
                meet(v)
                for half_ in range(2):
                    v.sem_inc(S("g_fl"), 4)
                    for j in range(4):
                        w_hi(v, j, 0)

                    def units(n, j):
                        v.wait_ge(S(f"ev{j}"), n + 2)
                        v.wait_ge(S("g_fl"), 4 * n + j + 1)
                        v.tensor_tensor(fsq[:, j, :], fr[:, j, :], fr[:, j, :], ALU.mult).then_inc(S("v_sq"), 1)
                        v.wait_ge(S("v_sq"), 4 * n + j + 5)
                        v.tensor_copy(fh[:, ds(4 * n + j, 1), :], fsq[:, j:j + 1, :]).then_inc(S("v_fh"), 1)
                    stream(4, units)
                    v.wait_ge(S("v_fh"), FH)
                    meet(v)
                    free(v, "ev")
                    for j in range(4):
                        w_hi(v, j, 0)

                    def add_down(n, j):
                        if j % 2 == 0:
                            return
                        v.wait_ge(S(f"p_mm{j}"), n + 2)
                        t = 2 * n + j // 2
                        v.scalar_tensor_tensor(hT[:, ds(t, 1), :], ps[:, j // 2:j // 2 + 1, :], mod[:, 40 + t, :],
                                               hT[:, ds(t, 1), :], ALU.mult, ALU.add).then_inc(S(f"ev{j // 2}"), 1)
                    stream(4, add_down)
                    for j in range(2):
                        v.wait_ge(S(f"ev{j}"), 5)
                    meet(v)
                ln_dve(v, lambda t: pcol[:, COL["ln2_g"] + t, :])
                meet(v)
            for b in range(2 * NT):
                v.wait_ge(S("p_tr"), b + 1)
                v.tensor_copy(xtok[:, b // 2, (b % 2) * 512:(b % 2 + 1) * 512], ps[:, b % 4, :]).then_inc(S("v_tr"), 1)


def kernel(**inputs):
    import concourse.bacc as _bacc
    from concourse.bass_utils import run_bass_kernel_spmd as _run

    nc = _bacc.Bacc("TRN2", target_bir_lowering=False, num_devices=1)
    arrays, args = {}, {}
    for name, x in inputs.items():
        x = np.ascontiguousarray(x)
        arrays[f"in_{name}"] = x
        args[name] = nc.dram_tensor(f"in_{name}", x.shape, mybir.dt.from_np(x.dtype), kind="ExternalInput").ap()
    arrays["in_consts"] = constants()
    consts = nc.dram_tensor("in_consts", (P, NCONST), F32, kind="ExternalInput").ap()
    out = nc.dram_tensor("out_h", (1, T, D), F32, kind="ExternalOutput").ap()
    encoder(nc, args, consts, out)
    r = _run(nc, [arrays], core_ids=[0])
    return r.results[0]["out_h"]
```

```python
from contextlib import ExitStack

import numpy as np
import concourse.bass as bass
from concourse import mybir

ALU = mybir.AluOpType
ACT = mybir.ActivationFunctionType
F32 = mybir.dt.float32
F32R = mybir.dt.float32r
BF16 = mybir.dt.bfloat16
ds = bass.ds

P = 128
D = 1024
T = 512
DEPTH = 2
KT = D // P
NT = T // P
HA = 4
DK = 128
DV = 256
FF = 4 * D
FT = FF // P
C = 64
NC = T // C
HP = 8
LORA = 64
GLORA = 160
N_RW = 3 * D + 4 * LORA + GLORA
QK0, V0, O0, G0, Z0 = 0, D, 2 * D, 3 * D, 3 * D + 16
GA0 = Z0 + N_RW
GB0 = GA0 + D
WD0, AD0, GD0 = Z0 + 3 * D, Z0 + 3 * D + 128, Z0 + 3 * D + 256
ALPHA = (2.0 * DEPTH) ** 0.25
DECAY = float(np.exp(-0.5))
LEVELS = 6
BIG = 1e30

B0 = dict(conv_w=0, conv_b=40, norm_g=48, w0=56, a0=72, k_k=88, k_a=96, r_k=104, gn_g=112, gn_b=120)
B1 = dict(mup=0, mun=24, ln1_g=48, ln1_b=56, b2=64, ln2_g=72, ln2_b=80, b1=88, mup_lo=120, mun_lo=123,
          mup_g2=126, mun_g2=127)
COL = {**B0, **{k: 128 + v for k, v in B1.items()}, "ada_b": 256}

CI, CBD, CG, CL, CR, CC = 0, 128, 256, 640, 640 + 12 * 128, 640 + 12 * 128 + 1024
NCONST = CC + 256


def constants():
    c = np.zeros((P, NCONST), np.float32)
    i = np.arange(P)
    c[:, CI:CI + P] = np.eye(P)
    same = (i[:, None] // C) == (i[None, :] // C)
    c[:, CBD:CBD + P] = same
    s, t = i[:, None] % C, i[None, :] % C
    q = np.arange(C)[None, :]
    for d in range(2):
        before = (s < t) if d == 0 else (s > t)
        upto = (s <= q) if d == 0 else (s >= q)
        c[:, CG + 192 * d:CG + 192 * d + 128] = same & before
        c[:, CG + 192 * d + 128:CG + 192 * d + 192] = upto
        for k in range(LEVELS):
            pair = same & ((s >> (k + 1)) == (t >> (k + 1))) & ((s >> k) != (t >> k))
            low = pair & ((s > t) if d == 0 else (s < t))
            o = CL + (6 * d + k) * 128
            c[:, o:o + 128] = low | (i[:, None] == i[None, :])
        pos = np.arange(T) % C
        c[:, CR + T * d:CR + T * (d + 1)] = pos != (0 if d == 0 else C - 1)
        hidden = (i[:, None] > i[None, :]) if d == 0 else (i[:, None] < i[None, :])
        c[:, CC + 128 * d:CC + 128 * (d + 1)] = np.where(hidden, -BIG, 0.0)
    return c


def encoder(nc, a, consts, out):
    ctx = ExitStack()
    rkv_dram = nc.dram_tensor("rkv_dram", (P, 3 * KT, T), F32).ap()
    h_dram = nc.dram_tensor("h_dram", (P, KT, T), F32).ap()
    with ctx:
        def sb(name, shape, dt=F32):
            return ctx.enter_context(nc.sbuf_tensor(name, shape, dt))

        NA = 28100
        both = ExitStack()
        hT = both.enter_context(nc.sbuf_tensor("hT", [P, KT, T], F32))
        wt = both.enter_context(nc.sbuf_tensor("wt", [P, 4, KT, P], F32))
        uT = both.enter_context(nc.sbuf_tensor("uT", [P, KT, T], F32))
        yA = both.enter_context(nc.sbuf_tensor("yA", [P, KT, T], F32))
        yB = both.enter_context(nc.sbuf_tensor("yB", [P, KT, T], F32))
        arena = both.enter_context(nc.sbuf_tensor("arena", [P, NA], F32))
        both.close()
        o_uh = NC * 2 * 192 * 3 + NC * P * 8
        o_ah = o_uh + NC * P * 4 + 2 * NC + 5 * P
        uh2 = sb("uh2", [P, KT, T], F32R)
        wtl = sb("wtl", [P, 4, KT, P], F32R)
        ul = sb("ul", [P, KT, T], F32R)
        abl = sb("abl", [P, 2 * KT, T], F32R)
        wh = sb("wh", [P, 4, KT, P], F32R)
        wl = sb("wl", [P, 4, KT, P], F32R)
        hh = sb("hh", [P, 2 * KT, T], F32R)
        sb("skip0", [P, o_uh - 16 * D])
        uh = sb("uh", [P, KT, T], F32R)
        sb("skip1", [P, o_ah - o_uh - KT * T])
        ah = sb("ah", [P, KT, T], F32R)
        sb("skip2", [P, NA - o_ah - KT * T])

        pcol = sb("pcol", [P, 3 * P, 1])
        mod = sb("mod", [P, 48, 1])
        mix0 = sb("mix0", [P, 28, 1])
        ka1 = sb("ka1", [P, KT, 1])
        b2g = sb("b2g", [P, KT])
        modr = sb("modr", [P, 48])
        lncol = sb("lncol", [P, 24, 1])
        cond = sb("cond", [P, 16, 1])
        eps = sb("eps", [P, 2])
        gbias = sb("gbias", [64, 2])
        ident = sb("ident", [P, P])
        bd = sb("bd", [P, P])
        ones = sb("ones", [P, P])
        mask = sb("mask", [P, NCONST - CG], BF16)
        tw = sb("tw", [P, T])
        ad = sb("ad", [P, T])
        gd = sb("gd", [P, T])
        gd2 = sb("gd2", [P, T])
        ps = ctx.enter_context(nc.psum_tensor("ps", [P, 8, 512], F32))

        class Carve:
            def __init__(self):
                self.at = 0

            def __call__(self, *shape, parts=P):
                n = int(np.prod(shape))
                v = arena[0:parts, self.at:self.at + n]
                self.at += n
                assert self.at <= NA, self.at
                if len(shape) == 2:
                    v = v.rearrange("p (a b) -> p a b", a=shape[0])
                if len(shape) == 3:
                    v = v.rearrange("p (a b c) -> p a b c", a=shape[0], b=shape[1])
                return v

        def m(o, n):
            return mask[:, o - CG:o - CG + n]

        maskG = [m(CG + 192 * d, 192) for d in range(2)]
        maskL = [[m(CL + (6 * d + k) * 128, 128) for k in range(LEVELS)] for d in range(2)]
        maskR = [m(CR + T * d, T) for d in range(2)]
        maskC = [m(CC + 128 * d, 128) for d in range(2)]

        cv = Carve()
        craw = cv(NCONST)
        xtok = cv(NT, D)
        sq8 = cv(KT, T)
        prow0 = cv(P)
        std = cv(T)
        rstd = cv(T)
        adaw0 = [cv(KT, 512) for _ in range(3)]
        adas0 = cv(4, 512)
        prow = arena[:, NA - 3 * P:NA].rearrange("p (a b) -> p a b", a=3)
        hsum = arena[:, NA - 3 * P - T:NA - 3 * P]
        assert cv.at <= NA - 3 * P - T
        ul2 = abl[:, KT:2 * KT, :]
        wqh = hh[:, 0:KT, :].rearrange("p (s a) (b n) -> p s (a b) n", s=4, n=P)
        wvh = wl[:, 0:2, :, :].rearrange("p s k n -> p (s k n)").rearrange("p (k n) -> p k n", k=KT)
        wvl = wh[:, 0:2, :, :].rearrange("p s k n -> p (s k n)").rearrange("p (k n) -> p k n", k=KT)
        cv = Carve()
        wv = cv(KT, DV)
        acol = cv(NT, 64)
        selh = cv(2, P)
        dg = cv(2, NT, P)
        cv.at = 6 * D
        rows = cv(2, T)
        vtok = cv(NT, DV)
        cv.at = 12 * D
        Ew = cv(2, NT, T)
        qk = cv(2, T)
        Pw = cv(2, NT, T)
        emx = cv(2, T)
        so = cv(2, T)
        rf = cv(2, T)
        hs = cv(2, T)
        ht = qk
        hq = cv(2, T)
        sg = hq
        hstd = cv(T)
        cv = Carve()
        cv.at = 12 * D
        wg16 = cv(KT, 16)
        wgp = cv(KT, 2, 64)
        gx = cv(6, T, parts=64)
        Gs = cv(T, parts=64)
        aS = cv(T, parts=64)
        zero = cv(T, parts=64)
        one = cv(T, parts=64)
        cv = Carve()
        AQ = [cv(NC, 192) for _ in range(2)]
        G1 = [cv(NC, 192) for _ in range(2)]
        G3 = [cv(NC, 192) for _ in range(2)]
        XT = [cv(NC, P) for _ in range(2)]
        Bt = [cv(NC, P) for _ in range(2)]
        Ktk = [cv(NC, P) for _ in range(2)]
        Vt = [cv(NC, P) for _ in range(2)]
        Bz = cv(NC, P)
        Kz = cv(NC, P)
        Xm = cv(NC, P)
        Rm = cv(NC, P)
        dend = [cv(NC) for _ in range(2)]
        Sst = cv(2, P)
        Sd = cv(P)
        Zs = cv(P)
        Us = cv(P)
        assert cv.at == NC * 2 * 192 * 3 + NC * P * 12 + 2 * NC + 5 * P
        rr, kr, vr, kk = cv(T), cv(T), cv(T), cv(T)
        sw, aa, kmf, Ex, ysum, yf = cv(T), cv(T), cv(T), cv(T), cv(T), cv(T)
        km = sw
        Lc, Lx, Ep, En, rks = (hT[:, q, :] for q in range(5))
        spare = wt[:, 3, :, :].rearrange("p a b -> p (a b)")
        bonus, gbuf = spare[:, 0:T], spare[:, T:2 * T]
        wup = cv(2, 2, P)
        gup = cv(P)
        gup2 = cv(P)
        kr_sq = En
        ysq = yB[:, HP - 1, :]
        assert o_ah + 9 * T <= NA - 3 * P
        Vz = XT[0]
        al, bl = abl[:, 0:KT, :], abl[:, KT:2 * KT, :]
        bh = hh[:, 0:KT, :]
        mh, ml = uh, hh[:, KT:2 * KT, :]
        merged = arena[:, 12 * D:16 * D].rearrange("p (a b) -> p a b", a=KT)
        pa_ = arena[:, 16 * D:17 * D].rearrange("p (a b) -> p a b", a=2)
        sga = arena[:, o_ah + KT * T:o_ah + KT * T + 2 * T].rearrange("p (a b) -> p a b", a=2)
        FH = FT // 2
        assert FH == 2 * KT
        fh, fl = hh, abl
        xs = arena[:, o_ah:o_ah + 4 * T].rearrange("p (a b) -> p a b", a=4)
        adaw = [arena[:, o:o + 8 * 512].rearrange("p (k n) -> p k n", k=KT) for o in (12 * D, 8 * D, o_ah)]
        adas = arena[:, 16 * D:17 * D].rearrange("p (a b) -> p a b", a=2)
        fr = arena[:, o_ah:o_ah + 4 * T].rearrange("p (a b) -> p a b", a=4)
        fsq = arena[:, o_ah + 4 * T:o_ah + 8 * T].rearrange("p (a b) -> p a b", a=4)

        sems = {}

        def S(name):
            if name not in sems:
                sems[name] = ctx.enter_context(nc.semaphore(name))
            return sems[name]

        arrived = [ctx.enter_context(nc.semaphore(f"arrived{j}")) for j in range(2)]
        opened = [ctx.enter_context(nc.semaphore(f"opened{j}")) for j in range(2)]

        cleared = [
            "ld_w0", "ld_w1", "ld_w2", "ld_w3", "ld_par", "ld_id", "ld_mask", "ld_vec", "ld_x", "st_out",
            "p_tr", "v_tr", "p_mm0", "p_mm1", "p_mm2", "p_mm3", "ev0", "ev1", "ev2", "ev3",
            "ld_ada", "v_ada", "p_ada", "v_mod", "p_mean", "v_cen", "a_sq", "p_var", "a_std", "v_rstd", "v_nrm", "v_out",
            "v_hs", "v_xl", "hi0", "hi1", "hi2", "hi3", "lo0", "lo1", "lo2", "lo3", "v_xh", "g_xl", "v_sq", "v_fh", "g_fl",
            "g_set", "v_set", "v_gb", "a_set", "v_u",
            "a_c0", "v_s1", "v_s2", "a_act", "v_gate", "a_gate",
            "ld_v", "ld_wv", "ld_up", "ld_gu", "st_h", "ld_h", "ld_r", "ld_k", "ld_vr",
            "st_x0", "st_x1", "st_x2", "st_x3", "v_conv", "a_sig", "v_qk", "p_v", "a_v", "a_o", "v_sel", "p_s", "p_nm", "p_nx",
            "v_dg", "a_E", "a_emx", "v_P", "p_den", "v_den", "p_num", "v_num", "v_h", "p_m2", "a_h2",
            "a_kk", "p_ss", "v_ss", "a_nrm", "v_kk", "p_lw", "a_lw", "v_L", "g_Lx", "a_exp", "v_km", "v_bd",
            "g_dend", "v_dend", "p_g", "v_g", "g_in", "p_bt", "a_bt", "g_vb",
            "v_hw", "g_hw", "p_T", "p_Yt", "v_R", "v_Y", "p_XY", "a_X", "a_Y",
            "p_Z", "a_Z", "p_U", "v_U", "p_S", "v_Sd", "v_S", "p_Y", "a_y",
            "p_pm", "v_pc", "a_psq", "p_pv", "a_pstd", "v_pr", "v_py", "v_rk", "p_bon", "v_bon", "p_gu", "a_gu",
        ]
        for n in cleared:
            S(n)
        lo = min(sems[n].num for n in cleared)
        hi = max(sems[n].num for n in cleared)
        assert hi - lo + 1 == len(cleared)

        def meet(e):
            e.sem_inc(arrived[0], 1)
            e.wait_ge(opened[0], 1)
            e.sem_inc(arrived[1], 1)
            e.wait_ge(opened[1], 1)

        def meet_sp(e):
            e.wait_ge(arrived[0], 4)
            e.sem_clear(range(lo, hi + 1))
            e.sem_clear(arrived[0])
            e.sem_clear(opened[1])
            e.sem_inc(opened[0], 1)
            e.wait_ge(arrived[1], 4)
            e.sem_clear(arrived[1])
            e.sem_clear(opened[0])
            e.sem_inc(opened[1], 1)

        block = ctx.enter_context(nc.Block())
        w_in, w_a, w_b, w_o = a["w_in"], a["w_branch_a"], a["w_branch_b"], a["w_out"]

        def sum_h(v, t, n):
            v.wait_ge(S("v_hs"), n + 1)
            v.tensor_tensor(hsum.rearrange("p (o t) -> p o t", o=1), hsum.rearrange("p (o t) -> p o t", o=1),
                            hT[:, ds(t, 1), :], ALU.add).then_inc(S("v_hs"), 1)

        def ln_pe(p):
            p.matmul(ps[:, 0, :], ones[:, 0:P], hsum, start=True, stop=True).then_inc(S("p_mean"), 1)
            for t in range(KT):
                p.wait_ge(S("a_sq"), t + 1)
                mm = p.matmul(ps[:, 1, :], ones[:, 0:P], sq8[:, t, :], start=t == 0, stop=t == KT - 1)
            mm.then_inc(S("p_var"), 1)

        def ln_act(s, b):
            for t in range(KT):
                s.wait_ge(S("v_cen"), t + 1)
                s.activation(sq8[:, t, :], hT[:, t, :], ACT.Square).then_inc(S("a_sq"), 1)
            s.wait_ge(S("p_var"), 1)
            s.activation(std, ps[:, 1, :], ACT.Sqrt, bias=eps[:, 0:1], scale=1.0 / D).then_inc(S("a_std"), 1)
            for t in range(KT):
                s.wait_ge(S("v_nrm"), t + 1)
                s.activation(hT[:, t, :], hT[:, t, :], ACT.Identity, bias=b(t)).then_inc(S("v_out"), 1)
            s.wait_ge(S("v_out"), KT)

        def ln_dve(v, g, between=None):
            v.wait_ge(S("p_mean"), 1)
            for t in range(KT):
                v.scalar_tensor_tensor(hT[:, t, :], ps[:, 0, :], -1.0 / D, hT[:, t, :], ALU.mult,
                                       ALU.add).then_inc(S("v_cen"), 1)
            if between:
                between()
            v.wait_ge(S("a_std"), 1)
            v.reciprocal(rstd, std).then_inc(S("v_rstd"), 1)
            v.wait_ge(S("v_rstd"), 1)
            v.wait_ge(S("a_sq"), KT)
            for t in range(KT):
                v.scalar_tensor_tensor(hT[:, t, :], hT[:, t, :], g(t), rstd, ALU.mult,
                                       ALU.mult).then_inc(S("v_nrm"), 1)

        def ada_sum(v, tile, w, acc):
            v.wait_ge(S("ld_ada"), 16 * tile + 16)
            v.tensor_scalar(acc, w[:, 0, :], cond[:, 8, :], None, ALU.mult).then_inc(S("v_ada"), 1)
            for k in range(1, KT):
                v.wait_ge(S("v_ada"), KT * tile + k)
                v.scalar_tensor_tensor(acc, w[:, k, :], cond[:, 8 + k, :], acc, ALU.mult, ALU.add).then_inc(S("v_ada"), 1)

        def ada_mm(p, tile, bank, acc):
            p.wait_ge(S("v_ada"), KT * (tile + 1))
            for j in range(4):
                mm = p.matmul(ps[:, bank, j * P:(j + 1) * P], acc[:, j * P:(j + 1) * P], ones[:, 0:P], start=True, stop=True)
            mm.then_inc(S("p_ada"), 1)

        def ada_take(v, tile, bank, at):
            v.wait_ge(S("p_ada"), tile + 1)
            v.tensor_copy(modr[:, ds(at, 4)], ps[:, bank, 0:T:P])\
             .then_inc(S("v_mod"), 1)

        def modulate(v, first):
            for t in range(KT):
                v.tensor_scalar(uT[:, t, :], hT[:, t, :], mod[:, first + 8 + t, :], mod[:, first + t, :],
                                ALU.mult, ALU.add).then_inc(S("v_u"), 1)

        def load_w(e, slot, src, col, n=P):
            e.dma_start(wt[:, slot, :, 0:n], src.rearrange("(k p) n -> p k n", p=P)[:, :, ds(col, n)])\
             .then_inc(S(f"ld_w{slot}"), 16)

        def w_hi(v, j, i):
            v.wait_ge(S(f"ld_w{j}"), 16 * i + 16)
            v.wait_ge(S(f"p_mm{j}"), i + 1)
            v.tensor_copy(wh[:, j, :, :], wt[:, j, :, :]).then_inc(S(f"hi{j}"), 1)

        def w_lo(g, j, i):
            g.wait_ge(S(f"hi{j}"), i + 1)
            g.tensor_tensor(wl[:, j, :, :], wt[:, j, :, :], wh[:, j, :, :].bitcast(F32), ALU.subtract)\
             .then_inc(S(f"lo{j}"), 1)

        def dense3(p, j, i, bank, xh, xl, first=True, last=True):
            p.wait_ge(S(f"hi{j}"), i + 1)
            for n, x in enumerate((xh, xl)):
                for k in range(KT):
                    p.matmul(ps[:, bank, :], wh[:, j, k, :], x[:, k, :], start=first and n == 0 and k == 0, stop=False)
            p.wait_ge(S(f"lo{j}"), i + 1)
            for k in range(KT):
                mm = p.matmul(ps[:, bank, :], wl[:, j, k, :], xh[:, k, :], start=False, stop=last and k == KT - 1)
            mm.then_inc(S(f"p_mm{j}"), 1)

        def free(e, name):
            for j in range(4):
                e.sem_inc(S(f"{name}{j}"), 1)

        def x_hi(v, x, xh, t):
            v.tensor_copy(xh[:, t, :], x[:, t, :]).then_inc(S("v_xh"), 1)

        def x_lo(g, x, xh, xl, t, n, done="g_xl"):
            g.wait_ge(S("v_xh"), n + 1)
            g.tensor_tensor(xl[:, t, :], x[:, t, :], xh[:, t, :].bitcast(F32), ALU.subtract).then_inc(S(done), 1)

        def shift(v, x, z, mp, mn, j):
            v.wait_ge(S("a_c0"), j + 1)
            v.scalar_tensor_tensor(x[:, 1:T], z[:, 0:T - 1], mp, x[:, 1:T], ALU.mult, ALU.add).then_inc(S("v_s1"), 1)
            v.wait_ge(S("v_s1"), j + 1)
            v.scalar_tensor_tensor(x[:, 0:T - 1], z[:, 1:T], mn, x[:, 0:T - 1], ALU.mult, ALU.add)\
             .then_inc(S("v_s2"), 1)

        def scale_h(v):
            for t in range(KT):
                v.tensor_scalar(hT[:, t, :], hT[:, t, :], ALPHA, None, ALU.mult).then_inc(S("v_cen"), 1)
            v.wait_ge(S("v_cen"), KT)

        def ml_regions(e, head, meet_):
            head(False, 0)
            meet_(e)
            with e.Fori(1, HA) as h:
                head(True, h)
                meet_(e)

        def span(d, t):
            return (t * P, T) if d == 0 else (0, (t + 1) * P)

        CHG = 6

        def rw_regions(e, half, meet_):
            half(1, False, False, False, True, -1)
            meet_(e)
            half(0, True, False, False, True, 0)
            meet_(e)
            half(1, True, True, False, True, 0)
            meet_(e)
            with e.Fori(1, HP - 1) as hp:
                half(0, True, True, False, True, hp)
                meet_(e)
                half(1, True, True, True, True, hp)
                meet_(e)
            half(0, True, True, False, True, HP - 1)
            meet_(e)
            half(1, True, True, True, False, HP - 1)
            meet_(e)
            half(0, False, True, False, False, HP)
            meet_(e)
            half(1, False, False, True, False, HP)
            meet_(e)

        @block.sync
        def _(e):
            def layer_vectors(l):
                def par(row, blk, src, n=8):
                    e.dma_start(prow[row:row + n, blk, :], src).then_inc(S("ld_vec"), 16)

                def vec(x):
                    return x.rearrange("(t p) -> t p", p=P)

                def vec2(x):
                    return x.rearrange("j (t p) -> (j t) p", p=P)
                par(B0["conv_w"], 0, vec2(a["mlstm_conv_w"][l]), 40)
                par(B0["conv_b"], 0, vec(a["mlstm_conv_b"][l]))
                par(B0["norm_g"], 0, vec(a["mlstm_norm_g"][l]))
                par(B0["w0"], 0, vec2(a["rwkv_w0"][l]), 16)
                par(B0["a0"], 0, vec2(a["rwkv_a0"][l]), 16)
                par(B0["k_k"], 0, vec(a["rwkv_k_k"][l]))
                par(B0["k_a"], 0, vec(a["rwkv_k_a"][l]))
                par(B0["r_k"], 0, a["rwkv_r_k"][l].rearrange("(t h) n -> t (h n)", h=2))
                par(B0["gn_g"], 0, vec(a["rwkv_gn_g"][l]))
                par(B0["gn_b"], 0, vec(a["rwkv_gn_b"][l]))
                mu = a["rwkv_mu"][l]
                par(B1["mup"], 1, vec(mu[0, 0:3 * D]), 24)
                par(B1["mun"], 1, vec(mu[1, 0:3 * D]), 24)
                par(B1["mup_lo"], 1, vec(mu[0, 3 * D:3 * D + 384]), 3)
                par(B1["mun_lo"], 1, vec(mu[1, 3 * D:3 * D + 384]), 3)
                for j in range(2):
                    e.dma_start(prow[126 + j:127 + j, 1, 0:32], mu[j:j + 1, 3 * D + 384:N_RW])\
                     .then_inc(S("ld_vec"), 16)
                par(B1["ln1_g"], 1, vec(a["ln1_g"][l]))
                par(B1["ln1_b"], 1, vec(a["ln1_b"][l]))
                par(B1["b2"], 1, vec(a["mlp_b2"][l]))
                par(B1["ln2_g"], 1, vec(a["ln2_g"][l]))
                par(B1["ln2_b"], 1, vec(a["ln2_b"][l]))
                par(B1["b1"], 1, vec(a["mlp_b1"][l]), 32)
                par(0, 2, vec(a["ada_b"][l]), 48)
                for j, n in enumerate(("mlstm_ig_b", "mlstm_fg_b")):
                    for d in range(2):
                        e.dma_start(gbias[32 * d:32 * d + 4, j:j + 1], a[n][l][d].rearrange("(h o) -> h o", o=1))\
                         .then_inc(S("ld_vec"), 16)
            e.dma_start(craw[:, 0:CG], consts[:, 0:CG]).then_inc(S("ld_id"), 16)
            e.dma_start(xtok, a["x"][0].rearrange("(t p) d -> p t d", p=P)).then_inc(S("ld_x"), 16)
            for j, n in enumerate(("ln0_g", "ln0_b")):
                e.dma_start(prow0[8 * j:8 * j + 8, :], a[n].rearrange("(t p) -> t p", p=P))\
                 .then_inc(S("ld_par"), 16)
            e.dma_start(prow0[16:24, :], a["c"].rearrange("o (t p) -> (o t) p", p=P)).then_inc(S("ld_par"), 16)

            def load_ada(dst, l, i):
                e.dma_start(dst, a["ada_w"][l].rearrange("(k p) n -> p k n", p=P)[:, :, ds(i * 512, 512)])\
                 .then_inc(S("ld_ada"), 16)
            load_ada(adaw0[0], 0, 0)
            e.dma_start(craw[:, CG:NCONST], consts[:, CG:NCONST]).then_inc(S("ld_mask"), 16)
            e.wait_ge(S("v_gb"), 2)
            layer_vectors(0)
            for i in range(1, 4):
                e.wait_ge(S("ld_ada"), 16 * i)
                if i == 3:
                    e.wait_ge(S("v_ada"), KT)
                load_ada(adaw0[i % 3], 0, i)
            e.wait_ge(S("ld_vec"), 16 * 27)
            meet_sp(e)
            with e.Fori(0, DEPTH) as l:
                meet_sp(e)
                def head_w(h, used):
                    for s, col in enumerate((QK0 + h * DK, QK0 + 512 + h * DK, O0 + h * DV, O0 + P + h * DV)):
                        used(s)
                        load_w(e, s, w_in[l], col)

                def v_w(h):
                    e.dma_start(wv, w_in[l].rearrange("(k p) n -> p k n", p=P)[:, :, ds(V0 + h * DV, DV)])\
                     .then_inc(S("ld_wv"), 16)
                e.dma_start(wg16, w_in[l].rearrange("(k p) n -> p k n", p=P)[:, :, G0:G0 + 16]).then_inc(S("ld_v"), 16)
                e.dma_start(h_dram, hT[:, :, :]).then_inc(S("st_h"), 16)
                v_w(0)
                head_w(0, lambda s: None)
                e.wait_ge(S("ld_wv"), 16)
                e.wait_ge(S("st_h"), 16)
                meet_sp(e)
                with e.Fori(0, HA) as h:
                    def used(s):
                        if s == 2:
                            e.wait_ge(S("p_v"), NT)
                            v_w(h + 1)
                        e.wait_ge(S(f"p_mm{s // 2}"), s % 2 + 1)
                    head_w(h + 1, used)
                    meet_sp(e)
                def rw_up(hp):
                    for j, n in enumerate(("rwkv_w_up", "rwkv_a_up")):
                        for d in range(2):
                            e.dma_start(wup[64 * d:64 * d + 64, j, d, :], a[n][l][d][:, ds(hp * P, P)])\
                             .then_inc(S("ld_up"), 16)

                def rw_gup(hp):
                    e.dma_start(gup, a["rwkv_g_up"][l][0:P, ds(hp * P, P)]).then_inc(S("ld_gu"), 16)
                    e.dma_start(gup2[0:GLORA - P, :], a["rwkv_g_up"][l][P:GLORA, ds(hp * P, P)]).then_inc(S("ld_gu"), 16)

                def rw_w(i, s):
                    load_w(e, s, w_in[l], Z0 + (i - 1) * 512 + s * P)
                for s, col in enumerate((WD0, AD0, GD0, GD0 + P)):
                    load_w(e, s, w_in[l], col)
                load_ada(adaw[0], l, 4)
                e.wait_ge(S("g_dend"), 2)
                rw_up(0)
                rw_gup(0)

                def store(i, s):
                    e.wait_ge(S("v_s2"), 4 * i + s + 1)
                    e.dma_start(rkv_dram[:, ds(4 * (i - 1) + s, 1), :], xs[:, s:s + 1, :]).then_inc(S(f"st_x{s}"), 16)
                for s in range(4):
                    e.wait_ge(S(f"lo{s}"), 1)
                    rw_w(1, s)
                e.wait_ge(S("ld_ada"), 16)
                load_ada(adaw[1], l, 5)
                e.wait_ge(S("ld_ada"), 32)
                e.wait_ge(S("v_ada"), KT)
                load_ada(adaw[0], l, 6)
                with e.Fori(2, 7) as i:
                    for s in range(4):
                        e.wait_ge(S(f"lo{s}"), i)
                        rw_w(i, s)
                        store(i - 1, s)
                    e.wait_ge(S("v_ada"), KT * (i + 1))
                    load_ada(adaw[0], l, 5 + i)
                for s in range(4):
                    store(6, s)
                for s in range(4):
                    e.wait_ge(S(f"st_x{s}"), 16 * 7)
                    e.wait_ge(S(f"ld_w{s}"), 16 * 7)
                e.wait_ge(S("ld_up"), 64)
                e.wait_ge(S("ld_gu"), 32)
                meet_sp(e)

                def load_x(x, name, m):
                    e.dma_start(x.rearrange("p (o t) -> p o t", o=1), rkv_dram[:, ds(m, 1), :]).then_inc(S(name), 16)

                def half1(hp):
                    load_x(kr, "ld_k", KT + hp + 1)
                    rw_up(hp + 1)
                    load_x(rr, "ld_r", hp + 1)
                    e.wait_ge(S("p_gu"), 1)
                    rw_gup(hp + 1)
                    e.wait_ge(S("v_bon"), 1)
                    load_x(vr, "ld_vr", 2 * KT + hp + 1)
                    e.wait_ge(S("ld_gu"), 32)
                    meet_sp(e)
                load_x(kr, "ld_k", KT)
                e.sem_inc(S("ld_up"), 64)
                load_x(rr, "ld_r", 0)
                load_x(vr, "ld_vr", 2 * KT)
                meet_sp(e)
                meet_sp(e)
                half1(0)
                with e.Fori(1, HP - 1) as hp:
                    meet_sp(e)
                    half1(hp)
                meet_sp(e)
                meet_sp(e)
                merge_src, merge_col = [w_in[l], w_a[l], w_in[l], w_b[l]], [GA0, 0, GB0, 0]

                def stream(n_iter, load, loaded):
                    for s in range(4):
                        if s in loaded:
                            e.sem_inc(S(f"ld_w{s}"), 16)
                        else:
                            load(0, s)
                    with e.Fori(1, n_iter) as i:
                        for s in range(4):
                            e.wait_ge(S(f"lo{s}"), i)
                            load(i, s)

                def ahead(n_iter, load, slots=range(4)):
                    for s in slots:
                        if n_iter:
                            e.wait_ge(S(f"lo{s}"), n_iter)
                        load(0, s)
                    for s in slots:
                        e.wait_ge(S(f"ld_w{s}"), 16 * n_iter + 16)

                def merge_w(i, s):
                    load_w(e, s, merge_src[s], merge_col[s] + i * P)

                def out_w(i, s):
                    load_w(e, s, w_o[l], i * 512 + s * P)

                def up_w(half_):
                    return lambda i, s: load_w(e, s, a["mlp_w1"][l], half_ * (FF // 2) + i * 512 + s * P)

                def down_w(half_):
                    def load(i, s):
                        q = 2 * half_ + s % 2
                        load_w(e, s, a["mlp_w2"][l][q * D:(q + 1) * D, :], i * 256 + (s // 2) * P)
                    return load
                e.dma_start(hT[:, :, :], h_dram).then_inc(S("ld_h"), 16)
                ahead(0, merge_w, range(3))
                e.wait_ge(S("ld_h"), 16)
                meet_sp(e)
                meet_sp(e)
                stream(KT, merge_w, range(3))
                ahead(KT, out_w)
                meet_sp(e)
                stream(2, out_w, range(4))
                e.wait_ge(S("v_gb"), 1)
                layer_vectors(1 - l)
                ahead(2, up_w(0))
                e.wait_ge(S("ld_vec"), 16 * 27)
                meet_sp(e)
                meet_sp(e)
                for half_ in range(2):
                    stream(4, up_w(half_), range(4))
                    ahead(4, down_w(half_))
                    meet_sp(e)
                    load_ada(adaw[2], 1 - l, 2 * half_)
                    stream(4, down_w(half_), range(4))
                    e.wait_ge(S("v_ada"), KT)
                    load_ada(adaw[2], 1 - l, 2 * half_ + 1)
                    if half_ == 0:
                        ahead(4, up_w(1))
                    else:
                        for s in range(4):
                            e.wait_ge(S(f"ld_w{s}"), 64)
                    meet_sp(e)
                meet_sp(e)
            for t in range(NT):
                e.wait_ge(S("v_tr"), 2 * t + 2)
                e.dma_start(out[0, t * P:(t + 1) * P, :], xtok[:, t, :]).then_inc(S("st_out"), 16)
            e.wait_ge(S("st_out"), 16 * NT)

        @block.tensor
        def _(p):
            p.wait_ge(S("v_set"), 6)
            p.wait_ge(S("ld_par"), 48)
            p.transpose(ps[:, 7, 0:24], prow0[0:24, :], ident[0:24, 0:24]).then_inc(S("p_tr"), 1)
            p.wait_ge(S("ld_x"), 16)
            for t in range(KT):
                if t >= 4:
                    p.wait_ge(S("v_tr"), t - 2)
                for q in range(NT):
                    mm = p.transpose(ps[:, t % 4, q * P:(q + 1) * P], xtok[:, q, t * P:(t + 1) * P], ident[:, :])
                mm.then_inc(S("p_tr"), 1)
            p.wait_ge(S("v_hs"), KT + 1)
            ln_pe(p)
            for i in range(4):
                ada_mm(p, i, 2 + i, adas0[:, i, :])
            meet(p)
            with p.Fori(0, DEPTH) as l:
                for b in range(3):
                    n = P if b < 2 else 48
                    mm = p.transpose(ps[:, b, 0:n], prow[0:n, b, :], ident[0:n, 0:n])
                mm.then_inc(S("p_tr"), 1)
                meet(p)
                p.wait_ge(S("v_u"), KT)
                p.wait_ge(S("g_set"), 5)
                for k in range(KT):
                    mm = p.matmul(ps[:, 4, :], wgp[:, k, :, :].rearrange("p j n -> p (j n)"), uT[:, k, :],
                                  start=k == 0, stop=k == KT - 1)
                mm.then_inc(S("p_mm1"), 1)
                p.wait_ge(S("v_gate"), 4)
                for t in range(NT):
                    mm = p.transpose(ps[:, 6, t * 64:(t + 1) * 64], aS[:, t * P:(t + 1) * P], ident[0:64, 0:64])
                mm.then_inc(S("p_tr"), 1)
                meet(p)
                def mean():
                    for c in range(2):
                        mm = p.matmul(ps[:, 4, :], ones[:, 0:P], hs[:, c, :], start=c == 0, stop=c == 1)
                    mm.then_inc(S("p_m2"), 1)

                def var():
                    p.wait_ge(S("a_h2"), 2)
                    for c in range(2):
                        mm = p.matmul(ps[:, 5, :], ones[:, 0:P], hq[:, c, :], start=c == 0, stop=c == 1)
                    mm.then_inc(S("p_m2"), 1)

                def stab(d):
                    if d:
                        p.wait_ge(S("a_E"), 7)
                        p.wait_ge(S("v_dg"), NT)
                        p.wait_ge(S("a_emx"), 1)
                    p.matmul(ps[:, 6, :], selh[:, d, :], rows[:, 0, :], start=True, stop=True).then_inc(S("p_nm"), 1)
                    p.matmul(ps[:, 7, :], selh[:, d, :], rows[:, 1, :], start=True, stop=True).then_inc(S("p_nx"), 1)

                def den(d):
                    p.wait_ge(S("v_P"), NT * (d + 1))
                    p.wait_ge(S("a_emx"), 2)
                    p.wait_ge(S("a_E"), 14)
                    for n in range(NT):
                        t = n if d == 0 else NT - 1 - n
                        lo_, hi_ = span(d, t)
                        mm = p.matmul(ps[:, 6 + d, lo_:hi_], ones[:, 0:P], Pw[:, d, t, lo_:hi_], start=n == 0, stop=n == NT - 1)
                    mm.then_inc(S("p_den"), 1)

                def num(d, c, bank):
                    for n in range(NT):
                        t = n if d == 0 else NT - 1 - n
                        lo_, hi_ = span(d, t)
                        mm = p.matmul(ps[:, bank, lo_:hi_], vtok[:, t, c * P:(c + 1) * P], Pw[:, d, t, lo_:hi_],
                                      start=n == 0, stop=n == NT - 1)
                    mm.then_inc(S("p_num"), 1)

                def project(s, bank):
                    for n, (w, x) in enumerate(((wqh, uh2), (wqh, ul2), (wtl, uh2))):
                        for k in range(KT):
                            mm = p.matmul(ps[:, bank, :], w[:, s, k, :], x[:, k, :], start=n == 0 and k == 0,
                                          stop=n == 2 and k == KT - 1)
                    return mm

                def head(post, h):
                    if post:
                        mean()
                    p.wait_ge(S("v_sel"), 2)
                    stab(0)
                    project(0, 0).then_inc(S("p_mm0"), 1)
                    if post:
                        var()
                    stab(1)
                    project(1, 1).then_inc(S("p_mm0"), 1)
                    if post:
                        p.wait_ge(S("v_h"), 2)
                        p.wait_ge(S("a_std"), 1)
                    for t in range(NT):
                        for n, (x, w) in enumerate(((uh2, wvh), (uh2, wvl), (ul2, wvh))):
                            for k in range(KT):
                                mm = p.matmul(ps[:, 4 + t // 2, (t % 2) * DV:(t % 2 + 1) * DV], x[:, k, t * P:(t + 1) * P],
                                              w[:, k, :], start=n == 0 and k == 0, stop=n == 2 and k == KT - 1)
                        mm.then_inc(S("p_v"), 1)
                    p.wait_ge(S("v_qk"), 2)
                    for t in range(NT):
                        p.matmul(ps[:, t, :], qk[:, 1, t * P:(t + 1) * P], qk[:, 0, :], start=True, stop=True)\
                         .then_inc(S("p_s"), 1)
                    for d in range(2):
                        p.wait_ge(S("a_v"), d + 1)
                        project(2 + d, 4 + d).then_inc(S("p_mm1"), 1)
                        den(d)
                    for c in range(2):
                        p.wait_ge(S("a_o"), c + 1)
                        num(0, c, 4 + c)
                    for c in range(2):
                        num(1, c, c)
                ml_regions(p, head, meet)
                free(p, "p_mm")
                mean()
                for j in range(4):
                    dense3(p, j, 0, j, uh2, ul2)
                    if j == 0:
                        var()
                ada_mm(p, 0, 6, adas[:, 0, :])
                with p.Fori(1, 7) as n:
                    for j in range(4):
                        p.wait_ge(S("v_s2"), 4 * (n - 1) + j + 1)
                        dense3(p, j, n, j, uh2, ul2)
                        if j == 1:
                            p.wait_ge(S("v_mod"), n)
                            ada_mm(p, n, 6, adas[:, 1, :])
                p.wait_ge(S("v_mod"), 7)
                ada_mm(p, 7, 6, adas[:, 1, :])
                meet(p)

                def half(d, inv, has_chain, post, prep, hp):
                    def chain(lo_, hi_):
                        if not has_chain:
                            return
                        for n in range(lo_, hi_):
                            cd = 1 - d
                            i, ph = n // 3, n % 3
                            c = i if cd == 0 else NC - 1 - i
                            S_in = Sst[:, (i + 1) % 2, :]
                            if ph == 0:
                                if i >= 1:
                                    p.wait_ge(S("v_S"), i)
                                mm = p.matmul(ps[:, 6, 0:P], G3[cd][:, c, 0:P], Vt[cd][:, c, :], start=True, stop=i == 0)
                                if i:
                                    mm = p.matmul(ps[:, 6, 0:P], AQ[cd][:, c, 0:P], S_in, start=False, stop=True)
                                mm.then_inc(S("p_Z"), 1)
                            elif ph == 1:
                                p.wait_ge(S("a_Z"), i + 1)
                                if i:
                                    p.wait_ge(S("a_y"), i)
                                p.matmul(ps[:, 7, 0:P], XT[cd][:, c, :], Zs, start=True, stop=True).then_inc(S("p_U"), 1)
                            else:
                                p.wait_ge(S("v_U"), i + 1)
                                if i < NC - 1:
                                    p.matmul(ps[:, 6, P:2 * P], Ktk[cd][:, c, :], Vt[cd][:, c, :], start=True, stop=False)
                                    p.matmul(ps[:, 6, P:2 * P], Bt[cd][:, c, :], Us, start=False, stop=True)\
                                     .then_inc(S("p_S"), 1)
                                if i:
                                    p.matmul(ps[:, 7, P:2 * P], S_in, AQ[cd][:, c, C:C + P], start=True, stop=False)
                                p.matmul(ps[:, 7, P:2 * P], Us, G1[cd][:, c, C:C + P], start=i == 0, stop=False)
                                p.matmul(ps[:, 7, P:2 * P], Vt[cd][:, c, :], G3[cd][:, c, C:C + P], start=False, stop=True)\
                                 .then_inc(S("p_Y"), 1)

                    def invert(n):
                        k, ph, q = n // 4, n // 2 % 2, n % 2
                        cs = range(4 * q, 4 * q + 4)
                        if ph == 0:
                            if k == 0:
                                p.wait_ge(S("a_bt"), 4)
                                p.wait_ge(S("g_in"), NC)
                                p.wait_ge(S("v_g"), NC)
                            elif k == 1:
                                p.wait_ge(S("v_R"), q + 1)
                            else:
                                p.wait_ge(S("a_X"), 2 * (k - 2) + q + 1)
                            for c in cs:
                                dst = ps[:, 2 * q, (c % 4) * P:(c % 4 + 1) * P]
                                if k == 0:
                                    mm = p.transpose(dst, G1[d][:, c, 0:P], ident[:, :])
                                else:
                                    mm = p.matmul(dst, G1[d][:, c, 0:P], Xm[:, c, :], start=True, stop=True)
                            mm.then_inc(S("p_T"), 1)
                            if k >= 2:
                                for c in cs:
                                    mm = p.transpose(ps[:, 2 * q + 1, (c % 4) * P:(c % 4 + 1) * P], Xm[:, c, :], ident[:, :])
                                mm.then_inc(S("p_Yt"), 1)
                        elif k >= 1:
                            p.wait_ge(S("v_R"), 2 * k + q + 1)
                            if k == 1:
                                p.wait_ge(S("v_Y"), q + 1)
                            else:
                                p.wait_ge(S("a_Y"), 2 * (k - 2) + q + 1)
                            for c in cs:
                                p_c = slice((c % 4) * P, (c % 4 + 1) * P)
                                if k < LEVELS - 1:
                                    mm = p.matmul(ps[:, 2 * q, p_c], XT[d][:, c, :], Rm[:, c, :], start=True, stop=True)
                                else:
                                    mm = p.matmul(ps[:, 2 * q + 1, p_c], Rm[:, c, :], XT[d][:, c, :], start=True, stop=True)
                            mm.then_inc(S("p_XY"), 1)

                    def lora(j, bank, dd):
                        p.matmul(ps[:, bank, :], wup[:, j, dd, :], (tw, ad)[j][:, :], start=True, stop=True)\
                         .then_inc(S("p_lw"), 1)

                    def turn(z, q, bank):
                        for c in range(4):
                            mm = p.transpose(ps[:, bank, c * P:(c + 1) * P], z[:, 4 * q + c, :], ident[:, :])
                        mm.then_inc(S("p_bt"), 1)

                    def prepare(n):
                        if d == 0 and inv and n in (0, 1):
                            turn(Vz, n, 4 + n)
                        if d == 0 and not prep:
                            return
                        if d == 0:
                            if n == 3:
                                p.wait_ge(S("a_bt"), 6)
                                lora(0, 4, 1)
                                lora(1, 5, 1)
                            return
                        if n == 0 and post:
                            p.matmul(ps[:, 5, :], bd[:, :], ysum, start=True, stop=True).then_inc(S("p_pm"), 1)
                        if n == 4 and post:
                            p.wait_ge(S("a_psq"), 1)
                            p.matmul(ps[:, 5, :], bd[:, :], ysq, start=True, stop=True).then_inc(S("p_pv"), 1)
                        if n == 7 and inv:
                            if post:
                                p.wait_ge(S("a_pstd"), 1)
                            p.matmul(ps[:, 5, :], gup, gd[:, :], start=True, stop=False)
                            p.matmul(ps[:, 5, :], gup2, gd2[:, :], start=False, stop=True).then_inc(S("p_gu"), 1)
                        if n == 13 and inv:
                            p.wait_ge(S("a_gu"), 1)
                            p.matmul(ps[:, 5, :], bd[:, :], rks, start=True, stop=True).then_inc(S("p_bon"), 1)
                        if not prep:
                            return
                        if n == 0:
                            p.wait_ge(S("ld_up"), 64)
                            lora(0, 4, 0)
                        if n == 2:
                            p.wait_ge(S("a_lw"), 1)
                            lora(1, 4, 0)
                        if n == 4:
                            p.wait_ge(S("a_lw"), 2)
                            p.wait_ge(S("a_kk"), 1)
                            p.matmul(ps[:, 4, :], bd[:, :], kr_sq, start=True, stop=True).then_inc(S("p_ss"), 1)

                    if inv:
                        for b in range(NC):
                            if b >= 6:
                                p.wait_ge(S("v_g"), b - 5)
                            for c in range(2 * (b % 4), 2 * (b % 4) + 2):
                                mm = p.matmul(ps[:, b % 6, (c % 2) * 192:(c % 2 + 1) * 192], (Bz if b < 4 else Kz)[:, c, :],
                                              AQ[d][:, c, :], start=True, stop=True)
                            mm.then_inc(S("p_g"), 1)
                            if b % 2:
                                chain(b // 2, b // 2 + 1)
                        for j, z in enumerate((Bz, Kz)):
                            for q in range(2):
                                n = 2 * j + q
                                p.wait_ge(S("v_g"), min(NC, 3 + n))
                                turn(z, q, (NC + n) % 6)
                            chain(4 + j, 5 + j)
                    else:
                        chain(0, CHG)
                    for n in range(24):
                        if inv:
                            invert(n)
                        if CHG + n < 24:
                            chain(CHG + n, CHG + n + 1)
                        prepare(n)
                rw_regions(p, half, meet)

                free(p, "p_mm")
                with p.Fori(0, KT) as n:
                    for j, (xh, xl) in enumerate(((uh, ul), (ah, al), (uh, ul), (bh, bl))):
                        p.wait_ge(S(f"ev{j}"), n + 1)
                        dense3(p, j, n, j, xh, xl)
                meet(p)
                free(p, "p_mm")
                p.wait_ge(S("g_xl"), 4)
                p.wait_ge(S("v_xl"), 4)
                with p.Fori(0, 2) as n:
                    for j in range(4):
                        p.wait_ge(S(f"ev{j}"), n + 1)
                        dense3(p, j, n, j, mh, ml)
                meet(p)
                ln_pe(p)
                meet(p)
                for half_ in range(2):
                    free(p, "p_mm")
                    with p.Fori(0, 4) as n:
                        for j in range(4):
                            p.wait_ge(S(f"ev{j}"), n + 1)
                            dense3(p, j, n, j, uh, ul)
                    meet(p)
                    free(p, "p_mm")

                    def down(n):
                        for j in range(4):
                            k0, q = (j % 2) * KT, j // 2
                            if j % 2 == 0:
                                p.wait_ge(S(f"ev{q}"), n + 1)
                            dense3(p, j, n, q, fh[:, k0:k0 + KT, :], fl[:, k0:k0 + KT, :], j % 2 == 0, j % 2 == 1)
                    with p.Fori(0, 3) as n:
                        down(n)
                    ada_mm(p, 0, 6, adas[:, 0, :])
                    down(3)
                    ada_mm(p, 1, 7, adas[:, 1, :])
                    meet(p)
                ln_pe(p)
                meet(p)
            for t in range(NT):
                for q in range(2):
                    b = 2 * t + q
                    if b >= 4:
                        p.wait_ge(S("v_tr"), b - 3)
                    for c in range(4):
                        mm = p.transpose(ps[:, b % 4, c * P:(c + 1) * P], hT[:, 4 * q + c, t * P:(t + 1) * P], ident[:, :])
                    mm.then_inc(S("p_tr"), 1)

        @block.scalar
        def _(s):
            s.wait_ge(S("v_set"), 4)
            s.wait_ge(S("v_tr"), KT + 1)
            s.activation(cond[:, 0:8, :], lncol[:, 16:24, :], ACT.Sigmoid).then_inc(S("a_set"), 1)
            ln_act(s, lambda t: lncol[:, 8 + t, :])
            meet(s)
            with s.Fori(0, DEPTH) as l:
                meet(s)
                for j in range(2):
                    s.wait_ge(S("p_mm1"), 1)
                    s.activation(gx[:, j, :], ps[64 * j:64 * j + 64, 4, :], ACT.Identity, bias=gbias[:, j:j + 1]).then_inc(S("a_gate"), 1)
                s.wait_ge(S("a_gate"), 2)
                s.activation(gx[:, 2, :], gx[:, 1, :], ACT.Abs).then_inc(S("a_gate"), 1)
                s.wait_ge(S("a_gate"), 3)
                s.activation(gx[:, 3, :], gx[:, 2, :], ACT.Exp, scale=-1.0).then_inc(S("a_gate"), 1)
                s.wait_ge(S("a_gate"), 4)
                s.activation(gx[:, 4, :], gx[:, 3, :], ACT.Ln, bias=1.0).then_inc(S("a_gate"), 1)
                s.wait_ge(S("p_tr"), 1)
                s.activation(acol.rearrange("p a b -> p (a b)"), ps[:, 6, 0:256], ACT.Copy).then_inc(S("a_act"), 1)
                s.wait_ge(S("a_act"), 1)
                meet(s)
                def norm(h):
                    for c in range(2):
                        s.wait_ge(S("v_h"), 1 + c)
                        s.activation(hq[:, c, :], hs[:, c, :], ACT.Square).then_inc(S("a_h2"), 1)
                    s.wait_ge(S("p_m2"), 2)
                    s.activation(hstd, ps[:, 5, :], ACT.Sqrt, bias=eps[:, 0:1], scale=1.0 / DV).then_inc(S("a_std"), 1)

                def weights(d, h):
                    s.wait_ge(S("p_nx"), d + 1)
                    s.activation(emx[:, d, :], ps[:, 7, :], ACT.Exp).then_inc(S("a_emx"), 1)
                    s.wait_ge(S("p_nm"), d + 1)
                    s.wait_ge(S("v_dg"), NT * d + NT)
                    for t in range(NT):
                        bias = acol[:, t, ds(32 * d + h, 1)]
                        s.activation(Ew[:, d, t, t * P:(t + 1) * P], dg[:, d, t, :], ACT.Exp, bias=bias).then_inc(S("a_E"), 1)
                        lo_, hi_ = ((t + 1) * P, T) if d == 0 else (0, t * P)
                        if hi_ > lo_:
                            s.activation(Ew[:, d, t, lo_:hi_], ps[:, 6, lo_:hi_], ACT.Exp, bias=bias).then_inc(S("a_E"), 1)

                def conv(j, h):
                    s.wait_ge(S("p_mm0"), j + 1)
                    s.activation(qk[:, j, :], ps[:, j, :], ACT.Identity, scale=pcol[:, 2 * 8 + 4 * j + h, :],
                                 bias=pcol[:, COL["conv_b"] + 4 * j + h, :]).then_inc(S("a_c0"), 1)

                def head(post, h):
                    weights(0, h)
                    if post:
                        norm(h)
                    conv(0, h)
                    weights(1, h)
                    conv(1, h)
                    for j in range(2):
                        s.wait_ge(S("v_conv"), 4 * j + 4)
                        s.activation(sg[:, j, :], qk[:, j, :], ACT.Sigmoid).then_inc(S("a_sig"), 1)
                    for j in range(2):
                        s.wait_ge(S("p_v"), 2 * j + 2)
                        s.activation(vtok[:, 2 * j:2 * j + 2, :].rearrange("p a b -> p (a b)"), ps[:, 4 + j, :], ACT.Copy)\
                         .then_inc(S("a_v"), 1)
                    for j in range(2):
                        s.wait_ge(S("p_mm1"), j + 1)
                        if post:
                            s.wait_ge(S("v_out"), 2)
                        s.activation(so[:, j, :], ps[:, 4 + j, :], ACT.Sigmoid).then_inc(S("a_o"), 1)
                    s.wait_ge(S("a_o"), 2)
                ml_regions(s, head, meet)
                norm(HA)
                for j, (x, n) in enumerate(((tw, P), (ad, P), (gd, P), (gd2, 32))):
                    s.wait_ge(S(f"p_mm{j}"), 2)
                    s.activation(x[0:n, :], ps[0:n, j, :], ACT.Identity, scale=mix0[0:n, 24 + j, :]).then_inc(S("a_c0"), 1)
                s.wait_ge(S("v_s2"), 4)
                s.activation(tw[:, :], tw[:, :], ACT.Tanh).then_inc(S("a_act"), 1)
                s.activation(gd[:, :], gd[:, :], ACT.Sigmoid).then_inc(S("a_act"), 1)
                s.activation(gd2[0:32, :], gd2[0:32, :], ACT.Sigmoid).then_inc(S("a_act"), 1)
                for j in range(4):
                    s.sem_inc(S(f"st_x{j}"), 16)
                s.wait_ge(S("v_out"), 2)
                with s.Fori(1, 7) as n:
                    for j in range(4):
                        s.wait_ge(S(f"p_mm{j}"), n + 2)
                        s.wait_ge(S(f"st_x{j}"), 16 * n)
                        s.activation(xs[:, j, :], ps[:, j, :], ACT.Identity, scale=mix0[:, ds(4 * (n - 1) + j, 1), :])\
                         .then_inc(S("a_c0"), 1)
                s.wait_ge(S("a_act"), 3)
                meet(s)

                def half(d, inv, has_chain, post, prep, hp):
                    def chain(lo_, hi_):
                        if not has_chain:
                            return
                        for n in range(lo_, hi_):
                            cd = 1 - d
                            i, ph = n // 3, n % 3
                            c = i if cd == 0 else NC - 1 - i
                            if ph == 0:
                                s.wait_ge(S("p_Z"), i + 1)
                                if i:
                                    s.wait_ge(S("p_U"), i)
                                s.activation(Zs, ps[:, 6, 0:P], ACT.Copy).then_inc(S("a_Z"), 1)
                            elif ph == 2 and cd == 0:
                                s.wait_ge(S("p_Y"), i + 1)
                                s.activation(yf[:, c * C:(c + 1) * C], ps[:, 7, P + C:2 * P], ACT.Copy).then_inc(S("a_y"), 1)

                    def invert(n):
                        k, ph, q = n // 4, n // 2 % 2, n % 2
                        if ph == 1 and 1 <= k < LEVELS - 1:
                            s.wait_ge(S("p_XY"), 2 * (k - 1) + q + 1)
                            if k >= 2:
                                s.wait_ge(S("p_Yt"), 2 * (k - 2) + q + 1)
                            s.activation(Xm[:, 4 * q:4 * q + 4, :].rearrange("p a b -> p (a b)"), ps[:, 2 * q, :],
                                         ACT.Copy).then_inc(S("a_X"), 1)
                        if (ph == 0 and k >= 2) or (ph == 1 and k == LEVELS - 1):
                            if ph == 0:
                                s.wait_ge(S("p_Yt"), 2 * (k - 2) + q + 1)
                            else:
                                s.wait_ge(S("p_XY"), 2 * (k - 1) + q + 1)
                            s.activation(XT[d][:, 4 * q:4 * q + 4, :].rearrange("p a b -> p (a b)"), ps[:, 2 * q + 1, :],
                                         ACT.Copy).then_inc(S("a_Y"), 1)

                    def decay(bank, dd, pair):
                        s.wait_ge(S("p_lw"), 1)
                        s.activation(sw, ps[:, bank, :], ACT.Sigmoid, bias=pcol[:, COL["w0"] + 8 * dd + pair, :])\
                         .then_inc(S("a_lw"), 1)

                    def rate(bank, dd, pair):
                        s.wait_ge(S("p_lw"), 2)
                        s.activation(aa, ps[:, bank, :], ACT.Sigmoid, bias=pcol[:, COL["a0"] + 8 * dd + pair, :])\
                         .then_inc(S("a_lw"), 1)

                    def exps():
                        s.wait_ge(S("v_L"), 1)
                        s.activation(Ep, Lc, ACT.Exp, scale=-DECAY).then_inc(S("a_exp"), 1)
                        s.activation(En, Lc, ACT.Exp, scale=DECAY).then_inc(S("a_exp"), 1)

                    def exps_x():
                        s.wait_ge(S("g_Lx"), 1)
                        s.activation(Ex, Lx, ACT.Exp, scale=-DECAY).then_inc(S("a_exp"), 1)

                    def turned(z, q, n, bank):
                        s.wait_ge(S("p_bt"), n + 1)
                        s.activation(z[:, 4 * q:4 * q + 4, :].rearrange("p a b -> p (a b)"), ps[:, bank, :], ACT.Copy)\
                         .then_inc(S("a_bt"), 1)

                    def prepare(n):
                        if d == 0 and inv and n in (0, 1):
                            turned(Vt[0], n, 4 + n, 4 + n)
                        if d == 0 and not prep:
                            return
                        if d == 0:
                            if n == 4:
                                decay(4, 1, hp)
                                rate(5, 1, hp)
                            if n == 7:
                                exps()
                            if n == 9:
                                exps_x()
                            return
                        if n == 3 and post:
                            s.wait_ge(S("v_pc"), 1)
                            s.activation(ysq, ysum, ACT.Square).then_inc(S("a_psq"), 1)
                        if n == 5 and post:
                            s.wait_ge(S("p_pv"), 1)
                            s.activation(ysq, ps[:, 5, :], ACT.Sqrt, bias=eps[:, 1:2], scale=1.0 / C).then_inc(S("a_pstd"), 1)
                        if n == 12 and inv:
                            if post:
                                s.wait_ge(S("v_py"), 3)
                            s.wait_ge(S("p_gu"), 1)
                            s.activation(gbuf, ps[:, 5, :], ACT.Copy).then_inc(S("a_gu"), 1)
                        if not prep:
                            return
                        if n == 1:
                            decay(4, 0, hp + 1)
                        if n == 3:
                            rate(4, 0, hp + 1)
                        if n == 1:
                            s.wait_ge(S("ld_k"), 16)
                            s.activation(kr_sq, kr, ACT.Square, scale=pcol[:, COL["k_k"] + hp + 1, :]).then_inc(S("a_kk"), 1)
                        if n == 8:
                            s.wait_ge(S("v_ss"), 1)
                            s.activation(Ex, Ex, ACT.Sqrt).then_inc(S("a_nrm"), 1)
                        if n == 10:
                            exps()
                        if n == 15:
                            s.wait_ge(S("v_kk"), 1)
                            exps_x()

                    if inv:
                        chain(0, 4)
                        for j, z in enumerate((Bt[d], Ktk[d])):
                            for q in range(2):
                                turned(z, q, 2 * j + q, (NC + 2 * j + q) % 6)
                            chain(4 + j, 5 + j)
                    else:
                        chain(0, CHG)
                    for n in range(24):
                        if inv:
                            invert(n)
                        if CHG + n < 24:
                            chain(CHG + n, CHG + n + 1)
                        prepare(n)
                    if inv:
                        s.wait_ge(S("a_Y"), 2 * (LEVELS - 1))
                    if prep:
                        s.wait_ge(S("a_exp"), 3)
                    if has_chain:
                        s.wait_ge(S("a_Z"), NC)
                        if d == 1:
                            s.wait_ge(S("a_y"), NC)
                    if d == 1 and inv:
                        s.wait_ge(S("a_gu"), 1)
                rw_regions(s, half, meet)
                for j in range(2):
                    s.sem_inc(S(f"ev{2 * j}"), 1)
                with s.Fori(0, KT) as n:
                    for j in range(2):
                        s.wait_ge(S(f"p_mm{2 * j}"), n + 2)
                        s.wait_ge(S("v_out"), n + 1)
                        s.activation(sga[:, j, :], ps[:, 2 * j, :], ACT.Sigmoid).then_inc(S(f"ev{2 * j}"), 1)
                meet(s)
                meet(s)
                ln_act(s, lambda t: pcol[:, COL["ln1_b"] + t, :])
                for t in range(KT):
                    s.wait_ge(S("v_u"), t + 1)
                    s.activation(hT[:, t, :], hT[:, t, :], ACT.Identity, scale=ALPHA, bias=b2g[:, t:t + 1]).then_inc(S("a_act"), 1)
                s.wait_ge(S("a_act"), KT)
                meet(s)
                for half_ in range(2):
                    free(s, "ev")
                    s.sem_inc(S("v_sq"), 4)
                    with s.Fori(0, 4) as n:
                        for j in range(4):
                            s.wait_ge(S(f"p_mm{j}"), n + 2)
                            s.wait_ge(S("v_sq"), 4 * n + j + 1)
                            s.activation(fr[:, j, :], ps[:, j, :], ACT.Relu,
                                         bias=pcol[:, COL["b1"] + FH * half_ + 4 * n + j, :]).then_inc(S(f"ev{j}"), 1)
                    meet(s)
                    meet(s)
                ln_act(s, lambda t: pcol[:, COL["ln2_b"] + t, :])
                meet(s)

        @block.gpsimd
        def _(g):
            meet(g)
            with g.Fori(0, DEPTH) as l:
                meet(g)
                g.memset(wgp, 0.0).then_inc(S("g_set"), 1)
                g.wait_ge(S("g_set"), 1)
                g.wait_ge(S("ld_v"), 16)
                for d in range(2):
                    for j in range(2):
                        g.tensor_copy(wgp[:, :, j, 32 * d:32 * d + 4], wg16[:, :, 8 * d + 4 * j:8 * d + 4 * j + 4])\
                         .then_inc(S("g_set"), 1)
                def head_lo():
                    for j in (0, 1, 4, 2, 3):
                        g.wait_ge(S("v_hw"), (0, 1, 4, 2, 3).index(j) + 1)
                        if j == 4:
                            g.tensor_tensor(wvl, wv, wvh.bitcast(F32), ALU.subtract).then_inc(S("g_hw"), 1)
                        else:
                            g.tensor_tensor(wtl[:, j, :, :], wt[:, j, :, :], wqh[:, j, :, :].bitcast(F32), ALU.subtract)\
                             .then_inc(S("g_hw"), 1)
                    g.wait_ge(S("g_hw"), 5)
                for t in range(4):
                    x_lo(g, uT, uh2, ul2, t, t)
                g.wait_ge(S("g_xl"), 4)
                head_lo()
                meet(g)
                ml_regions(g, lambda post, h: head_lo(), meet)

                def weights(n_iter):
                    with g.Fori(0, n_iter) as n:
                        for j in range(4):
                            w_lo(g, j, n)
                g.memset(wup, 0.0).then_inc(S("g_dend"), 1)
                g.memset(gup2, 0.0).then_inc(S("g_dend"), 1)
                weights(7)
                meet(g)

                def half(d, inv, has_chain, post, prep, hp):
                    if not inv and prep:
                        g.memset(Bz, 0.0).then_inc(S("g_dend"), 1)
                        g.memset(Kz, 0.0).then_inc(S("g_dend"), 1)
                        g.memset(AQ[0], 0.0).then_inc(S("g_dend"), 1)
                        g.memset(Vz, 0.0).then_inc(S("g_dend"), 1)
                        g.memset(AQ[1], 0.0).then_inc(S("g_dend"), 1)
                    if not inv and not prep:
                        if d == 0:
                            for t in range(KT):
                                x_lo(g, uT, uh, ul, t, t)
                            for t in range(KT):
                                x_lo(g, yA, ah, al, t, KT + t)
                        else:
                            for t in range(KT):
                                x_lo(g, yB, bh, bl, t, t)
                        g.wait_ge(S("g_xl"), KT * (2 - d))
                        return
                    if inv:
                        for c in range(4):
                            g.wait_ge(S("v_g"), c + 1)
                            for c2 in range(2 * c, 2 * c + 2):
                                g.tensor_tensor(G1[d][:, c2, 0:P], G1[d][:, c2, 0:P], ident[:, :], ALU.add)\
                                 .then_inc(S("g_in"), 1)
                        if d == 1:
                            g.tensor_copy(Vt[1], Vt[0]).then_inc(S("g_vb"), 1)
                        g.wait_ge(S("g_in"), NC)
                    if prep:
                        g.wait_ge(S("v_L"), 1)
                        g.wait_ge(S("a_lw"), 1)
                        g.tensor_tensor(Lx, Lc, sw, ALU.subtract).then_inc(S("g_Lx"), 1)
                        g.wait_ge(S("g_Lx"), 1)
                    if inv and d == 1:
                        g.wait_ge(S("g_vb"), 1)
                    if not inv:
                        g.wait_ge(S("g_dend"), 5)
                rw_regions(g, half, meet)
                weights(KT)
                meet(g)
                for t in range(4):
                    x_lo(g, merged, mh, ml, t, t)
                weights(2)
                meet(g)
                for t in range(6):
                    x_lo(g, uT, uh, ul, t, t)
                g.wait_ge(S("g_xl"), 6)
                meet(g)
                for half_ in range(2):
                    for j in range(4):
                        w_lo(g, j, 0)

                    def units(n, last):
                        for j in range(4):
                            g.wait_ge(S("v_fh"), 4 * n + j + 1)
                            g.tensor_tensor(fl[:, ds(4 * n + j, 1), :], fsq[:, j:j + 1, :], fh[:, ds(4 * n + j, 1), :].bitcast(F32),
                                            ALU.subtract).then_inc(S("g_fl"), 1)
                            if not last:
                                w_lo(g, j, n + 1)
                    with g.Fori(0, 3) as n:
                        units(n, False)
                    units(3, True)
                    g.wait_ge(S("g_fl"), FH + 4)
                    meet(g)
                    weights(4)
                    meet(g)
                meet(g)

        @block.vector
        def _(v):
            v.memset(hsum, 0.0).then_inc(S("v_hs"), 1)
            v.memset(prow[96:128, 1, :], 0.0).then_inc(S("v_gb"), 1)
            v.memset(ones[:, :], 1.0).then_inc(S("v_set"), 1)
            v.memset(gbias[:, :], 0.0).then_inc(S("v_gb"), 1)
            v.memset(gd2[:, :], 0.0).then_inc(S("v_set"), 1)
            v.memset(eps[:, 0:1], 1e-5).then_inc(S("v_set"), 1)
            v.memset(eps[:, 1:2], 64e-5).then_inc(S("v_set"), 1)
            v.wait_ge(S("ld_id"), 16)
            v.tensor_copy(ident[:, :], craw[:, CI:CI + P]).then_inc(S("v_set"), 1)
            v.tensor_copy(bd[:, :], craw[:, CBD:CBD + P]).then_inc(S("v_set"), 1)
            v.wait_ge(S("p_tr"), 1)
            v.tensor_copy(lncol[:, :, 0], ps[:, 7, 0:24]).then_inc(S("v_tr"), 1)
            for t in range(KT):
                v.wait_ge(S("p_tr"), t + 2)
                v.tensor_copy(hT[:, t, :], ps[:, t % 4, :]).then_inc(S("v_tr"), 1)
                v.wait_ge(S("v_tr"), t + 2)
                sum_h(v, t, t)
            v.wait_ge(S("a_set"), 1)
            v.tensor_tensor(cond[:, 8:16, :], cond[:, 0:8, :], lncol[:, 16:24, :], ALU.mult).then_inc(S("v_set"), 1)
            v.wait_ge(S("v_set"), 7)
            v.wait_ge(S("ld_mask"), 16)
            v.tensor_copy(mask[:, :], craw[:, CG:NCONST]).then_inc(S("v_set"), 1)
            ada_sum(v, 0, adaw0[0], adas0[:, 0, :])
            ln_dve(v, lambda t: lncol[:, t, :], lambda: ada_sum(v, 1, adaw0[1], adas0[:, 1, :]))
            for i in range(2, 4):
                ada_sum(v, i, adaw0[i % 3], adas0[:, i, :])
            for i in range(4):
                ada_take(v, i, 2 + i, 4 * i)
            v.wait_ge(S("v_mod"), 4)
            meet(v)
            with v.Fori(0, DEPTH) as l:
                v.wait_ge(S("p_tr"), 1)
                for b in range(3):
                    n = P if b < 2 else 48
                    v.tensor_copy(pcol[:, b * P:b * P + n, 0], ps[:, b, 0:n]).then_inc(S("v_tr"), 1)
                v.wait_ge(S("v_tr"), 3)
                cmu = COL["mup"]
                v.tensor_tensor(mix0[:, 0:24, 0], pcol[:, cmu:cmu + 24, 0], pcol[:, cmu + 24:cmu + 48, 0], ALU.add).then_inc(S("v_gate"), 1)
                lo_ = COL["mup_lo"]
                v.tensor_tensor(mix0[:, 24:27, 0], pcol[:, lo_:lo_ + 3, 0], pcol[:, lo_ + 3:lo_ + 6, 0], ALU.add).then_inc(S("v_gate"), 1)
                v.tensor_tensor(mix0[:, 27:28, 0], pcol[:, lo_ + 6:lo_ + 7, 0], pcol[:, lo_ + 7:lo_ + 8, 0], ALU.add).then_inc(S("v_gate"), 1)
                v.tensor_scalar(ka1[:, :, 0], pcol[:, COL["k_a"]:COL["k_a"] + 8, 0], -1.0, 1.0, ALU.mult, ALU.add).then_inc(S("v_gate"), 1)
                v.wait_ge(S("v_gate"), 3)
                v.tensor_scalar(mix0[:, :, 0], mix0[:, :, 0], -1.0, 1.0, ALU.mult, ALU.add).then_inc(S("v_gate"), 1)
                v.tensor_tensor(mod[:, 0:16, 0], modr[:, 0:16], pcol[:, 256:272, 0], ALU.add).then_inc(S("v_gate"), 1)
                v.wait_ge(S("v_gate"), 6)
                v.tensor_scalar(mod[:, 8:16, 0], mod[:, 8:16, 0], 1.0, None, ALU.add).then_inc(S("v_gate"), 1)
                v.wait_ge(S("v_gate"), 7)
                meet(v)
                v.memset(zero, 0.0).then_inc(S("v_set"), 1)
                v.memset(one, 1.0).then_inc(S("v_set"), 1)
                v.memset(rows[64:P, :, :], 0.0).then_inc(S("v_out"), 1)
                modulate(v, 0)
                v.wait_ge(S("v_u"), KT)
                v.wait_ge(S("st_h"), 16)
                for t in range(KT):
                    x_hi(v, uT, uh2, t)
                for t in range(4, KT):
                    x_lo(v, uT, uh2, ul2, t, t, "v_xl")
                v.wait_ge(S("v_xl"), 4)

                def head_hi(j):
                    if j == 4:
                        v.wait_ge(S("ld_wv"), 16)
                        v.tensor_copy(wvh, wv).then_inc(S("v_hw"), 1)
                    else:
                        v.wait_ge(S(f"ld_w{j}"), 16)
                        v.tensor_copy(wqh[:, j, :, :], wt[:, j, :, :]).then_inc(S("v_hw"), 1)
                for j in (0, 1, 4, 2, 3):
                    head_hi(j)
                v.wait_ge(S("a_gate"), 5)
                v.scalar_tensor_tensor(gx[:, 5, :], gx[:, 1, :], 0.0, gx[:, 4, :], ALU.min, ALU.subtract).then_inc(S("v_gate"), 1)
                v.wait_ge(S("v_gate"), 1)
                v.wait_ge(S("v_set"), 2)
                v.tensor_tensor_scan(Gs[0:32, :], one[0:32, :], gx[0:32, 5, :], 0.0, ALU.mult, ALU.add).then_inc(S("v_gate"), 1)
                v.tensor_tensor_scan(Gs[32:64, ::-1], one[32:64, :], gx[32:64, 5, ::-1], 0.0, ALU.mult, ALU.add).then_inc(S("v_gate"), 1)
                v.wait_ge(S("v_gate"), 3)
                v.tensor_tensor(aS, gx[:, 0, :], Gs, ALU.subtract).then_inc(S("v_gate"), 1)
                v.wait_ge(S("v_gate"), 4)
                v.tensor_tensor_scan(gx[0:32, 2, :], zero[0:32, :], aS[0:32, :], -3e38, ALU.add, ALU.max).then_inc(S("v_gate"), 1)
                v.tensor_tensor_scan(gx[32:64, 2, ::-1], zero[32:64, :], aS[32:64, ::-1], -3e38, ALU.add, ALU.max).then_inc(S("v_gate"), 1)
                v.wait_ge(S("v_gate"), 6)
                v.tensor_scalar(rows[0:64, 0, :], gx[:, 2, :], -1.0, None, ALU.mult).then_inc(S("v_gate"), 1)
                v.wait_ge(S("v_gate"), 7)
                v.tensor_tensor(rows[0:64, 1, :], rows[0:64, 0, :], Gs, ALU.subtract).then_inc(S("v_gate"), 1)
                v.wait_ge(S("v_gate"), 8)
                v.wait_ge(S("v_out"), 1)
                meet(v)
                def centre():
                    v.wait_ge(S("p_m2"), 1)
                    for c in range(2):
                        v.scalar_tensor_tensor(hs[:, c, :], ps[:, 4, :], -1.0 / DV, hs[:, c, :], ALU.mult, ALU.add).then_inc(S("v_h"), 1)

                def scale(h):
                    v.wait_ge(S("a_std"), 1)
                    v.reciprocal(rf[:, 0, :], hstd).then_inc(S("v_rstd"), 1)
                    v.wait_ge(S("v_rstd"), 1)
                    v.wait_ge(S("v_h"), 2)
                    v.wait_ge(S("a_h2"), 2)
                    for c in range(2):
                        v.scalar_tensor_tensor(hs[:, c, :], hs[:, c, :], pcol[:, COL["norm_g"] + 2 * (h - 1) + c, :], rf[:, 0, :], ALU.mult,
                                               ALU.mult).then_inc(S("v_nrm"), 1)
                    v.wait_ge(S("v_nrm"), 2)
                    for c in range(2):
                        v.tensor_tensor(yA[:, ds(2 * (h - 1) + c, 1), :], hs[:, c:c + 1, :], so[:, c:c + 1, :], ALU.mult).then_inc(S("v_out"), 1)

                def modulation():
                    v.wait_ge(S("v_mod"), 8)
                    v.tensor_tensor(mod[:, 16:48, 0], modr[:, 16:48], pcol[:, 272:304, 0], ALU.add).then_inc(S("v_mod"), 1)
                    v.wait_ge(S("v_mod"), 9)
                    for i, o in enumerate((16, 32, 40)):
                        v.tensor_scalar(mod[:, o:o + 8, 0], mod[:, o:o + 8, 0], 1.0, None, ALU.add).then_inc(S("v_mod"), 1)
                    v.wait_ge(S("v_mod"), 12)
                    v.tensor_tensor(b2g[:, :], pcol[:, COL["b2"]:COL["b2"] + 8, 0], mod[:, 40:48, 0], ALU.mult).then_inc(S("v_mod"), 1)
                    v.wait_ge(S("v_mod"), 13)

                def diagonal(d):
                    v.wait_ge(S("p_nm"), d + 1)
                    for t in range(NT):
                        v.tensor_tensor(dg[:, d, t, :], ps[:, 6, t * P:(t + 1) * P], maskC[d], ALU.add).then_inc(S("v_dg"), 1)

                def conv(j, h):
                    v.wait_ge(S("a_c0"), j + 1)
                    for n, tap in enumerate((0, 1, 3, 4)):
                        o = tap - 2
                        dst = slice(max(0, -o), T - max(0, o))
                        src = slice(max(0, o), T - max(0, -o))
                        if n:
                            v.wait_ge(S("v_conv"), 4 * j + n)
                        v.scalar_tensor_tensor(qk[:, j, dst], ps[:, j, src], pcol[:, 8 * tap + 4 * j + h, :],
                                               qk[:, j, dst], ALU.mult, ALU.add).then_inc(S("v_conv"), 1)

                def weigh(d):
                    nE = 7 * d
                    for t in range(NT):
                        lo_, hi_ = span(d, t)
                        nE += 2 if hi_ - lo_ > P else 1
                        v.wait_ge(S("a_E"), nE)
                        v.wait_ge(S("p_s"), t + 1)
                        v.tensor_tensor(Pw[:, d, t, lo_:hi_], ps[:, t, lo_:hi_], Ew[:, d, t, lo_:hi_], ALU.mult).then_inc(S("v_P"), 1)

                def inv_den(d):
                    v.wait_ge(S("p_den"), d + 1)
                    v.wait_ge(S("a_emx"), d + 1)
                    v.tensor_scalar(rf[:, d, :], ps[:, 6 + d, :], -1.0, None, ALU.mult).then_inc(S("v_gate"), 1)
                    v.wait_ge(S("v_gate"), 3 * d + 1)
                    v.tensor_tensor(rf[:, d, :], ps[:, 6 + d, :], rf[:, d, :], ALU.max).then_inc(S("v_gate"), 1)
                    v.wait_ge(S("v_gate"), 3 * d + 2)
                    v.tensor_tensor(rf[:, d, :], rf[:, d, :], emx[:, d, :], ALU.max).then_inc(S("v_den"), 1)
                    v.wait_ge(S("v_den"), d + 1)
                    v.reciprocal(rf[:, d, :], rf[:, d, :]).then_inc(S("v_gate"), 1)
                    v.wait_ge(S("v_gate"), 3 * d + 3)

                def head(post, h):
                    for d in range(2):
                        v.tensor_copy(selh[:, d, :], ident[:, ds(32 * d + h, 1)].broadcast_to([P, P])).then_inc(S("v_sel"), 1)
                    if post:
                        centre()
                    diagonal(0)
                    conv(0, h)
                    diagonal(1)
                    if post:
                        scale(h)
                    conv(1, h)
                    for j in range(2):
                        v.wait_ge(S("a_sig"), j + 1)
                        v.scalar_tensor_tensor(qk[:, j, :], qk[:, j, :], 1.0 if j == 0 else DK ** -0.5, sg[:, j, :],
                                               ALU.mult, ALU.mult).then_inc(S("v_qk"), 1)
                    weigh(0)
                    weigh(1)
                    for j in (0, 1, 4):
                        head_hi(j)
                    inv_den(0)
                    head_hi(2)
                    inv_den(1)
                    for c in range(2):
                        v.wait_ge(S("p_num"), c + 1)
                        v.tensor_tensor(hs[:, c, :], ps[:, 4 + c, :], rf[:, 0, :], ALU.mult).then_inc(S("v_num"), 1)
                    head_hi(3)
                    for c in range(2):
                        v.wait_ge(S("p_num"), c + 3)
                        v.tensor_tensor(ht[:, c, :], ps[:, c, :], rf[:, 1, :], ALU.mult).then_inc(S("v_num"), 1)
                    for c in range(2):
                        v.wait_ge(S("v_num"), 3 + c)
                        v.tensor_tensor(hs[:, c, :], hs[:, c, :], ht[:, c, :], ALU.add).then_inc(S("v_den"), 1)
                    v.wait_ge(S("v_den"), 4)
                ml_regions(v, head, meet)

                def stream(n_iter, evac, first=0):
                    with v.Fori(first, n_iter - 1) as n:
                        for j in range(4):
                            evac(n, j)
                            w_hi(v, j, n + 1)
                    for j in range(4):
                        evac(n_iter - 1, j)
                for j in range(4):
                    w_hi(v, j, 0)
                    if j == 0:
                        centre()
                scale(HA)
                ada_sum(v, 0, adaw[0], adas[:, 0, :])
                for j, (x, n) in enumerate(((tw, P), (ad, P), (gd, P), (gd2, 32))):
                    mp = pcol[0:n, COL["mup_lo"] + j, :] if j < 3 else pcol[0:32, COL["mup_g2"], :]
                    mn = pcol[0:n, COL["mun_lo"] + j, :] if j < 3 else pcol[0:32, COL["mun_g2"], :]
                    shift(v, x[0:n, :], ps[0:n, j, :], mp, mn, j)
                    w_hi(v, j, 1)
                ada_sum(v, 1, adaw[1], adas[:, 1, :])
                ada_take(v, 0, 6, 16)

                def shift_x(n, j):
                    m, at = 4 * (n - 1) + j, 4 * n + j
                    v.wait_ge(S("a_c0"), at + 1)
                    v.scalar_tensor_tensor(xs[:, j:j + 1, 1:T], ps[:, j:j + 1, 0:T - 1], pcol[:, ds(COL["mup"] + m, 1), :],
                                           xs[:, j:j + 1, 1:T], ALU.mult, ALU.add).then_inc(S("v_s1"), 1)
                    v.wait_ge(S("v_s1"), at + 1)
                    v.scalar_tensor_tensor(xs[:, j:j + 1, 0:T - 1], ps[:, j:j + 1, 1:T], pcol[:, ds(COL["mun"] + m, 1), :],
                                           xs[:, j:j + 1, 0:T - 1], ALU.mult, ALU.add).then_inc(S("v_s2"), 1)
                    if j == 2:
                        ada_take(v, n, 6, 16 + 4 * n)
                        v.wait_ge(S("ld_ada"), 16 * n + 32)
                        v.tensor_scalar(adas[:, 1, :], adaw[0][:, 0, :], cond[:, 8, :], None, ALU.mult).then_inc(S("v_ada"), 1)
                    for k in ((), (), (1, 2, 3), (4, 5, 6, 7))[j]:
                        v.wait_ge(S("v_ada"), KT * (n + 1) + k)
                        v.scalar_tensor_tensor(adas[:, 1, :], adaw[0][:, k, :], cond[:, 8 + k, :], adas[:, 1, :],
                                               ALU.mult, ALU.add).then_inc(S("v_ada"), 1)
                stream(7, shift_x, 1)
                ada_take(v, 7, 6, 44)
                modulation()
                v.wait_ge(S("v_s2"), 28)
                meet(v)

                def half(d, inv, has_chain, post, prep, hp):
                    dd = 1 - d
                    pair = hp if d == 0 else hp + 1
                    last = HP - 1 if not inv else hp - 1
                    kmd = km if d == 0 else kmf

                    def ch(x):
                        return x.rearrange("p (c t) -> p c t", c=NC)

                    def bdiag(dst, x, y):
                        for z in range(2):
                            h0, h1 = 64 * z, 64 * z + 64
                            v.tensor_tensor(dst[h0:h1, :, h0:h1], ch(x)[h0:h1], ch(y)[h0:h1], ALU.mult).then_inc(S("v_bd"), 1)

                    def chain(lo_, hi_):
                        if not has_chain:
                            return
                        for n in range(lo_, hi_):
                            cd = 1 - d
                            i, ph = n // 3, n % 3
                            c = i if cd == 0 else NC - 1 - i
                            S_in, S_out = Sst[:, (i + 1) % 2, :], Sst[:, i % 2, :]
                            if ph == 1:
                                if i and i < NC - 1:
                                    v.tensor_scalar(Sd, S_in, dend[cd][:, c:c + 1], None, ALU.mult).then_inc(S("v_Sd"), 1)
                                v.wait_ge(S("p_U"), i + 1)
                                if i:
                                    v.wait_ge(S("p_Y"), i)
                                v.tensor_copy(Us, ps[:, 7, 0:P]).then_inc(S("v_U"), 1)
                            elif ph == 2:
                                if i < NC - 1:
                                    v.wait_ge(S("p_S"), i + 1)
                                    if i:
                                        v.wait_ge(S("v_Sd"), i)
                                        v.scalar_tensor_tensor(S_out, ps[:, 6, P:2 * P], dend[cd][:, c:c + 1], Sd, ALU.mult, ALU.add)\
                                         .then_inc(S("v_S"), 1)
                                    else:
                                        v.tensor_scalar(S_out, ps[:, 6, P:2 * P], dend[cd][:, c:c + 1], None, ALU.mult).then_inc(S("v_S"), 1)
                                    v.wait_ge(S("v_S"), i + 1)
                                if cd == 1:
                                    v.wait_ge(S("p_Y"), i + 1)
                                    v.tensor_tensor(ysum[:, c * C:(c + 1) * C], yf[:, c * C:(c + 1) * C], ps[:, 7, P + C:2 * P], ALU.add)\
                                     .then_inc(S("a_y"), 1)

                    def invert(n):
                        k, ph, q = n // 4, n // 2 % 2, n % 2
                        if ph == 0:
                            v.wait_ge(S("p_T"), 2 * k + q + 1)
                            if k >= 2:
                                v.wait_ge(S("p_XY"), 2 * (k - 2) + q + 1)
                            R = Xm if k == 0 else Rm
                            v.tensor_tensor(R[:, 4 * q:4 * q + 4, :], ps[:, 2 * q, :].rearrange("p (c x) -> p c x", c=4),
                                            maskL[d][k].rearrange("p (o x) -> p o x", o=1).broadcast_to([P, 4, P]), ALU.mult)\
                             .then_inc(S("v_R"), 1)
                        if n in (4 - 2 * d, 5 - 2 * d):
                            q = n % 2
                            v.wait_ge(S("g_in"), 4 * q + 4)
                            if d == 0:
                                v.wait_ge(S("p_bt"), 6)
                            v.tensor_tensor(XT[d][:, 4 * q:4 * q + 4, :], G1[d][:, 4 * q:4 * q + 4, 0:P],
                                            maskL[1 - d][0].rearrange("p (o x) -> p o x", o=1).broadcast_to([P, 4, P]), ALU.mult)\
                             .then_inc(S("v_Y"), 1)

                    def scan():
                        v.wait_ge(S("a_lw"), 1)
                        if dd == 0:
                            v.tensor_tensor_scan(Lc, maskR[0], sw, 0.0, ALU.mult, ALU.add).then_inc(S("v_L"), 1)
                        else:
                            v.tensor_tensor_scan(Lc[:, ::-1], maskR[1][:, ::-1], sw[:, ::-1], 0.0, ALU.mult, ALU.add).then_inc(S("v_L"), 1)

                    def k_scale():
                        v.wait_ge(S("a_lw"), 2)
                        if dd == 1:
                            v.wait_ge(S("g_Lx"), 1)
                        v.tensor_scalar(kmd, aa, pcol[:, COL["k_a"] + pair, :], ka1[:, pair, :],
                                        ALU.mult, ALU.add).then_inc(S("v_km"), 1)

                    def k_mul():
                        v.wait_ge(S("v_km"), 1)
                        v.tensor_tensor(kmd, kmd, kr, ALU.mult).then_inc(S("v_km"), 1)

                    def rate():
                        v.scalar_tensor_tensor(aa, kk, -1.0, aa, ALU.mult, ALU.mult).then_inc(S("v_km"), 1)

                    def fill_k():
                        if not inv:
                            v.wait_ge(S("g_dend"), 5)
                        else:
                            v.wait_ge(S("p_bt"), 4)
                        v.wait_ge(S("a_exp"), 2)
                        v.wait_ge(S("v_km"), 2)
                        bdiag(Kz, kmd, En)

                    def fill_b():
                        v.wait_ge(S("v_km"), 3)
                        bdiag(Bz, aa, En)

                    def fill_a():
                        if has_chain:
                            v.wait_ge(S("p_Y"), NC)
                        v.wait_ge(S("a_exp"), 3)
                        v.tensor_copy(dend[dd], Ep[:, (C - 1 if dd == 0 else 0):T:C]).then_inc(S("v_dend"), 1)
                        bdiag(AQ[dd], kk, Ex)

                    def fill_q():
                        v.tensor_tensor(AQ[dd][:, :, P:P + C], ch(rr), ch(Ep), ALU.mult).then_inc(S("v_bd"), 1)

                    def finish(n):
                        if n == 2:
                            v.wait_ge(S("p_pm"), 1)
                            v.scalar_tensor_tensor(ysum, ps[:, 5, :], -1.0 / C, ysum, ALU.mult, ALU.add).then_inc(S("v_pc"), 1)
                        if n in (8, 9):
                            v.wait_ge(S("a_pstd"), 1)
                            half_ = ysq[:, (n - 8) * T // 2:(n - 7) * T // 2]
                            v.reciprocal(half_, half_).then_inc(S("v_pr"), 1)
                        if n == 10:
                            v.wait_ge(S("v_pr"), 2)
                            v.scalar_tensor_tensor(ysum, ysum, pcol[:, COL["gn_g"] + last, :], ysq, ALU.mult, ALU.mult).then_inc(S("v_py"), 1)
                            v.wait_ge(S("v_py"), 1)
                            v.scalar_tensor_tensor(ysum, ysum, pcol[:, COL["gn_b"] + last, :], bonus, ALU.add, ALU.add).then_inc(S("v_py"), 1)
                        if n == 11:
                            v.wait_ge(S("v_py"), 2)
                            v.tensor_tensor(yB[:, last, :], ysum, gbuf, ALU.mult).then_inc(S("v_py"), 1)

                    def prepare(n):
                        if d == 0 and not prep:
                            return
                        if d == 0:
                            if n == 6:
                                scan()
                            if n == 8:
                                k_scale()
                            if n == 9:
                                k_mul()
                            if n == 10:
                                v.wait_ge(S("v_km"), 2)
                                rate()
                            if n == 11:
                                v.tensor_tensor(rks, km, kmf, ALU.add).then_inc(S("v_rk"), 1)
                            if n == 12:
                                v.wait_ge(S("v_rk"), 1)
                                v.scalar_tensor_tensor(rks, rr, pcol[:, COL["r_k"] + pair, :], rks, ALU.mult, ALU.mult).then_inc(S("v_rk"), 1)
                            if n == 13:
                                fill_k()
                            if n == 15:
                                fill_b()
                            if n == 19:
                                fill_a()
                            if n == 20:
                                fill_q()
                            return
                        if post:
                            finish(n)
                        if n == 15 and inv:
                            v.wait_ge(S("p_bon"), 1)
                            v.tensor_tensor(bonus, ps[:, 5, :], vr, ALU.mult).then_inc(S("v_bon"), 1)
                        if not prep:
                            return
                        if n == 5:
                            v.wait_ge(S("p_ss"), 1)
                            v.tensor_scalar(Ex, ps[:, 4, :], 1e-24, None, ALU.max).then_inc(S("v_ss"), 1)
                        if n in (12, 13):
                            v.wait_ge(S("a_nrm"), 1)
                            half_ = Ex[:, (n - 12) * T // 2:(n - 11) * T // 2]
                            v.reciprocal(half_, half_).then_inc(S("v_ss"), 1)
                        if n == 14:
                            v.wait_ge(S("v_ss"), 3)
                            v.wait_ge(S("ld_k"), 16)
                            v.scalar_tensor_tensor(kk, kr, pcol[:, COL["k_k"] + pair, :], Ex, ALU.mult, ALU.mult).then_inc(S("v_kk"), 1)
                        if n == 6:
                            scan()
                        if n == 7:
                            k_scale()
                            v.wait_ge(S("ld_k"), 16)
                            k_mul()
                        if n == 11:
                            fill_k()
                        if n == 14:
                            v.wait_ge(S("v_kk"), 1)
                            v.wait_ge(S("v_km"), 2)
                            rate()
                        if n == 16:
                            fill_b()
                        if n == 18:
                            fill_a()
                        if n == 19:
                            v.wait_ge(S("ld_r"), 16)
                            fill_q()
                        if n == 20:
                            v.wait_ge(S("ld_vr"), 16)
                            for z in range(2):
                                v.tensor_copy(Vz[64 * z:64 * z + 64, :, 64 * z:64 * z + 64], ch(vr)[64 * z:64 * z + 64])\
                                 .then_inc(S("v_bd"), 1)

                    if not inv and not prep:
                        if d == 0:
                            for n in range(24):
                                chain(n, n + 1)
                                if n < 16:
                                    x_hi(v, uT if n < KT else yA, uh if n < KT else ah, n % KT)
                            v.wait_ge(S("v_xh"), 2 * KT)
                            v.wait_ge(S("a_y"), NC)
                        else:
                            for n in range(12):
                                finish(n)
                                if n < KT - 1:
                                    x_hi(v, yB, bh, n)
                            v.wait_ge(S("v_py"), 3)
                            x_hi(v, yB, bh, KT - 1)
                            scale_h(v)
                            v.wait_ge(S("v_xh"), KT)
                        return
                    if inv:
                        for b in range(NC):
                            v.wait_ge(S("p_g"), b + 1)
                            G = G1[d] if b < 4 else G3[d]
                            c0 = 2 * (b % 4)
                            v.tensor_tensor(G[:, c0:c0 + 2, :], ps[:, b % 6, 0:384].rearrange("p (c x) -> p c x", c=2),
                                            maskG[d].rearrange("p (o x) -> p o x", o=1).broadcast_to([P, 2, 192]), ALU.mult)\
                             .then_inc(S("v_g"), 1)
                            if b % 2:
                                chain(b // 2, b // 2 + 1)
                        chain(4, CHG)
                    for n in range(24):
                        if inv:
                            invert(n)
                        if CHG + n < 24:
                            chain(CHG + n, CHG + n + 1)
                        prepare(n)
                    if inv:
                        v.wait_ge(S("v_R"), 2 * LEVELS)
                    if prep:
                        v.wait_ge(S("v_bd"), 7 + 2 * d)
                    if has_chain and d == 0:
                        v.wait_ge(S("a_y"), NC)
                rw_regions(v, half, meet)
                v.sem_inc(S("v_out"), 1)
                for j in range(2):
                    v.sem_inc(S(f"ev{2 * j + 1}"), 1)
                for j in range(4):
                    w_hi(v, j, 0)

                def merge(n, j):
                    if j % 2 == 0:
                        return
                    if j == 1:
                        v.wait_ge(S("v_out"), n + 1)
                    v.wait_ge(S(f"ev{j - 1}"), n + 2)
                    v.wait_ge(S(f"p_mm{j}"), n + 2)
                    v.tensor_tensor(pa_[:, j // 2, :], ps[:, j, :], sga[:, j // 2, :], ALU.mult).then_inc(S(f"ev{j}"), 1)
                    if j == 3:
                        v.wait_ge(S("ev1"), n + 2)
                        v.wait_ge(S("ev3"), n + 2)
                        v.tensor_tensor(merged[:, ds(n, 1), :], pa_[:, 0:1, :], pa_[:, 1:2, :], ALU.add).then_inc(S("v_out"), 1)
                stream(KT, merge)
                v.wait_ge(S("v_out"), KT + 1)
                meet(v)
                v.memset(prow[96:128, 1, :], 0.0).then_inc(S("v_gb"), 1)
                free(v, "ev")
                w_hi(v, 0, 0)
                for t in range(KT):
                    x_hi(v, merged, mh, t)
                for t in range(4, KT):
                    x_lo(v, merged, mh, ml, t, t, "v_xl")
                for j in range(1, 4):
                    w_hi(v, j, 0)

                v.memset(hsum, 0.0).then_inc(S("v_hs"), 1)

                def add_out(n, j):
                    v.wait_ge(S(f"p_mm{j}"), n + 2)
                    v.scalar_tensor_tensor(hT[:, ds(4 * n + j, 1), :], ps[:, j:j + 1, :], mod[:, 16 + 4 * n + j, :],
                                           hT[:, ds(4 * n + j, 1), :], ALU.mult, ALU.add).then_inc(S(f"ev{j}"), 1)
                    v.wait_ge(S(f"ev{j}"), n + 2)
                    sum_h(v, 4 * n + j, 4 * n + j)
                stream(2, add_out)
                for j in range(4):
                    v.wait_ge(S(f"ev{j}"), 3)
                v.wait_ge(S("v_hs"), KT + 1)
                meet(v)
                ln_dve(v, lambda t: pcol[:, COL["ln1_g"] + t, :])
                for t in range(KT):
                    v.wait_ge(S("v_out"), t + 1)
                    v.tensor_scalar(uT[:, t, :], hT[:, t, :], mod[:, 32 + t, :], mod[:, 24 + t, :], ALU.mult, ALU.add)\
                     .then_inc(S("v_u"), 1)
                    v.wait_ge(S("v_u"), t + 1)
                    x_hi(v, uT, uh, t)
                for t in range(6, KT):
                    x_lo(v, uT, uh, ul, t, t, "v_xl")
                v.wait_ge(S("v_xl"), 2)
                v.wait_ge(S("v_xh"), KT)
                meet(v)
                for half_ in range(2):
                    v.sem_inc(S("g_fl"), 4)
                    for j in range(4):
                        w_hi(v, j, 0)

                    def units(n, j):
                        v.wait_ge(S(f"ev{j}"), n + 2)
                        v.wait_ge(S("g_fl"), 4 * n + j + 1)
                        v.tensor_tensor(fsq[:, j, :], fr[:, j, :], fr[:, j, :], ALU.mult).then_inc(S("v_sq"), 1)
                        v.wait_ge(S("v_sq"), 4 * n + j + 5)
                        v.tensor_copy(fh[:, ds(4 * n + j, 1), :], fsq[:, j:j + 1, :]).then_inc(S("v_fh"), 1)
                    stream(4, units)
                    v.wait_ge(S("v_fh"), FH)
                    meet(v)
                    free(v, "ev")
                    v.memset(hsum, 0.0).then_inc(S("v_hs"), 1)
                    for j in range(4):
                        w_hi(v, j, 0)

                    def add_down(n, j):
                        if j % 2 == 0:
                            return
                        v.wait_ge(S(f"p_mm{j}"), n + 2)
                        t = 2 * n + j // 2
                        v.scalar_tensor_tensor(hT[:, ds(t, 1), :], ps[:, j // 2:j // 2 + 1, :], mod[:, 40 + t, :],
                                               hT[:, ds(t, 1), :], ALU.mult, ALU.add).then_inc(S(f"ev{j // 2}"), 1)
                        if half_:
                            v.wait_ge(S(f"ev{j // 2}"), n + 2)
                            sum_h(v, t, t)
                    ada_sum(v, 0, adaw[2], adas[:, 0, :])
                    with v.Fori(0, 3) as n:
                        for j in range(4):
                            add_down(n, j)
                            w_hi(v, j, n + 1)
                    ada_sum(v, 1, adaw[2], adas[:, 1, :])
                    for j in range(4):
                        add_down(3, j)
                    for i in range(2):
                        ada_take(v, i, 6 + i, 8 * half_ + 4 * i)
                    v.wait_ge(S("v_mod"), 2)
                    v.wait_ge(S("v_hs"), KT * half_ + 1)
                    for j in range(2):
                        v.wait_ge(S(f"ev{j}"), 5)
                    meet(v)
                ln_dve(v, lambda t: pcol[:, COL["ln2_g"] + t, :])
                meet(v)
            for b in range(2 * NT):
                v.wait_ge(S("p_tr"), b + 1)
                v.tensor_copy(xtok[:, b // 2, (b % 2) * 512:(b % 2 + 1) * 512], ps[:, b % 4, :]).then_inc(S("v_tr"), 1)


def kernel(**inputs):
    import concourse.bacc as _bacc
    from concourse.bass_utils import run_bass_kernel_spmd as _run

    nc = _bacc.Bacc("TRN2", target_bir_lowering=False, num_devices=1)
    arrays, args = {}, {}
    for name, x in inputs.items():
        x = np.ascontiguousarray(x)
        arrays[f"in_{name}"] = x
        args[name] = nc.dram_tensor(f"in_{name}", x.shape, mybir.dt.from_np(x.dtype), kind="ExternalInput").ap()
    arrays["in_consts"] = constants()
    consts = nc.dram_tensor("in_consts", (P, NCONST), F32, kind="ExternalInput").ap()
    out = nc.dram_tensor("out_h", (1, T, D), F32, kind="ExternalOutput").ap()
    encoder(nc, args, consts, out)
    r = _run(nc, [arrays], core_ids=[0])
    return r.results[0]["out_h"]
```
